# Optimizing a Trainium2 kernel written in Bass

```python
import functools
import jax, jax.numpy as jnp
from jax import lax
import numpy as np

D_MODEL = 2048
BATCH = 1
SEQ = 256
DEPTH = 1
DEC_BATCH = 8
DEC_SEQ = 8
PAST_LEN = 2048
PAGE_SIZE = 128

N_META = 16
CHUNK = 128
M_HEADS = 4
M_DK = 256
M_DV = 256
M_WIDTH = M_HEADS * M_DV
C_WIDTH = 1024
CONV_W = 3
D_FF = 4 * D_MODEL
EPS = 1e-6
D_IN = 2 * M_HEADS * M_DK + 2 * M_WIDTH + 2 * M_HEADS + 3 * C_WIDTH + 2 * D_MODEL

kernel_name = 'hybrid_mlstm_shortconv_decode_step'

def _split_points():
    sizes = (M_HEADS * M_DK, M_HEADS * M_DK, M_WIDTH, M_HEADS, M_HEADS, M_WIDTH,
             C_WIDTH, C_WIDTH, C_WIDTH, D_MODEL, D_MODEL)
    pts, acc = [], 0
    for s in sizes[:-1]:
        acc += s
        pts.append(acc)
    return pts

def rmsnorm(x, g):
    xf = x.astype(jnp.float32)
    y = xf * lax.rsqrt(jnp.mean(xf * xf, axis=-1, keepdims=True) + EPS)
    return (y * g.astype(jnp.float32)).astype(x.dtype)

def mlstm_chunk(q, k, v, ig, lf, C, n, m):
    f32 = jnp.float32
    q, k, v, ig, lf = (a.astype(f32) for a in (q, k, v, ig, lf))
    C, n, m = C.astype(f32), n.astype(f32), m.astype(f32)
    L = q.shape[2]
    b = jnp.cumsum(lf, axis=-1)
    causal = jnp.tril(jnp.ones((L, L), dtype=bool))
    logw = jnp.where(causal, b[..., :, None] - b[..., None, :] + ig[..., None, :], -jnp.inf)
    inter = b + m[..., None]
    m_t = jnp.maximum(inter, jnp.max(logw, axis=-1))
    w_inter = jnp.exp(inter - m_t)
    s = jnp.einsum('bhtd,bhsd->bhts', q, k) * jnp.exp(logw - m_t[..., None])
    num = w_inter[..., None] * jnp.einsum('bhtd,bhde->bhte', q, C) + jnp.einsum('bhts,bhse->bhte', s, v)
    den = w_inter * jnp.einsum('bhtd,bhd->bht', q, n) + jnp.sum(s, axis=-1)
    h = num / jnp.maximum(jnp.abs(den), jnp.exp(-m_t))[..., None]
    m_new = m_t[..., -1]
    decay = jnp.exp(b[..., -1] + m - m_new)
    wk = jnp.exp(b[..., -1:] - b + ig - m_new[..., None])
    C_new = decay[..., None, None] * C + jnp.einsum('bhs,bhsd,bhse->bhde', wk, k, v)
    n_new = decay[..., None] * n + jnp.einsum('bhs,bhsd->bhd', wk, k)
    return h, (C_new, n_new, m_new)

def mlstm_prompt(q, k, v, ig, lf):
    bsz, t = q.shape[0], q.shape[2]
    f32 = jnp.float32
    C0 = jnp.zeros((bsz, M_HEADS, M_DK, M_DV), f32)
    n0 = jnp.zeros((bsz, M_HEADS, M_DK), f32)
    m0 = jnp.zeros((bsz, M_HEADS), f32)
    h0, st = mlstm_chunk(q[:, :, :N_META], k[:, :, :N_META], v[:, :, :N_META],
                         ig[:, :, :N_META], lf[:, :, :N_META], C0, n0, m0)
    nc = (t - N_META) // CHUNK

    def to_chunks(a):
        a = a[:, :, N_META:]
        a = a.reshape(a.shape[:2] + (nc, CHUNK) + a.shape[3:])
        return jnp.moveaxis(a, 2, 0)

    def step(carry, xs):
        h, carry = mlstm_chunk(*xs, *carry)
        return carry, h

    st, hs = lax.scan(step, st, tuple(to_chunks(a) for a in (q, k, v, ig, lf)))
    hs = jnp.moveaxis(hs, 0, 2).reshape(bsz, M_HEADS, nc * CHUNK, M_DV)
    return jnp.concatenate([h0, hs], axis=2), st

def causal_conv(zp, w):
    L = zp.shape[1] - (CONV_W - 1)
    y = w[0] * zp[:, 0:L]
    for j in range(1, CONV_W):
        y = y + w[j] * zp[:, j:j + L]
    return y

def conv_prompt(z, w):
    zp = jnp.pad(z, ((0, 0), (CONV_W - 1, 0), (0, 0)))
    return causal_conv(zp, w), z[:, -(CONV_W - 1):]

def conv_step(z, w, buf):
    zp = jnp.concatenate([buf.astype(z.dtype), z], axis=1)
    return causal_conv(zp, w), zp[:, -(CONV_W - 1):]

def trunk_layer(x, lw, mlstm_fn, conv_fn):
    g_mix, w_in, b_in, w_conv, p_a, p_b, w_o, g_ffn, w_up, w_down = lw
    bsz, t = x.shape[0], x.shape[1]
    xn = rmsnorm(x, g_mix)
    z = xn @ w_in + b_in
    zq, zk, zv, zi, zf, zo, zu, zc, zb, zga, zgb = jnp.split(z, _split_points(), axis=-1)
    heads = lambda a, d: a.reshape(bsz, t, M_HEADS, d).transpose(0, 2, 1, 3)
    q = heads(zq, M_DK)
    k = heads(zk, M_DK) * (M_DK ** -0.5)
    v = heads(zv, M_DV)
    ig = zi.astype(jnp.float32).transpose(0, 2, 1)
    lf = jax.nn.log_sigmoid(zf.astype(jnp.float32)).transpose(0, 2, 1)
    h, m_state = mlstm_fn(q, k, v, ig, lf)
    h = h.transpose(0, 2, 1, 3).reshape(bsz, t, M_WIDTH).astype(x.dtype)
    h_a = jax.nn.sigmoid(zo) * h
    conv_out, conv_state = conv_fn(zc * zu, w_conv)
    y_b = zb * conv_out
    merged = jax.nn.sigmoid(zga) * (h_a @ p_a) + jax.nn.sigmoid(zgb) * (y_b @ p_b)
    x = x + merged @ w_o
    u = jax.nn.relu(rmsnorm(x, g_ffn) @ w_up)
    x = x + (u * u) @ w_down
    return x, m_state, conv_state

def setup_inputs(seed: int = 0) -> dict:
    key = jax.random.key(seed)
    ks = jax.random.split(key, 20)
    nrm = lambda kk, shape, scale: jax.random.normal(kk, shape, jnp.float32) * scale
    f_off = 2 * M_HEADS * M_DK + M_WIDTH + M_HEADS
    b_in = nrm(ks[0], (DEPTH, D_IN), 0.02)
    b_in = b_in.at[:, f_off:f_off + M_HEADS].add(jnp.linspace(3.0, 6.0, M_HEADS))
    return {
        'x_prompt': nrm(ks[1], (BATCH, SEQ, D_MODEL), 1.0),
        'x_sample': nrm(ks[2], (DEC_BATCH, DEC_SEQ, D_MODEL), 1.0),
        'state_mlstm_C': nrm(ks[3], (DEPTH, DEC_BATCH, M_HEADS, M_DK, M_DV), 0.5),
        'state_mlstm_n': nrm(ks[4], (DEPTH, DEC_BATCH, M_HEADS, M_DK), 0.5),
        'state_mlstm_m': nrm(ks[5], (DEPTH, DEC_BATCH, M_HEADS), 1.0),
        'state_conv': nrm(ks[6], (DEPTH, DEC_BATCH, CONV_W - 1, C_WIDTH), 1.0),
        'meta_tokens': nrm(ks[7], (N_META, D_MODEL), 1.0),
        'g_mix': 1.0 + nrm(ks[8], (DEPTH, D_MODEL), 0.02),
        'w_in': nrm(ks[9], (DEPTH, D_MODEL, D_IN), D_MODEL ** -0.5),
        'b_in': b_in,
        'w_conv': nrm(ks[10], (DEPTH, CONV_W, C_WIDTH), CONV_W ** -0.5),
        'p_a': nrm(ks[11], (DEPTH, M_WIDTH, D_MODEL), M_WIDTH ** -0.5),
        'p_b': nrm(ks[12], (DEPTH, C_WIDTH, D_MODEL), C_WIDTH ** -0.5),
        'w_o': nrm(ks[13], (DEPTH, D_MODEL, D_MODEL), D_MODEL ** -0.5),
        'g_ffn': 1.0 + nrm(ks[14], (DEPTH, D_MODEL), 0.02),
        'w_up': nrm(ks[15], (DEPTH, D_MODEL, D_FF), D_MODEL ** -0.5),
        'w_down': nrm(ks[16], (DEPTH, D_FF, D_MODEL), D_FF ** -0.5),
        'g_final': 1.0 + nrm(ks[17], (D_MODEL,), 0.02),
    }

def reference(x_prompt, x_sample, state_mlstm_C, state_mlstm_n, state_mlstm_m, state_conv,
              meta_tokens, g_mix, w_in, b_in, w_conv, p_a, p_b, w_o, g_ffn, w_up, w_down, g_final):
    bsz = x_prompt.shape[0]
    meta = jnp.broadcast_to(meta_tokens.astype(x_prompt.dtype)[None], (bsz, N_META, D_MODEL))
    xp = jnp.concatenate([meta, x_prompt], axis=1)
    xs = x_sample
    Cp, n_p, mp, cvp, Cs, n_s, ms, cvs = [], [], [], [], [], [], [], []
    for l in range(DEPTH):
        lw = (g_mix[l], w_in[l], b_in[l], w_conv[l], p_a[l], p_b[l], w_o[l], g_ffn[l], w_up[l], w_down[l])
        xp, (c1, n1, m1), cv1 = trunk_layer(xp, lw, mlstm_prompt, conv_prompt)
        mfn = functools.partial(mlstm_chunk, C=state_mlstm_C[l], n=state_mlstm_n[l], m=state_mlstm_m[l])
        cfn = functools.partial(conv_step, buf=state_conv[l])
        xs, (c2, n2, m2), cv2 = trunk_layer(xs, lw, mfn, cfn)
        Cp.append(c1); n_p.append(n1); mp.append(m1); cvp.append(cv1)
        Cs.append(c2); n_s.append(n2); ms.append(m2); cvs.append(cv2)
    y_prompt = rmsnorm(xp, g_final)[:, N_META:]
    y_sample = rmsnorm(xs, g_final)
    st = lambda lst, ref: jnp.stack(lst).astype(ref.dtype)
    return (y_prompt, y_sample,
            st(Cp, state_mlstm_C), st(n_p, state_mlstm_n), st(mp, state_mlstm_m), st(cvp, state_conv),
            st(Cs, state_mlstm_C), st(n_s, state_mlstm_n), st(ms, state_mlstm_m), st(cvs, state_conv))


_drawn_inputs = setup_inputs


def setup_inputs(seed=0):
    import zlib

    import numpy as np

    out = dict(_drawn_inputs(seed))
    spreads = {}
    factors = {'g_ffn': 3.676, 'g_final': 2.826}
    for name, (base, spread) in spreads.items():
        noise = np.random.default_rng([zlib.crc32(name.encode()), seed]).standard_normal(out[name].shape)
        drawn = base * np.exp(spread * noise) if base else spread * noise
        out[name] = __import__('jax').numpy.asarray(drawn.astype(out[name].dtype))
    for name, factor in factors.items():
        out[name] = (out[name] * factor).astype(out[name].dtype)
    return out
```

```python
from contextlib import ExitStack

import concourse.bass as bass
from concourse import mybir

F32 = mybir.dt.float32
F32R = mybir.dt.float32r
ALU = mybir.AluOpType
ACT = mybir.ActivationFunctionType
P = 128
ds = bass.ds

EPS = 1e-6
BIG = 1e30
FAR = 3e38
RING = 4
LEAD = 3
UK = 4
GC = 256
GB = GC // P


def build(nc, x_prompt, x_sample, state_C, state_n, state_m, state_conv, meta, g_mix, w_in, b_in,
          w_conv, p_a, p_b, w_o, g_ffn, w_up, w_down, g_final,
          y_prompt, y_sample, C_prompt, n_prompt, m_prompt, conv_prompt,
          C_sample, n_sample, m_sample, conv_sample):
    _, SEQ, D = x_prompt.shape
    NB, DS, _ = x_sample.shape
    _, _, H, DK, DV = state_C.shape
    NMETA = meta.shape[0]
    CW = w_conv.shape[2]
    TAPS = w_conv.shape[1]
    FF = w_up.shape[2]
    T0 = NMETA
    TP = NMETA + SEQ
    TS = NB * DS
    T = TP + TS
    TO = T - T0
    KB = D // P
    assert DK == GC and DV == GC and H * DV == CW == H * GC and D % (P * UK) == 0
    assert T <= 512 and TP % P == NMETA and TS <= P and TAPS == 3
    MW = H * DV
    CQ, CK, CV, CG = 0, H * DK, 2 * H * DK, 2 * H * DK + MW
    CO = CG + 2 * H
    CU, CC, CB = CO + MW, CO + MW + CW, CO + MW + 2 * CW
    CGA, CGB = CO + MW + 3 * CW, CO + MW + 3 * CW + D
    NB1, NB2 = CG // P, (CGB + D - CO) // P
    BQ, BK, BV = 0, CK // P, CV // P
    BO = NB1
    BU, BC_, BB = BO + MW // P, BO + (CU + CW - CO) // P, BO + (CB - CO) // P
    BGA, BGB = BO + (CGA - CO) // P, BO + (CGB - CO) // P
    KT = [(0, P), (P, P), (2 * P, NMETA), (TP, TS)]
    QT = [(T0, TP - T0, 0), (P, TP - P, TP - T0), (2 * P, TP - 2 * P, 2 * TP - T0 - P),
          (TP, TS, 3 * TP - T0 - 3 * P)]
    SW = QT[3][2] + TS
    RW = T + TO + TS
    REM, RWI = T, T + TO

    GH, UH = 7, 28
    QH = 7
    NMG = D // GC
    U_MERGE = UH * H
    U_WO = U_MERGE + 12 * NMG
    U_FF = U_WO + 4 * NMG
    NCH = FF // D
    UCH = 8 * NMG
    U_ALL = U_FF + NCH * UCH
    G_MERGE = GH * H
    G_WO = G_MERGE + 4 * NMG
    G_FF = G_WO + NMG

    with ExitStack() as ctx:
        def sem(name):
            return ctx.enter_context(nc.semaphore(name))

        def tile(stack, name, shape, dt=F32):
            return stack.enter_context(nc.sbuf_tensor(name, shape, dt))

        raw = tile(ctx, "raw", [P, RING, UK, GC])
        wh = tile(ctx, "w_high", [P, RING, UK, GC], F32R)
        wl = tile(ctx, "w_low", [P, RING, UK, GC], F32R)
        xT = tile(ctx, "x_T", [P, KB, T])
        xh = tile(ctx, "x_high", [P, KB, T], F32R)
        xl = tile(ctx, "x_low", [P, KB, T], F32R)
        ident = tile(ctx, "ident", [P, P])
        ones = tile(ctx, "ones", [P, P])
        rbc = tile(ctx, "r_bc", [P, T])
        biasT = tile(ctx, "bias_T", [P, NB1 + NB2])
        vecT = tile(ctx, "vec_T", [P, 3 * KB + TAPS * CW // P])
        VG, VF, VL, VC = 0, KB, 2 * KB, 3 * KB
        tmp = tile(ctx, "tmp", [P, GB, T])
        ssum = tile(ctx, "sum_sq_cols", [P, 3])
        rcol = tile(ctx, "r_cols", [P, 3])
        zlast = tile(ctx, "z_last", [P, CW // P, (TAPS - 1) * (1 + NB)])
        sqacc = tile(ctx, "sq_acc", [P, GB, TO])

        heads = ExitStack()
        mask = tile(heads, "mask", [P, TP])
        smask = tile(heads, "sample_mask", [TS, NB, DS])
        onehot = tile(heads, "onehot", [TS, NB])
        acol = tile(heads, "a_cols", [P, 4, H])
        wkcol = tile(heads, "wk_cols", [P, 4, H])
        deccol = tile(heads, "decay_cols", [NB, H])
        stT = tile(heads, "conv_state_T", [P, CW // P, NB, TAPS - 1])
        nT = tile(heads, "n_T", [P, GB, NB, H])
        rows = tile(heads, "rows", [H, RW])
        mrw = tile(heads, "m_row", [H, T])
        with ExitStack() as st:
            xtok = tile(st, "x_tok", [P, 3, D])
            gw = tile(st, "gate_w", [P, KB, 32])
            gh = tile(st, "gate_w_high", [P, KB, P], F32R)
            gl = tile(st, "gate_w_low", [P, KB, P], F32R)
            keep = tile(st, "keep_row", [H, T])
            fall = tile(st, "reset_row", [H, T])
            igr = tile(st, "ig_row", [H, T])
            fgr = tile(st, "fg_row", [H, T])
            e1r = tile(st, "e1_row", [H, T])
            brw = tile(st, "b_row", [H, T])
            arw = tile(st, "a_row", [H, T])
            a1r = tile(st, "a1_row", [H, T])
            wkr = tile(st, "wk_row", [H, T])
            wir = tile(st, "wint_row", [H, NB, DS])
            decr = tile(st, "decay_row", [H, NB])
            bi = tile(st, "ig_bias", [H, 1])
            bf = tile(st, "fg_bias", [H, 1])
            m0 = tile(st, "m0_row", [H, NB])
            brows = tile(st, "bias_rows", [NB1 + NB2, P])
            vrows = tile(st, "vec_rows", [3 * KB + TAPS * CW // P, P])
            crows = tile(st, "conv_rows", [NB * (TAPS - 1), CW])
            nrows = tile(st, "n_rows", [NB * H, DK])
            rdiag = tile(st, "r_diag", [P, 3, P])
        with ExitStack() as st:
            Cs = tile(st, "C_state", [P, NB, GB, DV])
            kwm = tile(st, "kw_masked", [TS, NB // 2, DK])
            kw = tile(st, "kw_tok", [P, 4, DK])
            vt = tile(st, "v_tok", [P, 4, DV])
            E = tile(st, "key_weights", [P, SW])
            S = tile(st, "scores", [P, SW])
            qT = tile(st, "q_T", [P, GB, T])
            kT = tile(st, "k_T", [P, GB, T])
            vT = tile(st, "v_T", [P, GB, T])
            hT = tile(st, "h_T", [P, GB, TO])
            zu = tile(st, "zu", [P, GB, T])
            zp = tile(st, "z_prompt", [P, GB, TP])
            zs = tile(st, "z_sample", [P, GB, NB, DS + TAPS - 1])
            rowh = tile(st, "rows_head", [H, RW])
            bc = tile(st, "rows_bc", [P, RW])
            den = tile(st, "den", [P, TO])
            qw = tile(st, "q_inter", [P, GB, NB, DS])
            qn = tile(st, "q_n", [P, GB, NB, DS])
            cpo = tile(st, "C_prompt_out", [P, GB, DV])
            npo = tile(st, "n_prompt_out", [1, DK])
            nin = tile(st, "n_in", [NB, DK])
            nso = tile(st, "n_sample_out", [NB, DK])
            ha = tile(st, "h_a", [P, MW // P, TO])
            yb = tile(st, "y_b", [P, CW // P, TO])
        heads.close()
        with ExitStack() as st:
            hah = tile(st, "h_a_high", [P, MW // P, TO], F32R)
            hal = tile(st, "h_a_low", [P, MW // P, TO], F32R)
            ybh = tile(st, "y_b_high", [P, CW // P, TO], F32R)
            ybl = tile(st, "y_b_low", [P, CW // P, TO], F32R)
            mgh = tile(st, "merged_high", [P, KB, TO], F32R)
            mgl = tile(st, "merged_low", [P, KB, TO], F32R)
            clast = tile(st, "conv_last", [(TAPS - 1) * (1 + NB), CW])
        sga, sgb = tmp[:, :, 0:TO], sqacc[:]
        with ExitStack() as st:
            uh = tile(st, "u_high", [P, KB, TO], F32R)
            ul = tile(st, "u_low", [P, KB, TO], F32R)
            yo = tile(st, "y_out", [P, 3, D])
            gfb = tile(st, "g_final_bc", [P, D])
            ur = tile(st, "u_relu", [P, GB, TO])
            uq = tile(st, "u_squared", [P, GB, TO])

        ps = ctx.enter_context(nc.psum_tensor("ps", [P, 8, 512], F32))
        ACC = [ps[:, 0:2, :], ps[:, 2:4, :], ps[:, 6:8, :]]
        M = [ps[:, 4 + n, :] for n in range(4)]
        HEAD_ACC = [0, 1, 0, 1, 0, 1, 2]
        YBANK = [0, 1, 2, 3, 5, 6]

        landed = [sem(f"raw_landed{s}") for s in range(RING)]
        high_done = sem("high_done")
        low_done = sem("low_done")
        unit_used = sem("unit_used")
        evacuated = sem("evacuated")
        biased = sem("biased")
        s_const = sem("const_built")
        s_vrows = sem("vec_rows_in")
        s_brows = sem("bias_rows_in")
        s_xtok = [sem(f"x_tok_in{n}") for n in range(3)]
        s_gw = sem("gate_w_in")
        s_small = sem("small_in")
        s_colT = sem("cols_transposed")
        s_col = sem("cols_ready")
        s_xtr = sem("x_transposed")
        s_xT = sem("x_T_ready")
        s_xh = sem("x_high_ready")
        s_xl = sem("x_low_ready")
        s_sq = sem("sum_sq_ready")
        s_ms = sem("mean_sq_ready")
        s_rt = sem("root_ready")
        s_rc = sem("r_col_ready")
        s_rd = sem("r_diag_ready")
        s_rm = sem("r_bc_product")
        s_r = sem("r_bc_ready")
        s_gz = sem("gate_w_zeroed")
        s_ghl = sem("gate_w_split")
        s_gp = sem("gate_product")
        s_row = sem("row_step")
        s_rowa = sem("row_step_act")
        s_rowT = sem("rows_transposed")
        s_rowc = sem("row_cols_ready")
        s_rowh = sem("rows_head_ready")
        s_bcp = sem("rows_bc_product")
        s_bc = sem("rows_bc_ready")
        s_x = sem("exponent_ready")
        s_e = sem("key_weights_ready")
        s_qw = sem("q_inter_ready")
        s_qn = sem("q_n_ready")
        s_ktr = sem("k_transposed")
        s_kw = sem("kw_ready")
        s_kwm = sem("kw_masked_ready")
        s_sc = sem("score_product")
        s_s = sem("scores_ready")
        s_vtr = sem("v_transposed")
        s_vt = sem("v_tok_ready")
        s_num = sem("num_den_product")
        s_abs = sem("abs_den_ready")
        s_den = sem("den_steps")
        s_h = sem("h_ready")
        s_cpp = sem("C_prompt_product")
        s_cpo = sem("C_prompt_ready")
        s_nso = sem("n_sample_ready")
        s_cup = sem("C_update_product")
        s_cst = sem("C_state_new")
        s_Cin = sem("C_state_in")
        s_nin = sem("n_in")
        s_out = sem("state_stored")
        s_z = sem("z_ready")
        s_cv = sem("conv_step")
        s_yb = sem("y_b_ready")
        s_ha = sem("h_a_ready")
        s_hyh = sem("h_y_high")
        s_hyl = sem("h_y_low")
        s_clt = sem("conv_last_transposed")
        s_clo = sem("conv_last_ready")
        s_mout = sem("m_stored")
        s_cout = sem("conv_stored")
        s_sga = sem("gate_a_ready")
        s_sgb = sem("gate_b_ready")
        s_mgs = sem("merged_step")
        s_mgh = sem("merged_high_ready")
        s_mgl = sem("merged_low_ready")
        s_x1 = sem("x1_ready")
        s_x1h = sem("x1_high_ready")
        s_x1q = sem("x1_sq_ready")
        s_x1l = sem("x1_low_ready")
        s_acc = sem("sq_acc_step")
        s_r2p = sem("r2_product")
        s_r2 = sem("r2_step")
        s_r2a = sem("r2_root")
        s_uq = sem("u_sq_ready")
        s_uh = sem("u_high_ready")
        s_ul = sem("u_low_ready")
        s_x2 = sem("x2_ready")
        s_x2q = sem("x2_sq_ready")
        s_ac2 = sem("sq_acc2_step")
        s_r3p = sem("r3_product")
        s_r3 = sem("r3_step")
        s_r3a = sem("r3_root")
        s_yt = sem("y_transposed")
        s_y = sem("y_ready")
        s_yout = sem("y_stored")
        s_gfb = sem("g_final_in")

        def cut(w):
            return w[0].rearrange("(u k p) n -> p u k n", k=UK, p=P)

        win, wpa, wpb, wwo, wup, wdn = (cut(w) for w in (w_in, p_a, p_b, w_o, w_up, w_down))
        NU = D // (P * UK)

        block = ctx.enter_context(nc.Block())

        @block.sync
        def _(sp):
            sp.sem_inc(s_out, 16)
            sp.dma_start(xtok[0:NMETA, 0, :], meta).then_inc(s_xtok[0], 16)
            sp.dma_start(xtok[NMETA:P, 0, :], x_prompt[0, 0:P - NMETA, :]).then_inc(s_xtok[0], 16)
            sp.dma_start(xtok[:, 1, :], x_prompt[0, P - NMETA:2 * P - NMETA, :]).then_inc(s_xtok[1], 16)
            sp.dma_start(xtok[0:NMETA, 2, :], x_prompt[0, SEQ - NMETA:SEQ, :]).then_inc(s_xtok[2], 16)
            sp.dma_start(xtok[NMETA:NMETA + TS, 2, :],
                         x_sample.rearrange("b t d -> (b t) d")).then_inc(s_xtok[2], 16)
            sp.dma_start(gw[:], w_in[0, :, CG:CG + 32].rearrange("(k p) n -> p k n", p=P)).then_inc(s_gw, 16)

            def stream(base, s, w, part, col):
                sp.wait_ge(low_done, base + s + 1)
                sp.dma_start(raw[:, s % RING:s % RING + 1], w[:, ds(part, 1), :, ds(col, GC)]) \
                  .then_inc(landed[s % RING], 16)

            with sp.Fori(0, H) as h:
                for g, col in enumerate((CQ, CK, CV, CU, CC, CB, CO)):
                    for u in range(NU):
                        stream(UH * h, 4 * g + u, win, u, col + GC * h)
                    if g == 1:
                        sp.wait_ge(s_xh, KB)
                        sp.wait_ge(s_sq, 3)
                        sp.wait_ge(s_out, 16 + 80 * h)
                        for d in range(GB):
                            sp.dma_start(Cs[:, :, d, :], state_C[0, :, ds(h, 1), P * d:P * d + P, :]
                                         .rearrange("b o p e -> p (b o) e")).then_inc(s_Cin, 16)
                        sp.dma_start(nin[:], state_n[0, :, ds(h, 1), :].rearrange("b o d -> b (o d)")) \
                            .then_inc(s_nin, 16)
                sp.wait_ge(s_cpo, 2 * h + 2)
                sp.dma_start(C_prompt[0, :, ds(h, 1), :, :]
                             .rearrange("b o (g p) e -> p (b o g) e", p=P), cpo[:]).then_inc(s_out, 16)
                sp.dma_start(n_prompt[0, :, ds(h, 1), :].rearrange("b o d -> b (o d)"), npo[:]) \
                    .then_inc(s_out, 16)
                sp.wait_ge(s_nso, h + 1)
                sp.dma_start(n_sample[0, :, ds(h, 1), :].rearrange("b o d -> b (o d)"), nso[:]) \
                    .then_inc(s_out, 16)
                sp.wait_ge(s_cst, 1 + 8 * h + 8)
                for d in range(GB):
                    sp.dma_start(C_sample[0, :, ds(h, 1), P * d:P * d + P, :]
                                 .rearrange("b o p e -> p (b o) e"), Cs[:, :, d, :]).then_inc(s_out, 16)
            with sp.Fori(1, NMG + 1) as j1:
                first = U_MERGE - 12 + 12 * j1
                for g, col in enumerate((CGA, CGB)):
                    for u in range(NU):
                        stream(first, 4 * g + u, win, u, GC * j1 + (col - GC))
                for g, w in enumerate((wpa, wpb)):
                    for u in range(MW // (P * UK)):
                        stream(first, 8 + 2 * g + u, w, u, GC * j1 + (-GC))
            with sp.Fori(0, NMG) as j:
                for u in range(NU):
                    stream(U_WO + 4 * j, u, wwo, u, GC * j)
            with sp.Fori(0, NCH) as c:
                with sp.Fori(0, NMG) as j:
                    for u in range(NU):
                        stream(U_FF + UCH * c + 4 * j, u, wup, u, D * c + GC * j)
                with sp.Fori(0, NMG) as j:
                    for u in range(NU):
                        stream(U_FF + UCH * c + 4 * NMG + 4 * j, u, wdn, NU * c + u, GC * j)
            for n, (t0, nt) in enumerate(((0, P), (P, P))):
                sp.wait_ge(s_y, 4 * n + 4)
                sp.dma_start(y_prompt[0, t0:t0 + nt, :], yo[:, n, :]).then_inc(s_yout, 16)
            sp.wait_ge(s_y, 12)
            sp.dma_start(y_sample.rearrange("b t d -> (b t) d"), yo[0:TS, 2, :]).then_inc(s_yout, 16)
            sp.wait_ge(s_yout, 48)
            sp.wait_ge(s_out, 16 + 16 * 5 * H)
            sp.wait_ge(s_mout, 32)
            sp.wait_ge(s_cout, 32)

        @block.gpsimd
        def _(pool):
            g = nc.gpsimd
            g.memset(ident[:], 0.0).then_inc(s_const, 1)
            g.memset(ones[:], 1.0).then_inc(s_const, 1)
            g.memset(mask[:], 0.0).then_inc(s_const, 1)
            g.memset(smask[:], 0.0).then_inc(s_const, 1)
            g.memset(onehot[:], 1.0).then_inc(s_const, 1)
            g.memset(keep[:], 1.0).then_inc(s_const, 1)
            g.memset(fall[:], 0.0).then_inc(s_const, 1)
            pool.wait_ge(s_const, 7)
            g.affine_select(out=ident[:], in_=ident[:], compare_op=ALU.not_equal, fill=1.0, base=0,
                            pattern=[[1, P]], channel_multiplier=-1).then_inc(s_const, 1)
            g.affine_select(out=mask[:], in_=mask[:], compare_op=ALU.is_ge, fill=BIG, base=0,
                            pattern=[[1, TP]], channel_multiplier=-1).then_inc(s_const, 1)
            g.affine_select(out=smask[:], in_=smask[:], compare_op=ALU.is_ge, fill=BIG, base=0,
                            pattern=[[DS, NB], [1, DS]], channel_multiplier=-1).then_inc(s_const, 1)
            g.affine_select(out=onehot[:], in_=onehot[:], compare_op=ALU.is_ge, fill=0.0, base=0,
                            pattern=[[-DS, NB]], channel_multiplier=1).then_inc(s_const, 1)
            g.memset(keep[:, 0:1], 0.0).then_inc(s_const, 1)
            g.memset(keep[:, TP:T:DS], 0.0).then_inc(s_const, 1)
            g.memset(fall[:, 0:1], -FAR).then_inc(s_const, 1)
            g.memset(fall[:, TP:T:DS], -FAR).then_inc(s_const, 1)
            pool.wait_ge(s_const, 15)
            g.affine_select(out=smask[:], in_=smask[:], compare_op=ALU.is_ge, fill=BIG, base=0,
                            pattern=[[-DS, NB], [0, DS]], channel_multiplier=1).then_inc(s_const, 1)
            g.affine_select(out=onehot[:], in_=onehot[:], compare_op=ALU.is_ge, fill=0.0, base=DS - 1,
                            pattern=[[DS, NB]], channel_multiplier=-1).then_inc(s_const, 1)
            pool.wait_ge(s_row, 9)
            with nc.allow_non_contiguous_dma(reason="36 stabilisers"):
                pool.dma_start(m_prompt.rearrange("l b h -> h (l b)"), mrw[:, TP - 1:TP]).then_inc(s_mout, 16)
                pool.dma_start(m_sample.rearrange("l b h -> h (l b)"), mrw[:, TP + DS - 1:T:DS]) \
                    .then_inc(s_mout, 16)
            with pool.Fori(0, H) as h:
                for half in range(2):
                    if half == 0:
                        pool.wait_ge(s_kw, h + 1)
                    pool.wait_ge(s_cup, 1 + 8 * h + 4 * half)
                    k3 = kw[0:TS, 3:4, :].to_broadcast([TS, NB // 2, DK])
                    oh = onehot[:, 4 * half:4 * half + 4].unsqueeze(2).to_broadcast([TS, NB // 2, DK])
                    g.tensor_tensor(kwm[:], k3, oh, ALU.mult).then_inc(s_kwm, 1)
            pool.wait_ge(s_clo, 1)
            pool.dma_start(conv_prompt[0, 0], clast[0:TAPS - 1, :]).then_inc(s_cout, 16)
            pool.dma_start(conv_sample[0].rearrange("b r c -> (b r) c"),
                           clast[TAPS - 1:, :]).then_inc(s_cout, 16)
            pool.wait_ge(evacuated, 2 + G_FF)
            pool.dma_start(gfb[:], g_final.partition_broadcast(P)).then_inc(s_gfb, 16)

        @block.scalar
        def _(act):
            a = nc.scalar
            for s in (s_mgh, s_uh):
                act.sem_inc(s, 1)
            act.dma_start(vrows[0:KB, :], g_mix.rearrange("l (k p) -> (l k) p", p=P)).then_inc(s_vrows, 16)
            act.dma_start(vrows[KB:2 * KB, :], g_ffn.rearrange("l (k p) -> (l k) p", p=P)).then_inc(s_vrows, 16)
            act.dma_start(vrows[2 * KB:3 * KB, :], g_final.rearrange("(k p) -> k p", p=P)).then_inc(s_vrows, 16)
            act.dma_start(vrows[3 * KB:, :], w_conv.rearrange("l r (k p) -> (l r k) p", p=P)).then_inc(s_vrows, 16)
            act.dma_start(brows[0:NB1, :], b_in[0, 0:CG].rearrange("(k p) -> k p", p=P)).then_inc(s_brows, 16)
            act.dma_start(brows[NB1:, :], b_in[0, CO:].rearrange("(k p) -> k p", p=P)).then_inc(s_brows, 16)
            act.dma_start(crows[:], state_conv[0].rearrange("b r c -> (b r) c")).then_inc(s_brows, 16)
            act.dma_start(nrows[:], state_n[0].rearrange("b h d -> (b h) d")).then_inc(s_brows, 16)
            with nc.allow_non_contiguous_dma(reason="40 numbers"):
                act.dma_start(bi[:], b_in[0, CG:CG + H].rearrange("(h o) -> h o", o=1)).then_inc(s_small, 16)
                act.dma_start(bf[:], b_in[0, CG + H:CO].rearrange("(h o) -> h o", o=1)).then_inc(s_small, 16)
                act.dma_start(m0[:], state_m[0].rearrange("b h -> h b")).then_inc(s_small, 16)

            for n, nt in enumerate((P, P, NMETA + TS)):
                act.wait_ge(s_xtok[n], 16 if n == 1 else 32)
                if n > 0:
                    act.wait_ge(s_sq, n)
                a.activation(wh[0:nt, 0:2].rearrange("p s k n -> p (s k n)"), xtok[0:nt, n, :], ACT.Square,
                             accum_out=ssum[0:nt, n:n + 1]).then_inc(s_sq, 1)
            act.wait_ge(s_gw, 16)
            act.wait_ge(s_gz, 1)
            a.activation(gh[:, :, 0:H], gw[:, :, 0:H], ACT.Copy).then_inc(s_ghl, 1)
            a.activation(gh[:, :, 32:32 + H], gw[:, :, H:2 * H], ACT.Copy).then_inc(s_ghl, 1)
            act.wait_ge(s_col, 1)
            for k in range(KB):
                act.wait_ge(s_xT, k // 2 + 1)
                a.activation(xh[:, k, :], xT[:, k, :], ACT.Copy, scale=vecT[:, VG + k:VG + k + 1]).then_inc(s_xh, 1)
            act.wait_ge(s_ms, 1)
            a.activation(ssum[:, 0:2], ssum[:, 0:2], ACT.Sqrt).then_inc(s_rt, 1)
            a.activation(ssum[0:NMETA + TS, 2:3], ssum[0:NMETA + TS, 2:3], ACT.Sqrt).then_inc(s_rt, 1)

            def split(base, s):
                q = s // RING
                act.wait_ge(landed[s % RING], 4 * base + 16 * q + 16)
                act.wait_ge(unit_used, base + s + 1)
                a.activation(wh[:, s % RING], raw[:, s % RING], ACT.Copy).then_inc(high_done, 1)

            act.wait_ge(s_sq, 3)
            for n in range(LEAD):
                split(0, n)
            act.wait_ge(s_row, 1)
            a.activation(e1r[:], fgr[:], ACT.Abs).then_inc(s_rowa, 1)
            act.wait_ge(s_rowa, 1)
            a.activation(e1r[:], e1r[:], ACT.Exp, scale=-1.0).then_inc(s_rowa, 1)
            act.wait_ge(s_rowa, 2)
            a.activation(e1r[:], e1r[:], ACT.Ln, bias=1.0).then_inc(s_rowa, 1)
            act.wait_ge(s_row, 9)
            a.activation(rows[:, REM:REM + TO], mrw[:, T0:T], ACT.Exp, scale=-1.0).then_inc(s_rowa, 1)
            act.wait_ge(s_row, 11)
            a.activation(rows[:, RWI:RWI + TS].rearrange("p (b t) -> p b t", t=DS), wir[:], ACT.Exp).then_inc(s_rowa, 1)
            a.activation(wkr[:], wkr[:], ACT.Exp).then_inc(s_rowa, 1)
            act.wait_ge(s_rowT, 1)

            with act.Fori(0, H) as h:
                def add_bias(g, out, col, func=ACT.Identity):
                    act.wait_ge(evacuated, 2 + GH * h + g + 1)
                    for b in range(GB):
                        ins = a.activation(out[:, b, :], tmp[:, b, 0:out.shape[2]], func,
                                           bias=biasT[:, ds(col + GB * h + b, 1)])
                    ins.then_inc(biased, 1)

                for p in range(UH):
                    split(UH * h, p + LEAD)
                    if p == 1:
                        act.wait_ge(s_bcp, 1 + h + 1)
                        act.wait_ge(s_cst, 1 + 8 * h)
                        act.wait_ge(s_den, 1 + 2 * h)
                        act.wait_ge(s_rowT, 1)
                        a.activation(bc[:], ps[:, 4:6, :].rearrange("p b n -> p (b n)")[:, 0:RW],
                                     ACT.Copy).then_inc(s_bc, 1)
                    if p == 3:
                        add_bias(0, qT, BQ)
                    if p == 5:
                        act.wait_ge(s_x, h + 1)
                        for n, ((k0, nk), (q0, nq, off)) in enumerate(zip(KT, QT)):
                            ins = a.activation(E[0:nk, off:off + nq], E[0:nk, off:off + nq], ACT.Exp, scale=-1.0,
                                               bias=acol[0:nk, n, ds(h, 1)])
                        ins.then_inc(s_e, 1)
                    if p == 7:
                        add_bias(1, kT, BK)
                    if p == 9:
                        act.wait_ge(s_ktr, h + 1)
                        act.wait_ge(s_cup, 1 + 8 * h)
                        for n, (k0, nk) in enumerate(KT):
                            ins = a.activation(kw[0:nk, n, :], M[n // 2][0:nk, (n % 2) * DK:(n % 2 + 1) * DK],
                                               ACT.Copy, scale=wkcol[0:nk, n, ds(h, 1)])
                        ins.then_inc(s_kw, 1)
                    if p == 11:
                        add_bias(2, vT, BV)
                    if p == 13:
                        act.wait_ge(s_vtr, h + 1)
                        for n, (k0, nk) in enumerate(KT):
                            ins = a.activation(vt[0:nk, n, :], M[n // 2][0:nk, (n % 2) * DV:(n % 2 + 1) * DV],
                                               ACT.Copy)
                        ins.then_inc(s_vt, 1)
                    if p == 15:
                        add_bias(3, zu, BU)
                        act.wait_ge(s_num, 1 + h + 1)
                        a.activation(den[:], M[0][:, 0:TO], ACT.Abs).then_inc(s_abs, 1)
                    if p == 17:
                        act.wait_ge(s_cpp, h + 1)
                        act.wait_ge(s_out, 16 + 80 * h)
                        a.activation(cpo[:].rearrange("p g e -> p (g e)"), M[0], ACT.Copy).then_inc(s_cpo, 1)
                        a.activation(npo[:], M[1][0:1, 0:DK], ACT.Copy).then_inc(s_cpo, 1)
                    if p == 19:
                        add_bias(4, tmp, BC_)
                    if p == 23:
                        add_bias(5, tmp[:, :, 0:TO], BB)
                    if p == 27:
                        add_bias(6, tmp[:, :, 0:TO], BO, ACT.Sigmoid)

            act.wait_ge(s_ha, 1 + H)
            act.wait_ge(s_out, 16 + 80 * H)
            act.wait_ge(s_cst, 1 + 8 * H)
            act.wait_ge(s_mout, 32)
            a.activation(hah[:], ha[:], ACT.Copy).then_inc(s_hyh, 1)
            act.wait_ge(s_yb, H)
            a.activation(ybh[:], yb[:], ACT.Copy).then_inc(s_hyh, 1)

            act.wait_ge(s_clt, 1)
            act.wait_ge(s_hyl, 2)
            a.activation(clast[:], ps[0:clast.shape[0], 4:6, :].rearrange("p b n -> p (b n)"), ACT.Copy) \
                .then_inc(s_clo, 1)

            with act.Fori(0, NMG) as j:
                for p in range(12):
                    split(U_MERGE + 12 * j, p + LEAD)
                    for pos, g, gate, done, col in ((3, 0, sga, s_sga, BGA), (7, 1, sgb, s_sgb, BGB)):
                        if p == pos:
                            act.wait_ge(evacuated, 2 + G_MERGE + 4 * j + g + 1)
                            for b in range(GB):
                                ins = a.activation(gate[:, b, :], gate[:, b, :], ACT.Sigmoid,
                                                   bias=biasT[:, ds(col + GB * j + b, 1)])
                            ins.then_inc(done, 1)
                    if p == 11:
                        act.wait_ge(s_mgs, 1 + 2 * j + 2)
                        a.activation(mgh[:, ds(GB * j, GB), :], sga, ACT.Copy).then_inc(s_mgh, 1)

            with act.Fori(0, NMG // 2) as jj:
                for pair in range(2):
                    j = 2 * jj + pair
                    for p in range(NU):
                        split(U_WO + 8 * jj, 4 * pair + p + LEAD)
                    act.wait_ge(evacuated, 2 + G_WO + j + 1)
                    act.wait_ge(s_acc, j + 1)
                    a.activation(tmp[:, :, 0:TO], xT[:, ds(GB * j, GB), T0:T], ACT.Square).then_inc(s_x1q, 1)
                    for b in range(GB):
                        ins = a.activation(xh[:, ds(GB * j + b, 1), T0:T], xT[:, ds(GB * j + b, 1), T0:T], ACT.Copy,
                                           scale=vecT[:, ds(VF + GB * j + b, 1)])
                    ins.then_inc(s_x1h, 1)
            act.wait_ge(s_r2, 2)
            a.activation(rbc[:, 0:TO], rbc[:, 0:TO], ACT.Sqrt).then_inc(s_r2a, 1)

            def ffn(c, last):
                with act.Fori(0, NMG // 2) as jj:
                    for pair in range(2):
                        j = 2 * jj + pair
                        for p in range(NU):
                            split(U_FF + UCH * c + 8 * jj, 4 * pair + p + LEAD)
                        act.wait_ge(s_uq, 1 + NMG * c + j + 1)
                        a.activation(uh[:, ds(GB * j, GB), :], uq[:], ACT.Copy).then_inc(s_uh, 1)

                def down(jj, tail):
                    for pair in range(2):
                        for p in range(NU):
                            if not (tail and pair == 1 and p + LEAD >= NU):
                                split(U_FF + UCH * c + 4 * NMG + 8 * jj, 4 * pair + p + LEAD)
                        if last:
                            j = 2 * jj + pair
                            act.wait_ge(evacuated, 2 + G_FF + 2 * NMG * c + NMG + j + 1)
                            act.wait_ge(s_ac2, j + 1)
                            a.activation(tmp[:, :, 0:TO], xT[:, ds(GB * j, GB), T0:T], ACT.Square).then_inc(s_x2q, 1)

                with act.Fori(0, NMG // 2 - 1 if last else NMG // 2) as jj:
                    down(jj, False)
                if last:
                    down(NMG // 2 - 1, True)

            with act.Fori(0, NCH - 1) as c:
                ffn(c, False)
            ffn(NCH - 1, True)
            act.wait_ge(s_r3, 2)
            a.activation(rcol[:, 0:2], rcol[:, 0:2], ACT.Sqrt).then_inc(s_r3a, 1)
            a.activation(rcol[0:TS, 2:3], rcol[0:TS, 2:3], ACT.Sqrt).then_inc(s_r3a, 1)

        @block.vector
        def _(dve):
            v = nc.vector
            dve.sem_inc(low_done, RING)
            dve.sem_inc(evacuated, 2)
            for s in (s_ha, s_s, s_cst, s_den, s_cv, s_mgl, s_mgs, s_uq, s_ul):
                dve.sem_inc(s, 1)
            v.memset(gh[:].bitcast(F32), 0.0)
            v.memset(gl[:].bitcast(F32), 0.0).then_inc(s_gz, 1)
            dve.wait_ge(s_colT, 1)
            v.tensor_copy(vecT[:], M[0][:, 0:vecT.shape[1]])
            v.tensor_copy(biasT[:], M[0][:, 128:128 + NB1 + NB2])
            v.tensor_copy(stT[:].rearrange("p k b r -> p (k b r)"),
                          M[0][:, 256:256 + stT.shape[1] * NB * (TAPS - 1)])
            v.tensor_copy(nT[:].rearrange("p g b h -> p (g b h)"),
                          M[0][:, 384:384 + GB * NB * H]).then_inc(s_col, 1)
            dve.wait_ge(s_gw, 16)
            dve.wait_ge(s_ghl, 2)
            v.tensor_tensor(gl[:, :, 0:H], gw[:, :, 0:H], gh[:, :, 0:H].bitcast(F32), ALU.subtract).then_inc(s_ghl, 1)
            v.tensor_tensor(gl[:, :, 32:32 + H], gw[:, :, H:2 * H], gh[:, :, 32:32 + H].bitcast(F32),
                            ALU.subtract).then_inc(s_ghl, 1)
            for k in range(KB // 2 + 1):
                if k < KB // 2:
                    dve.wait_ge(s_xtr, k + 1)
                    v.tensor_copy(xT[:, 2 * k:2 * k + 2, :], ACC[k % 2][:, :, 0:T]).then_inc(s_xT, 1)
                if k > 0:
                    for b in (2 * k - 2, 2 * k - 1):
                        dve.wait_ge(s_xh, b + 1)
                        v.scalar_tensor_tensor(xl[:, b, :], xT[:, b, :], vecT[:, VG + b:VG + b + 1],
                                               xh[:, b, :].bitcast(F32), ALU.mult, ALU.subtract).then_inc(s_xl, 1)
            nt = NMETA + TS
            dve.wait_ge(s_sq, 3)
            v.tensor_scalar(ssum[:, 0:2], ssum[:, 0:2], 1.0 / D, EPS, ALU.mult, ALU.add)
            v.tensor_scalar(ssum[0:nt, 2:3], ssum[0:nt, 2:3], 1.0 / D, EPS, ALU.mult, ALU.add).then_inc(s_ms, 1)
            dve.wait_ge(s_rt, 2)
            v.reciprocal(rcol[:, 0:2], ssum[:, 0:2]).then_inc(s_rc, 1)
            v.reciprocal(rcol[0:nt, 2:3], ssum[0:nt, 2:3]).then_inc(s_rc, 1)
            dve.wait_ge(s_rc, 2)
            dve.wait_ge(s_const, 17)
            for n, m in enumerate((P, P, nt)):
                v.tensor_scalar(rdiag[0:m, n, 0:m], ident[0:m, 0:m], rcol[0:m, n:n + 1], None,
                                ALU.mult).then_inc(s_rd, 1)

            def split(base, s):
                dve.wait_ge(high_done, base + s + 1)
                dve.wait_ge(landed[s % RING], 4 * base + 16 * (s // RING) + 16)
                dve.wait_ge(unit_used, base + s + 1)
                v.tensor_tensor(wl[:, s % RING], raw[:, s % RING], wh[:, s % RING].bitcast(F32),
                                ALU.subtract).then_inc(low_done, 1)

            dve.wait_ge(s_rm, 1)
            v.tensor_copy(rbc[:], M[2][:, 0:T]).then_inc(s_r, 1)
            for n in range(LEAD):
                split(0, n)

            step = [0]

            def row(ins):
                step[0] += 1
                ins.then_inc(s_row, 1)
                dve.wait_ge(s_row, step[0])

            samp = lambda r, c=0: r[:, c + TP:c + T].rearrange("p (b t) -> p b t", t=DS)
            dve.wait_ge(s_gp, 1)
            dve.wait_ge(s_r, 1)
            dve.wait_ge(s_small, 48)
            v.tensor_tensor(fgr[:], M[3][32:32 + H, 0:T], rbc[32:32 + H, :], ALU.mult)
            v.tensor_tensor(igr[:], M[3][0:H, 0:T], rbc[0:H, :], ALU.mult).then_inc(s_gz, 1)
            dve.wait_ge(s_gz, 2)
            row(v.tensor_scalar(fgr[:], fgr[:], bf[:, 0:1], None, ALU.add))
            row(v.tensor_scalar(igr[:], igr[:], bi[:, 0:1], None, ALU.add))
            dve.wait_ge(s_rowa, 3)
            row(v.scalar_tensor_tensor(fgr[:], fgr[:], 0.0, e1r[:], ALU.min, ALU.subtract))
            dve.wait_ge(s_const, 17)
            row(v.tensor_tensor_scan(brw[:], keep[:], fgr[:], 0.0, ALU.mult, ALU.add))
            row(v.tensor_tensor(arw[:], igr[:], brw[:], ALU.subtract))
            v.tensor_copy(a1r[:, 1:TP], arw[:, 1:TP])
            v.tensor_copy(samp(a1r)[:, :, 1:DS], samp(arw)[:, :, 1:DS])
            row(v.tensor_scalar(a1r[:, 0:1], arw[:, 0:1], 0.0, None, ALU.max))
            row(v.tensor_tensor(samp(a1r)[:, :, 0], samp(arw)[:, :, 0], m0[:], ALU.max))
            row(v.tensor_tensor_scan(rows[:, 0:T], fall[:], a1r[:], 0.0, ALU.add, ALU.max))
            row(v.tensor_tensor(mrw[:], brw[:], rows[:, 0:T], ALU.add))
            mx = samp(rows)
            row(v.tensor_tensor(wir[:], m0[:].unsqueeze(2).to_broadcast([H, NB, DS]), mx, ALU.subtract))
            v.tensor_scalar(wkr[:, 0:TP], arw[:, 0:TP], rows[:, TP - 1:TP], None, ALU.subtract)
            row(v.tensor_tensor(samp(wkr), samp(arw), mx[:, :, DS - 1:DS].to_broadcast([H, NB, DS]),
                                ALU.subtract))
            dve.wait_ge(s_rowa, 6)
            row(v.tensor_copy(decr[:], rows[:, RWI:RWI + TS].rearrange("p (b t) -> p b t", t=DS)[:, :, DS - 1]))
            dve.wait_ge(s_rowT, 1)
            for n, (k0, nk) in enumerate(KT):
                v.tensor_copy(acol[0:nk, n, :], M[0][0:nk, n * H:(n + 1) * H])
                v.tensor_scalar(wkcol[0:nk, n, :], M[0][0:nk, (4 + n) * H:(5 + n) * H], DK ** -0.5, None, ALU.mult)
            v.tensor_copy(deccol[:], M[0][0:NB, 8 * H:9 * H]).then_inc(s_rowc, 1)
            dve.wait_ge(s_rowc, 1)

            scale = rbc[:, 0:T].unsqueeze(1).to_broadcast([P, GB, T])
            scale_o = rbc[:, T0:T].unsqueeze(1).to_broadcast([P, GB, TO])

            with dve.Fori(0, H) as h:
                def evacuate(g, n):
                    dve.wait_ge(unit_used, RING + UH * h + 4 * g + 4)
                    if g > 0:
                        dve.wait_ge(biased, GH * h + g)
                    v.tensor_tensor(tmp[:, :, 0:n], ACC[HEAD_ACC[g]][:, :, 0:n], scale if n == T else scale_o,
                                    ALU.mult).then_inc(evacuated, 1)

                for p in range(UH):
                    split(UH * h, p + LEAD)
                    if p == 0:
                        dve.wait_ge(s_bcp, 1 + h)
                        v.tensor_scalar(rowh[:], rows[:], ident[0:H, ds(h, 1)], None, ALU.mult).then_inc(s_rowh, 1)
                    if p == 3:
                        dve.wait_ge(s_ha, 1 + h)
                        evacuate(0, T)
                    if p == 4:
                        dve.wait_ge(s_bc, h + 1)
                        dve.wait_ge(s_s, 1 + h)
                        for n, ((k0, nk), (q0, nq, off)) in enumerate(zip(KT, QT)):
                            m = mask[0:nk, q0 - k0:q0 - k0 + nq] if n < 3 else \
                                smask[:].rearrange("p b t -> p (b t)")
                            ins = v.scalar_tensor_tensor(E[0:nk, off:off + nq], bc[0:nk, q0:q0 + nq],
                                                         acol[0:nk, n, ds(h, 1)], m, ALU.max, ALU.add)
                        ins.then_inc(s_x, 1)
                    if p == 6:
                        dve.wait_ge(biased, GH * h + 1)
                        dve.wait_ge(s_num, 1 + h)
                        v.tensor_tensor(qw[:], qT[:, :, TP:T].rearrange("p g (b t) -> p g b t", t=DS),
                                        bc[:, RWI:RWI + TS].rearrange("p (o b t) -> p o b t", o=1, t=DS)
                                        .to_broadcast([P, GB, NB, DS]), ALU.mult).then_inc(s_qw, 1)
                        dve.wait_ge(s_qw, h + 1)
                        v.tensor_tensor(qn[:], qw[:], nT[:, :, :, ds(h, 1)].to_broadcast([P, GB, NB, DS]),
                                        ALU.mult).then_inc(s_qn, 1)
                    if p == 7:
                        evacuate(1, T)
                    if p == 10:
                        dve.wait_ge(s_sc, h + 1)
                        dve.wait_ge(s_e, h + 1)
                        dve.wait_ge(s_num, 1 + h)
                        for n, ((k0, nk), (q0, nq, off)) in enumerate(zip(KT, QT)):
                            src = M[2][0:nk, off:off + nq] if n < 2 else M[3][0:nk, off - QT[2][2]:off - QT[2][2] + nq]
                            ins = v.scalar_tensor_tensor(S[0:nk, off:off + nq], src, DK ** -0.5,
                                                         E[0:nk, off:off + nq], ALU.mult, ALU.mult)
                        ins.then_inc(s_s, 1)
                    if p == 11:
                        evacuate(2, T)
                    if p == 15:
                        dve.wait_ge(s_cv, 1 + 12 * h)
                        evacuate(3, T)
                        dve.wait_ge(s_abs, h + 1)
                        v.tensor_tensor(den[:], den[:], bc[:, REM:REM + TO], ALU.max).then_inc(s_den, 1)
                        dve.wait_ge(s_den, 1 + 2 * h + 1)
                        v.reciprocal(den[:], den[:]).then_inc(s_den, 1)
                        dve.wait_ge(s_den, 1 + 2 * h + 2)
                        v.tensor_tensor(hT[:], ps[:, 6:8, 0:TO], den[:].unsqueeze(1).to_broadcast([P, GB, TO]),
                                        ALU.mult).then_inc(s_h, 1)
                    if p == 17:
                        dve.wait_ge(s_cpp, h + 1)
                        dve.wait_ge(s_cpo, 2 * h + 2)
                        dve.wait_ge(s_nin, 16 * h + 16)
                        dve.wait_ge(s_out, 16 + 80 * h)
                        v.scalar_tensor_tensor(nso[:], nin[:], deccol[:, ds(h, 1)], M[1][0:NB, DK:2 * DK],
                                               ALU.mult, ALU.add).then_inc(s_nso, 1)
                    if p == 19:
                        evacuate(4, T)
                        dve.wait_ge(biased, GH * h + 5)
                        v.tensor_copy(zs[:, :, :, 0:TAPS - 1], stT[:, ds(GB * h, GB), :, :])
                        v.tensor_tensor(zp[:], tmp[:, :, 0:TP], zu[:, :, 0:TP], ALU.mult)
                        v.tensor_tensor(zs[:, :, :, TAPS - 1:], tmp[:, :, TP:T].rearrange("p g (b t) -> p g b t", t=DS),
                                        zu[:, :, TP:T].rearrange("p g (b t) -> p g b t", t=DS), ALU.mult) \
                            .then_inc(s_z, 1)
                        dve.wait_ge(s_z, h + 1)
                        v.tensor_copy(zlast[:, ds(GB * h, GB), 0:TAPS - 1], zp[:, :, TP - TAPS + 1:TP])
                        v.tensor_copy(zlast[:, ds(GB * h, GB), TAPS - 1:].rearrange("p g (b r) -> p g b r", r=TAPS - 1),
                                      zs[:, :, :, DS:DS + TAPS - 1])
                    if p in (18, 19, 21, 22):
                        for b in range(2 * {18: 0, 19: 1, 21: 2, 22: 3}[p], 2 * {18: 0, 19: 1, 21: 2, 22: 3}[p] + 2):
                            dve.wait_ge(s_cup, 1 + 8 * h + b + 1)
                            bank = M[2 + b % 2] if b % 4 < 2 else M[b % 2]
                            v.scalar_tensor_tensor(Cs[:, b].rearrange("p g e -> p (g e)"),
                                                   Cs[:, b].rearrange("p g e -> p (g e)"),
                                                   bc[:, RWI + DS * b + DS - 1:RWI + DS * b + DS], bank,
                                                   ALU.mult, ALU.add).then_inc(s_cst, 1)
                    if p in (20, 21):
                        b = p - 20
                        out_p, out_s = zu[:, b, 0:SEQ], zu[:, b, SEQ:TO].rearrange("p (b t) -> p b t", t=DS)
                        for r in range(TAPS):
                            w = vecT[:, ds(VC + r * (CW // P) + GB * h + b, 1)]
                            src_p = zp[:, b, T0 - TAPS + 1 + r:T0 - TAPS + 1 + r + SEQ]
                            src_s = zs[:, b, :, r:r + DS]
                            for out, src in ((out_p, src_p), (out_s, src_s)):
                                if r == 0:
                                    v.tensor_scalar(out, src, w, None, ALU.mult).then_inc(s_cv, 1)
                                else:
                                    v.scalar_tensor_tensor(out, src, w, out, ALU.mult, ALU.add).then_inc(s_cv, 1)
                            dve.wait_ge(s_cv, 1 + 12 * h + 6 * b + 2 * r + 2)
                    if p == 23:
                        dve.wait_ge(s_z, h + 1)
                        evacuate(5, TO)
                        dve.wait_ge(biased, GH * h + 6)
                        v.tensor_tensor(yb[:, ds(GB * h, GB), :], tmp[:, :, 0:TO], zu[:, :, 0:TO], ALU.mult) \
                            .then_inc(s_yb, 1)
                    if p == 27:
                        dve.wait_ge(s_yb, h + 1)
                        evacuate(6, TO)
                        dve.wait_ge(biased, GH * h + 7)
                        dve.wait_ge(s_h, h + 1)
                        v.tensor_tensor(ha[:, ds(GB * h, GB), :], tmp[:, :, 0:TO], hT[:], ALU.mult).then_inc(s_ha, 1)

            dve.wait_ge(s_ha, 1 + H)
            dve.wait_ge(s_hyh, 1)
            v.tensor_tensor(hal[:], ha[:], hah[:].bitcast(F32), ALU.subtract).then_inc(s_hyl, 1)
            dve.wait_ge(s_hyh, 2)
            v.tensor_tensor(ybl[:], yb[:], ybh[:].bitcast(F32), ALU.subtract).then_inc(s_hyl, 1)
            dve.wait_ge(s_hyl, 2)

            with dve.Fori(0, NMG) as j:
                def evacuate_gate(g, gate):
                    dve.wait_ge(unit_used, RING + U_MERGE + 12 * j + 4 * g + 4)
                    v.tensor_tensor(gate, ACC[g][:, :, 0:TO], scale_o, ALU.mult).then_inc(evacuated, 1)

                for p in range(12):
                    split(U_MERGE + 12 * j, p + LEAD)
                    if p == 3:
                        dve.wait_ge(s_mgh, 1 + j)
                        dve.wait_ge(s_mgl, 1 + j)
                        evacuate_gate(0, sga)
                    if p == 7:
                        dve.wait_ge(s_mgs, 1 + 2 * j)
                        evacuate_gate(1, sgb)
                    if p == 9:
                        dve.wait_ge(s_sga, j + 1)
                        dve.wait_ge(unit_used, RING + U_MERGE + 12 * j + 10)
                        v.tensor_tensor(sga, ACC[0][:, :, 0:TO], sga, ALU.mult).then_inc(evacuated, 1)
                    if p == 11:
                        dve.wait_ge(s_sgb, j + 1)
                        dve.wait_ge(unit_used, RING + U_MERGE + 12 * j + 12)
                        v.tensor_tensor(sgb, ACC[1][:, :, 0:TO], sgb, ALU.mult).then_inc(evacuated, 1)
                        dve.wait_ge(evacuated, 2 + G_MERGE + 4 * j + 4)
                        v.tensor_tensor(sga, sga, sgb, ALU.add).then_inc(s_mgs, 2)
                        dve.wait_ge(s_mgh, 1 + j + 1)
                        v.tensor_tensor(mgl[:, ds(GB * j, GB), :], sga, mgh[:, ds(GB * j, GB), :].bitcast(F32),
                                        ALU.subtract).then_inc(s_mgl, 1)

            v.memset(sqacc[:], 0.0).then_inc(s_acc, 1)
            with dve.Fori(0, NMG // 2) as jj:
                for pair in range(2):
                    j = 2 * jj + pair
                    for p in range(NU):
                        split(U_WO + 8 * jj, 4 * pair + p + LEAD)
                    dve.wait_ge(unit_used, RING + U_WO + 8 * jj + 4 * pair + 4)
                    x1 = xT[:, ds(GB * j, GB), T0:T]
                    v.tensor_tensor(x1, ACC[pair][:, :, 0:TO], x1, ALU.add).then_inc(evacuated, 1)
                    dve.wait_ge(s_x1q, j + 1)
                    dve.wait_ge(s_acc, j + 1)
                    v.tensor_tensor(sqacc[:], sqacc[:], tmp[:, :, 0:TO], ALU.add).then_inc(s_acc, 1)
                    dve.wait_ge(s_x1h, j + 1)
                    for b in range(GB):
                        ins = v.scalar_tensor_tensor(
                            xl[:, ds(GB * j + b, 1), T0:T], xT[:, ds(GB * j + b, 1), T0:T],
                            vecT[:, ds(VF + GB * j + b, 1)], xh[:, ds(GB * j + b, 1), T0:T].bitcast(F32),
                            ALU.mult, ALU.subtract)
                    ins.then_inc(s_x1l, 1)
            dve.wait_ge(s_acc, NMG + 1)
            v.tensor_tensor(sqacc[:, 0, :], sqacc[:, 0, :], sqacc[:, 1, :], ALU.add).then_inc(s_r2, 1)
            dve.wait_ge(s_r2p, 1)
            v.tensor_scalar(rbc[:, 0:TO], M[0][:, 0:TO], 1.0 / D, EPS, ALU.mult, ALU.add).then_inc(s_r2, 1)
            dve.wait_ge(s_r2a, 1)
            v.reciprocal(rbc[:, 0:TO], rbc[:, 0:TO]).then_inc(s_r2, 1)
            dve.wait_ge(s_r2, 3)
            scale_u = rbc[:, 0:TO].unsqueeze(1).to_broadcast([P, GB, TO])

            def ffn(c, last):
                with dve.Fori(0, NMG // 2) as jj:
                    for pair in range(2):
                        j = 2 * jj + pair
                        for p in range(NU):
                            split(U_FF + UCH * c + 8 * jj, 4 * pair + p + LEAD)
                        dve.wait_ge(unit_used, RING + U_FF + UCH * c + 8 * jj + 4 * pair + 4)
                        dve.wait_ge(s_uq, 1 + NMG * c + j)
                        v.scalar_tensor_tensor(ur[:], ACC[pair][:, :, 0:TO], 0.0, scale_u, ALU.max, ALU.mult) \
                            .then_inc(evacuated, 1)
                        dve.wait_ge(evacuated, 2 + G_FF + 2 * NMG * c + j + 1)
                        dve.wait_ge(s_uh, 1 + NMG * c + j)
                        dve.wait_ge(s_ul, 1 + NMG * c + j)
                        v.tensor_tensor(uq[:], ur[:], ur[:], ALU.mult).then_inc(s_uq, 1)
                        dve.wait_ge(s_uh, 1 + NMG * c + j + 1)
                        v.tensor_tensor(ul[:, ds(GB * j, GB), :], uq[:], uh[:, ds(GB * j, GB), :].bitcast(F32),
                                        ALU.subtract).then_inc(s_ul, 1)

                def down(jj, tail):
                    for pair in range(2):
                        base = U_FF + UCH * c + 4 * NMG + 8 * jj
                        for p in range(NU):
                            if not (tail and pair == 1 and p + LEAD >= NU):
                                split(base, 4 * pair + p + LEAD)
                        j = 2 * jj + pair
                        dve.wait_ge(unit_used, RING + base + 4 * pair + 4)
                        dve.wait_ge(evacuated, 2 + G_FF + 2 * NMG * c)
                        x2 = xT[:, ds(GB * j, GB), T0:T]
                        v.tensor_tensor(x2, ACC[pair][:, :, 0:TO], x2, ALU.add).then_inc(evacuated, 1)
                        if last:
                            dve.wait_ge(s_x2q, j + 1)
                            dve.wait_ge(s_ac2, j + 1)
                            v.tensor_tensor(sqacc[:], sqacc[:], tmp[:, :, 0:TO], ALU.add).then_inc(s_ac2, 1)

                with dve.Fori(0, NMG // 2 - 1 if last else NMG // 2) as jj:
                    down(jj, False)
                if last:
                    down(NMG // 2 - 1, True)

            with dve.Fori(0, NCH - 1) as c:
                ffn(c, False)
            v.memset(sqacc[:], 0.0).then_inc(s_ac2, 1)
            ffn(NCH - 1, True)
            dve.wait_ge(s_ac2, NMG + 1)
            v.tensor_tensor(sqacc[:, 0, :], sqacc[:, 0, :], sqacc[:, 1, :], ALU.add).then_inc(s_r3, 1)
            dve.wait_ge(s_r3p, 1)
            v.tensor_scalar(rcol[:, 0:2], M[0][:, 0:2], 1.0 / D, EPS, ALU.mult, ALU.add)
            v.tensor_scalar(rcol[0:TS, 2:3], M[0][0:TS, 2:3], 1.0 / D, EPS, ALU.mult, ALU.add).then_inc(s_r3, 1)
            dve.wait_ge(s_r3a, 2)
            v.reciprocal(rcol[:, 0:2], rcol[:, 0:2])
            v.reciprocal(rcol[0:TS, 2:3], rcol[0:TS, 2:3]).then_inc(s_r3, 1)
            dve.wait_ge(s_r3, 3)
            dve.wait_ge(s_gfb, 16)
            for i, (n, q) in enumerate((n, q) for n in range(3) for q in range(KB // 4)):
                nt = P if n < 2 else TS
                dve.wait_ge(s_yt, i + 1)
                v.scalar_tensor_tensor(yo[0:nt, n, 512 * q:512 * q + 512], ps[0:nt, YBANK[i % 6], :],
                                       rcol[0:nt, n:n + 1], gfb[0:nt, 512 * q:512 * q + 512],
                                       ALU.mult, ALU.mult).then_inc(s_y, 1)

        @block.tensor
        def _(pe):
            def product(out, lhsT, rhs, start=True, stop=True):
                return pe.matmul(out, lhsT, rhs, start=start, stop=stop)

            pe.sem_inc(unit_used, RING)
            for s in (s_bcp, s_num, s_cup):
                pe.sem_inc(s, 1)
            pe.wait_ge(s_const, 17)
            pe.wait_ge(s_vrows, 64)
            pe.wait_ge(s_brows, 64)
            nv, nb, nc2 = vrows.shape[0], brows.shape[0], crows.shape[0]
            pe.transpose(M[0][:, 0:nv], vrows[:], ident[0:nv, 0:nv])
            pe.transpose(M[0][:, 128:128 + nb], brows[:], ident[0:nb, 0:nb])
            for k in range(CW // P):
                pe.transpose(M[0][:, 256 + nc2 * k:256 + nc2 * (k + 1)], crows[:, P * k:P * k + P], ident[0:nc2, 0:nc2])
            for g in range(GB):
                ins = pe.transpose(M[0][:, 384 + NB * H * g:384 + NB * H * (g + 1)], nrows[:, P * g:P * g + P],
                                   ident[0:NB * H, 0:NB * H])
            ins.then_inc(s_colT, 1)
            for n in range(3):
                pe.wait_ge(s_xtok[n], 16 if n == 1 else 32)
            for k in range(KB // 2):
                if k >= 2:
                    pe.wait_ge(s_xT, k - 1)
                for b in range(2):
                    for n, nt in enumerate((P, P, NMETA + TS)):
                        c0 = P * (2 * k + b)
                        ins = pe.transpose(ACC[k % 2][:, b, P * n:P * n + nt], xtok[0:nt, n, c0:c0 + P],
                                           ident[0:nt, 0:nt])
                ins.then_inc(s_xtr, 1)
            pe.wait_ge(s_rd, 3)
            for n, nt in enumerate((P, P, NMETA + TS)):
                ins = product(M[2][:, P * n:P * n + nt], ones[0:nt, :], rdiag[0:nt, n, 0:nt])
            ins.then_inc(s_rm, 1)
            pe.wait_ge(s_xl, KB)
            pe.wait_ge(s_ghl, 4)
            for k in range(KB):
                product(M[3][:, 0:T], gh[:, k, :], xh[:, k, :], start=k == 0, stop=False)
                product(M[3][:, 0:T], gh[:, k, :], xl[:, k, :], start=False, stop=False)
                ins = product(M[3][:, 0:T], gl[:, k, :], xh[:, k, :], start=False, stop=k == KB - 1)
            ins.then_inc(s_gp, 1)
            pe.wait_ge(s_row, 12)
            pe.wait_ge(s_col, 1)
            for n, (k0, nk) in enumerate(KT):
                pe.transpose(M[0][0:nk, n * H:(n + 1) * H], arw[:, k0:k0 + nk], ident[0:H, 0:H])
                pe.transpose(M[0][0:nk, (4 + n) * H:(5 + n) * H], wkr[:, k0:k0 + nk], ident[0:H, 0:H])
            pe.transpose(M[0][0:NB, 8 * H:9 * H], decr[:], ident[0:H, 0:H]).then_inc(s_rowT, 1)

            def unit(base, s, acc, rh, rl, kb, c0, first, last):
                pe.wait_ge(low_done, RING + base + s + 1)
                w, n = s % RING, acc.shape[2]
                for b in range(GB):
                    for k in range(UK):
                        hi, lo = (t[:, w, k, P * b:P * b + P] for t in (wh, wl))
                        mh, ml = (t[:, kb + k, c0:c0 + n] for t in (rh, rl))
                        product(acc[:, b, :], hi, mh, start=first and k == 0, stop=False)
                        product(acc[:, b, :], hi, ml, start=False, stop=False)
                        ins = product(acc[:, b, :], lo, mh, start=False, stop=last and k == UK - 1)
                ins.then_inc(unit_used, 1)

            with pe.Fori(0, H) as h:
                for p in range(UH):
                    g, u = p // 4, p % 4
                    n, c0 = (T, 0) if g < 5 else (TO, T0)
                    if u == 0:
                        pe.wait_ge(evacuated, GH * h + g + 1)
                    if p == 24:
                        pe.wait_ge(s_cst, 1 + 8 * h + 6)
                    unit(UH * h, p, ACC[HEAD_ACC[g]][:, :, 0:n], xh, xl, UK * u, c0, u == 0, u == 3)
                    if p == 1:
                        pe.wait_ge(s_rowh, h + 1)
                        pe.wait_ge(s_cst, 1 + 8 * h)
                        pe.wait_ge(s_rowc, 1)
                        product(ps[:, 4, 0:512], ones[0:H, :], rowh[:, 0:512])
                        product(ps[:, 5, 0:RW - 512], ones[0:H, :], rowh[:, 512:RW]).then_inc(s_bcp, 1)
                    if p == 9:
                        pe.wait_ge(biased, GH * h + 2)
                        pe.wait_ge(s_bc, h + 1)
                        for n, (k0, nk) in enumerate(KT):
                            for d in range(GB):
                                ins = pe.transpose(M[n // 2][0:nk, (n % 2) * DK + P * d:(n % 2) * DK + P * d + P],
                                                   kT[:, d, k0:k0 + nk], ident[:])
                        ins.then_inc(s_ktr, 1)
                        for n, ((k0, nk), (q0, nq, off)) in enumerate(zip(KT, QT)):
                            out = M[2][0:nk, off:off + nq] if n < 2 else M[3][0:nk, off - QT[2][2]:off - QT[2][2] + nq]
                            for d in range(GB):
                                ins = product(out, kT[:, d, k0:k0 + nk], qT[:, d, q0:q0 + nq], d == 0, d == GB - 1)
                        ins.then_inc(s_sc, 1)
                    if p == 13:
                        pe.wait_ge(biased, GH * h + 3)
                        pe.wait_ge(s_kw, h + 1)
                        for n, (k0, nk) in enumerate(KT):
                            for d in range(GB):
                                ins = pe.transpose(M[n // 2][0:nk, (n % 2) * DV + P * d:(n % 2) * DV + P * d + P],
                                                   vT[:, d, k0:k0 + nk], ident[:])
                        ins.then_inc(s_vtr, 1)
                    if p == 15:
                        pe.wait_ge(s_s, 1 + h + 1)
                        pe.wait_ge(s_vt, h + 1)
                        pe.wait_ge(s_qn, h + 1)
                        pe.wait_ge(s_Cin, 32 * h + 32)
                        for e in range(GB + 1):
                            out = M[2 + e] if e < GB else M[0]
                            for n, ((k0, nk), (q0, nq, off)) in enumerate(zip(KT, QT)):
                                w = vt[0:nk, n, P * e:P * e + P] if e < GB else ones[0:nk, :]
                                product(out[:, q0 - T0:q0 - T0 + nq], w, S[0:nk, off:off + nq],
                                        start=n in (0, 3), stop=n == 2)
                            for d in range(GB):
                                if e < GB:
                                    for b in range(NB):
                                        c0 = TP - T0 + DS * b
                                        ins = product(out[:, c0:c0 + DS], Cs[:, b, d, P * e:P * e + P],
                                                      qw[:, d, b, :], start=False, stop=d == GB - 1 and b == NB - 1)
                                else:
                                    ins = product(out[:, TP - T0:TO], ones[:],
                                                  qn[:, d].rearrange("p b t -> p (b t)"),
                                                  start=False, stop=d == GB - 1)
                        ins.then_inc(s_num, 1)
                    if p == 17:
                        pe.wait_ge(s_abs, h + 1)
                        for d in range(GB):
                            for n, (k0, nk) in enumerate(KT[0:3]):
                                product(M[0][:, DV * d:DV * d + DV], kw[0:nk, n, P * d:P * d + P], vt[0:nk, n, :],
                                        n == 0, n == 2)
                        for n, (k0, nk) in enumerate(KT[0:3]):
                            product(M[1][0:1, 0:DK], ones[0:nk, 0:1], kw[0:nk, n, :], n == 0, n == 2)
                        product(M[1][0:NB, DK:2 * DK], onehot[:], kw[0:TS, 3, :]).then_inc(s_cpp, 1)
                    if p in (18, 19, 21, 22):
                        i = (18, 19, 21, 22).index(p)
                        pe.wait_ge(s_kwm, 2 * h + i // 2 + 1)
                        if i == 0:
                            pe.wait_ge(s_h, h + 1)
                        if i == 1:
                            pe.wait_ge(s_cpo, 2 * h + 2)
                            pe.wait_ge(s_nso, h + 1)
                        if i > 1:
                            pe.wait_ge(s_cst, 1 + 8 * h + 2 * i - 2)
                        for b in (2 * i, 2 * i + 1):
                            bank = M[2 + b % 2] if b % 4 < 2 else M[b % 2]
                            for d in range(GB):
                                ins = product(bank[:, DV * d:DV * d + DV], kwm[:, b % 4, P * d:P * d + P],
                                              vt[0:TS, 3, :])
                            ins.then_inc(s_cup, 1)

            nl = clast.shape[0]
            pe.wait_ge(s_cst, 1 + 8 * H)
            pe.wait_ge(s_yb, H)
            for k in range(CW // P):
                ins = pe.transpose(M[k // 4][0:nl, P * (k % 4):P * (k % 4) + P], zlast[:, k, :], ident[:])
            ins.then_inc(s_clt, 1)

            with pe.Fori(0, NMG) as j:
                for g in range(4):
                    pe.wait_ge(evacuated, G_MERGE + 4 * j + g + 1)
                    acc = ACC[g % 2][:, :, 0:TO]
                    if g < 2:
                        for u in range(NU):
                            unit(U_MERGE + 12 * j, 4 * g + u, acc, xh, xl, UK * u, T0, u == 0, u == NU - 1)
                    else:
                        pe.wait_ge(s_hyl, g - 1)
                        rh, rl = ((hah, hal), (ybh, ybl))[g - 2]
                        for u in range(2):
                            unit(U_MERGE + 12 * j, 4 + 2 * g + u, acc, rh, rl, UK * u, 0, u == 0, u == 1)
            with pe.Fori(0, NMG // 2) as jj:
                for pair in range(2):
                    pe.wait_ge(evacuated, G_WO + 2 * jj + pair + 1)
                    for u in range(NU):
                        pe.wait_ge(s_mgl, 1 + 2 * u + 2)
                        unit(U_WO + 8 * jj, 4 * pair + u, ACC[pair][:, :, 0:TO], mgh, mgl, UK * u, 0,
                             u == 0, u == NU - 1)
            pe.wait_ge(s_r2, 1)
            product(M[0][:, 0:TO], ones[:], sqacc[:, 0, :]).then_inc(s_r2p, 1)
            with pe.Fori(0, NCH) as c:
                with pe.Fori(0, NMG // 2) as jj:
                    for pair in range(2):
                        pe.wait_ge(evacuated, G_FF + 2 * NMG * c + 2 * jj + pair + 1)
                        for u in range(NU):
                            pe.wait_ge(s_x1l, 2 * u + 2)
                            unit(U_FF + UCH * c + 8 * jj, 4 * pair + u, ACC[pair][:, :, 0:TO], xh, xl, UK * u, T0,
                                 u == 0, u == NU - 1)
                with pe.Fori(0, NMG // 2) as jj:
                    for pair in range(2):
                        pe.wait_ge(evacuated, G_FF + 2 * NMG * c + NMG + 2 * jj + pair + 1)
                        for u in range(NU):
                            pe.wait_ge(s_ul, 1 + NMG * c + 2 * u + 2)
                            unit(U_FF + UCH * c + 4 * NMG + 8 * jj, 4 * pair + u, ACC[pair][:, :, 0:TO], uh, ul,
                                 UK * u, 0, u == 0, u == NU - 1)
            pe.wait_ge(s_r3, 1)
            for n, (c0, nt) in enumerate(((0, P), (P, P), (2 * P, TS))):
                ins = product(M[0][0:nt, n:n + 1], sqacc[:, 0, c0:c0 + nt], ones[:, 0:1])
            ins.then_inc(s_r3p, 1)
            pe.wait_ge(evacuated, 2 + G_FF + 2 * NMG * NCH)
            for i, (n, q) in enumerate((n, q) for n in range(3) for q in range(KB // 4)):
                nt = P if n < 2 else TS
                if i >= 6:
                    pe.wait_ge(s_y, i - 5)
                for k in range(4):
                    ins = pe.transpose(ps[0:nt, YBANK[i % 6], P * k:P * k + P],
                                       xT[:, 4 * q + k, T0 + P * n:T0 + P * n + nt], ident[:])
                ins.then_inc(s_yt, 1)


_INS = ["x_prompt", "x_sample", "state_mlstm_C", "state_mlstm_n", "state_mlstm_m", "state_conv", "meta_tokens",
        "g_mix", "w_in", "b_in", "w_conv", "p_a", "p_b", "w_o", "g_ffn", "w_up", "w_down", "g_final"]


def kernel(**inputs):
    import numpy as np
    import concourse.bacc as bacc
    from concourse.bass_utils import run_bass_kernel_spmd

    nc = bacc.Bacc("TRN2", target_bir_lowering=False, num_devices=1)
    arrays, args = {}, []
    for name in _INS:
        a = np.ascontiguousarray(inputs[name])
        arrays[f"in_{name}_dram"] = a
        args.append(nc.dram_tensor(f"in_{name}_dram", a.shape, mybir.dt.from_np(a.dtype), kind="ExternalInput").ap())
    L, NB, H, DK, DV = inputs["state_mlstm_C"].shape
    taps, cw = inputs["state_conv"].shape[2:]
    shapes = [inputs["x_prompt"].shape, inputs["x_sample"].shape,
              (L, 1, H, DK, DV), (L, 1, H, DK), (L, 1, H), (L, 1, taps, cw),
              (L, NB, H, DK, DV), (L, NB, H, DK), (L, NB, H), (L, NB, taps, cw)]
    for i, shape in enumerate(shapes):
        args.append(nc.dram_tensor(f"out_{i}_dram", tuple(shape), F32, kind="ExternalOutput").ap())
    build(nc, *args)
    r = run_bass_kernel_spmd(nc, [arrays], core_ids=[0])
    return tuple(r.results[0][f"out_{i}_dram"] for i in range(len(shapes)))
```

```python
from contextlib import ExitStack

import concourse.bass as bass
from concourse import mybir

F32 = mybir.dt.float32
F32R = mybir.dt.float32r
ALU = mybir.AluOpType
ACT = mybir.ActivationFunctionType
P = 128
ds = bass.ds

EPS = 1e-6
GAP = 64
BIG = 1e30
FAR = 3e38
RING = 4
LEAD = 3
UK = 4
GC = 256
GB = GC // P


def build(nc, x_prompt, x_sample, state_C, state_n, state_m, state_conv, meta, g_mix, w_in, b_in,
          w_conv, p_a, p_b, w_o, g_ffn, w_up, w_down, g_final,
          y_prompt, y_sample, C_prompt, n_prompt, m_prompt, conv_prompt,
          C_sample, n_sample, m_sample, conv_sample):
    _, SEQ, D = x_prompt.shape
    NB, DS, _ = x_sample.shape
    _, _, H, DK, DV = state_C.shape
    NMETA = meta.shape[0]
    CW = w_conv.shape[2]
    TAPS = w_conv.shape[1]
    FF = w_up.shape[2]
    T0 = NMETA
    TP = NMETA + SEQ
    TS = NB * DS
    T = TP + TS
    TO = T - T0
    KB = D // P
    assert DK == GC and DV == GC and H * DV == CW == H * GC and D % (P * UK) == 0
    assert T <= 512 and TP % P == NMETA and TS <= P and TAPS == 3
    MW = H * DV
    CQ, CK, CV, CG = 0, H * DK, 2 * H * DK, 2 * H * DK + MW
    CO = CG + 2 * H
    CU, CC, CB = CO + MW, CO + MW + CW, CO + MW + 2 * CW
    CGA, CGB = CO + MW + 3 * CW, CO + MW + 3 * CW + D
    NB1, NB2 = CG // P, (CGB + D - CO) // P
    BQ, BK, BV = 0, CK // P, CV // P
    BO = NB1
    BU, BC_, BB = BO + MW // P, BO + (CU + CW - CO) // P, BO + (CB - CO) // P
    BGA, BGB = BO + (CGA - CO) // P, BO + (CGB - CO) // P
    KT = [(0, P), (P, P), (2 * P, NMETA), (TP, TS)]
    QT = [(T0, TP - T0, 0), (P, TP - P, TP - T0), (2 * P, TP - 2 * P, 2 * TP - T0 - P),
          (TP, TS, 3 * TP - T0 - 3 * P)]
    SW = QT[3][2] + TS
    RW = T + TO + TS
    REM, RWI = T, T + TO

    NU = D // (P * UK)
    NMG = D // GC
    NCH = FF // D
    assert NU == RING and NU % 2 == 0
    UCV, UH = 2 * NU, 6 * NU
    U_HEAD = UCV * H
    U_MERGE = U_HEAD + UH * H
    U_WO = U_MERGE + 3 * NU * NMG
    U_FF = U_WO + NU * NMG
    UCH = 2 * NU * NMG
    GH = 5
    G_HEAD = 2 * H
    G_MERGE = G_HEAD + GH * H
    G_WO = G_MERGE + 4 * NMG
    G_FF = G_WO + NMG

    with ExitStack() as ctx:
        def sem(name):
            return ctx.enter_context(nc.semaphore(name))

        def tile(stack, name, shape, dt=F32):
            return stack.enter_context(nc.sbuf_tensor(name, shape, dt))

        raw = tile(ctx, "raw", [P, RING, UK, GC])
        wh = tile(ctx, "w_high", [P, RING, UK, GC], F32R)
        wl = tile(ctx, "w_low", [P, RING, UK, GC], F32R)
        xT = tile(ctx, "x_T", [P, KB, T])
        xh = tile(ctx, "x_high", [P, KB, T], F32R)
        xl = tile(ctx, "x_low", [P, KB, T], F32R)
        ident = tile(ctx, "ident", [P, P])
        ones = tile(ctx, "ones", [P, P])
        rbc = tile(ctx, "r_bc", [P, T])
        biasT = tile(ctx, "bias_T", [P, NB1 + NB2])
        vecT = tile(ctx, "vec_T", [P, 3 * KB + TAPS * CW // P])
        VG, VF, VL, VC = 0, KB, 2 * KB, 3 * KB
        tmp = tile(ctx, "tmp", [P, GB, T])
        ssum = tile(ctx, "sum_sq_cols", [P, 3])
        rcol = tile(ctx, "r_cols", [P, 3])
        rtmp = tile(ctx, "r_tmp", [P, 3])
        zlast = tile(ctx, "z_last", [P, CW // P, (TAPS - 1) * (1 + NB)])
        sqacc = tile(ctx, "sq_acc", [P, GB, TO])

        heads = ExitStack()
        yb = tile(heads, "y_b", [P, CW // P, TO])
        mask = tile(heads, "mask", [P, TP])
        smask = tile(heads, "sample_mask", [TS, NB, DS])
        onehot = tile(heads, "onehot", [2 * TS, NB])
        fold = tile(heads, "fold", [2 * TS, TS])
        acol = tile(heads, "a_cols", [P, 4, H])
        wkcol = tile(heads, "wk_cols", [P, 4, H])
        deccol = tile(heads, "decay_cols", [NB, H])
        stT = tile(heads, "conv_state_T", [P, CW // P, NB, TAPS - 1])
        nT = tile(heads, "n_T", [P, GB, NB, H])
        rows = tile(heads, "rows", [H, RW])
        mrw = tile(heads, "m_row", [H, T])
        with ExitStack() as st:
            xtok = tile(st, "x_tok", [P, 3, D])
            gw = tile(st, "gate_w", [P, KB, 32])
            gh = tile(st, "gate_w_high", [P, KB, P], F32R)
            gl = tile(st, "gate_w_low", [P, KB, P], F32R)
            keep = tile(st, "keep_row", [H, T])
            fall = tile(st, "reset_row", [H, T])
            igr = tile(st, "ig_row", [H, T])
            fgr = tile(st, "fg_row", [H, T])
            seqs = tile(st, "sequence_of", [2 * TS, 2, NB])
            e1r = tile(st, "e1_row", [H, T])
            brw = tile(st, "b_row", [H, T])
            arw = tile(st, "a_row", [H, T])
            a1r = tile(st, "a1_row", [H, T])
            wkr = tile(st, "wk_row", [H, T + TS])
            wir = tile(st, "wint_row", [H, NB, DS])
            decr = tile(st, "decay_row", [H, NB])
            bi = tile(st, "ig_bias", [H, 1])
            bf = tile(st, "fg_bias", [H, 1])
            m0 = tile(st, "m0_row", [H, NB])
            brows = tile(st, "bias_rows", [NB1 + NB2, P])
            vrows = tile(st, "vec_rows", [3 * KB + TAPS * CW // P, P])
            crows = tile(st, "conv_rows", [NB * (TAPS - 1), CW])
            nrows = tile(st, "n_rows", [NB * H, DK])
            rdiag = tile(st, "r_diag", [P, 3, P])
        with ExitStack() as st:
            zu = tile(st, "zu", [P, GB, T])
            zp = tile(st, "z_prompt", [P, GB, TP])
            zs = tile(st, "z_sample", [P, GB, NB, DS + TAPS - 1])
        QS = P + DS
        with ExitStack() as st:
            kwm = tile(st, "kw_masked", [2 * TS, NB // 2, DK], F32R)
            kw = tile(st, "kw_tok", [P, 3, DK])
            kws = tile(st, "kw_sample", [2 * TS, DK], F32R)
            vt = tile(st, "v_tok", [P, 4, DV])
            vsh = tile(st, "v_sample_high", [2 * TS, DV], F32R)
            vsl = tile(st, "v_sample_low", [TS, DV], F32R)
            E = tile(st, "key_weights", [P, SW])
            bc = tile(st, "rows_bc", [P, RW])
            den = tile(st, "den", [P, TO])
            qw = tile(st, "q_inter", [P, GB, NB, DS])
            qn = tile(st, "q_n", [P, GB, NB, DS])
            qm = tile(st, "q_masked", [P, GB, NB * QS], F32R)
            cq = tile(st, "C_q", [P, DV])
            qT = tile(st, "q_T", [P, GB, T])
            kT = tile(st, "k_T", [P, GB, T + TS])
            hT = tile(st, "h_T", [P, GB, TO])
            cpo = tile(st, "C_prompt_out", [P, GB, DV])
            npo = tile(st, "n_prompt_out", [1, DK])
            nin = tile(st, "n_in", [NB, DK])
            nso = tile(st, "n_sample_out", [NB, DK])
            tile(st, "gap", [P, GAP])
            Cs = tile(st, "C_state", [P, NB, GB, DV])
            ha = tile(st, "h_a", [P, MW // P, TO])
        rowh = vt[0:H].rearrange("p n e -> p (n e)")[:, 0:RW]
        heads.close()
        with ExitStack() as st:
            mgh = tile(st, "merged_high", [P, KB, TO], F32R)
            hah = tile(st, "h_a_high", [P, MW // P, TO], F32R)
            hal = tile(st, "h_a_low", [P, MW // P, TO], F32R)
            ybh = tile(st, "y_b_high", [P, CW // P, TO], F32R)
            ybl = tile(st, "y_b_low", [P, CW // P, TO], F32R)
            mgl = tile(st, "merged_low", [P, KB, TO], F32R)
            clast = tile(st, "conv_last", [(TAPS - 1) * (1 + NB), CW])
        sga, sgb = tmp[:, :, 0:TO], sqacc[:]
        with ExitStack() as st:
            uh = tile(st, "u_high", [P, KB, TO], F32R)
            ul = tile(st, "u_low", [P, KB, TO], F32R)
            yo = tile(st, "y_out", [P, 3, D])
            gfb = tile(st, "g_final_bc", [P, D])
            ur = tile(st, "u_relu", [P, GB, TO])
            uq = tile(st, "u_squared", [P, GB, TO])

        ps = ctx.enter_context(nc.psum_tensor("ps", [P, 8, 512], F32))
        ACC = [ps[:, 0:2, :], ps[:, 2:4, :], ps[:, 6:8, :]]
        M = [ps[:, 4 + n, :] for n in range(4)]
        HEAD_ACC = [0, 1, 0, 1, 2]
        YBANK = [0, 1, 2, 3, 5, 6]

        landed = [sem(f"raw_landed{s}") for s in range(RING)]
        high_done = sem("high_done")
        low_done = sem("low_done")
        unit_used = sem("unit_used")
        evacuated = sem("evacuated")
        biased = sem("biased")
        s_const = sem("const_built")
        s_vrows = sem("vec_rows_in")
        s_brows = sem("bias_rows_in")
        s_xtok = [sem(f"x_tok_in{n}") for n in range(3)]
        s_gw = sem("gate_w_in")
        s_small = sem("small_in")
        s_colT = sem("cols_transposed")
        s_col = sem("cols_ready")
        s_xtr = sem("x_transposed")
        s_xT = sem("x_T_ready")
        s_xh = sem("x_high_ready")
        s_xl = sem("x_low_ready")
        s_sq = sem("sum_sq_ready")
        s_ms = sem("mean_sq_ready")
        s_rt = sem("root_ready")
        s_rc = sem("r_col_ready")
        s_rd = sem("r_diag_ready")
        s_rm = sem("r_bc_product")
        s_r = sem("r_bc_ready")
        s_gz = sem("gate_w_zeroed")
        s_ghl = sem("gate_w_split")
        s_gp = sem("gate_product")
        s_row = sem("row_step")
        s_rowa = sem("row_step_act")
        s_rowT = sem("rows_transposed")
        s_rowc = sem("row_cols_ready")
        s_rowh = sem("rows_head_ready")
        s_bcp = sem("rows_bc_product")
        s_bc = sem("rows_bc_ready")
        s_x = sem("exponent_ready")
        s_e = sem("key_weights_ready")
        s_qw = sem("q_inter_ready")
        s_qn = sem("q_n_ready")
        s_ktr = sem("k_transposed")
        s_kw = sem("kw_ready")
        s_kwm = sem("kw_masked_ready")
        s_sc = sem("score_product")
        s_s = sem("scores_ready")
        s_vtr = sem("v_transposed")
        s_vt = sem("v_tok_ready")
        s_num = sem("num_den_product")
        s_abs = sem("abs_den_ready")
        s_den = sem("den_steps")
        s_h = sem("h_ready")
        s_cpp = sem("C_prompt_product")
        s_cpo = sem("C_prompt_ready")
        s_nso = sem("n_sample_ready")
        s_cup = sem("C_update_product")
        s_cst = sem("C_state_new")
        s_Cin = sem("C_state_in")
        s_nin = sem("n_in")
        s_out = sem("small_states_stored")
        s_outC = sem("C_sample_stored")
        s_zu = sem("zu_ready")
        s_zc = sem("zc_ready")
        s_z = sem("z_ready")
        s_qmh = sem("q_masked_high")
        s_qml = sem("q_masked_low")
        s_qmz = sem("q_masked_zeroed")
        s_fold = sem("fold_ready")
        s_kwl = sem("kw_low_ready")
        s_vsl = sem("v_low_ready")
        s_cqp = sem("C_q_product")
        s_cq = sem("C_q_ready")
        s_set = sem("columns_set")
        s_cv = sem("conv_step")
        s_yb = sem("y_b_ready")
        s_ha = sem("h_a_ready")
        s_hyh = sem("h_y_high")
        s_hyl = sem("h_y_low")
        s_clt = sem("conv_last_transposed")
        s_clo = sem("conv_last_ready")
        s_mout = sem("m_stored")
        s_cout = sem("conv_stored")
        s_sga = sem("gate_a_ready")
        s_sgb = sem("gate_b_ready")
        s_mgs = sem("merged_step")
        s_mgh = sem("merged_high_ready")
        s_mgl = sem("merged_low_ready")
        s_x1 = sem("x1_ready")
        s_x1h = sem("x1_high_ready")
        s_x1q = sem("x1_sq_ready")
        s_x1l = sem("x1_low_ready")
        s_acc = sem("sq_acc_step")
        s_r2p = sem("r2_product")
        s_r2 = sem("r2_step")
        s_r2a = sem("r2_root")
        s_uq = sem("u_sq_ready")
        s_uh = sem("u_high_ready")
        s_ul = sem("u_low_ready")
        s_x2 = sem("x2_ready")
        s_x2q = sem("x2_sq_ready")
        s_ac2 = sem("sq_acc2_step")
        s_r3p = sem("r3_product")
        s_r3 = sem("r3_step")
        s_r3a = sem("r3_root")
        s_yt = sem("y_transposed")
        s_y = sem("y_ready")
        s_yout = sem("y_stored")
        s_gfb = sem("g_final_in")

        def cut(w):
            return w[0].rearrange("(u k p) n -> p u k n", k=UK, p=P)

        win, wpa, wpb, wwo, wup, wdn = (cut(w) for w in (w_in, p_a, p_b, w_o, w_up, w_down))

        block = ctx.enter_context(nc.Block())

        def q_blocks(col):
            return qm[:].rearrange("p g (b c) -> p g b c", c=QS)[:, :, :, col:col + DS]

        @block.sync
        def _(sp):
            sp.dma_start(xtok[0:NMETA, 0, :], meta).then_inc(s_xtok[0], 16)
            sp.dma_start(xtok[NMETA:P, 0, :], x_prompt[0, 0:P - NMETA, :]).then_inc(s_xtok[0], 16)
            sp.dma_start(xtok[:, 1, :], x_prompt[0, P - NMETA:2 * P - NMETA, :]).then_inc(s_xtok[1], 16)
            sp.dma_start(xtok[0:NMETA, 2, :], x_prompt[0, SEQ - NMETA:SEQ, :]).then_inc(s_xtok[2], 16)
            sp.dma_start(xtok[NMETA:NMETA + TS, 2, :],
                         x_sample.rearrange("b t d -> (b t) d")).then_inc(s_xtok[2], 16)
            sp.dma_start(gw[:], w_in[0, :, CG:CG + 32].rearrange("(k p) n -> p k n", p=P)).then_inc(s_gw, 16)

            def stream(base, s, w, part, col):
                sp.wait_ge(low_done, base + s + 1)
                sp.dma_start(raw[:, s % RING:s % RING + 1], w[:, ds(part, 1), :, ds(col, GC)]) \
                  .then_inc(landed[s % RING], 16)

            with sp.Fori(0, H) as i:
                for g, col in enumerate((CU, CC)):
                    for u in range(NU):
                        stream(UCV * i, NU * g + u, win, u, col + GC * i)
            with sp.Fori(0, H) as h:
                def head_group(g, col):
                    for u in range(NU):
                        stream(U_HEAD + UH * h, NU * g + u, win, u, col + GC * h)

                for g, col in enumerate((CQ, CK, CV)):
                    head_group(g, col)
                for u in range(NU):
                    b0, d = NB // 2 * (u // GB), u % GB
                    sp.wait_ge(low_done, U_HEAD + UH * h + 3 * NU + u + 1)
                    sp.dma_start(raw[:, u], state_C[0, b0:b0 + NB // 2, ds(h, 1), P * d:P * d + P, :]
                                 .rearrange("b o p e -> p (b o) e")).then_inc(landed[u], 16)
                sp.wait_ge(s_rowc, 1)
                sp.wait_ge(s_outC, 16 + 32 * h)
                for d in range(GB):
                    sp.dma_start(Cs[:, :, d, :], state_C[0, :, ds(h, 1), P * d:P * d + P, :]
                                 .rearrange("b o p e -> p (b o) e")).then_inc(s_Cin, 16)
                sp.wait_ge(s_nso, 1 + h)
                sp.dma_start(nin[:], state_n[0, :, ds(h, 1), :].rearrange("b o d -> b (o d)")) \
                    .then_inc(s_nin, 16)
                for g, col in ((4, CB), (5, CO)):
                    head_group(g, col)
            with sp.Fori(1, NMG + 1) as j1:
                first = U_MERGE - 3 * NU + 3 * NU * j1
                for g, col in enumerate((CGA, CGB)):
                    for u in range(NU):
                        stream(first, 4 * g + u, win, u, GC * j1 + (col - GC))
                for g, w in enumerate((wpa, wpb)):
                    for u in range(MW // (P * UK)):
                        stream(first, 8 + 2 * g + u, w, u, GC * j1 + (-GC))
            with sp.Fori(0, NMG) as j:
                for u in range(NU):
                    stream(U_WO + 4 * j, u, wwo, u, GC * j)
            with sp.Fori(0, NCH) as c:
                with sp.Fori(0, NMG) as j:
                    for u in range(NU):
                        stream(U_FF + UCH * c + 4 * j, u, wup, u, D * c + GC * j)
                with sp.Fori(0, NMG) as j:
                    for u in range(NU):
                        stream(U_FF + UCH * c + 4 * NMG + 4 * j, u, wdn, NU * c + u, GC * j)
            for n, (t0, nt) in enumerate(((0, P), (P, P))):
                sp.wait_ge(s_y, 4 * n + 4)
                sp.dma_start(y_prompt[0, t0:t0 + nt, :], yo[:, n, :]).then_inc(s_yout, 16)
            sp.wait_ge(s_y, 12)
            sp.dma_start(y_sample.rearrange("b t d -> (b t) d"), yo[0:TS, 2, :]).then_inc(s_yout, 16)
            sp.wait_ge(s_yout, 48)
            sp.wait_ge(s_out, 16 + 48 * H)
            sp.wait_ge(s_outC, 16 + 32 * H)
            sp.wait_ge(s_mout, 32)
            sp.wait_ge(s_cout, 32)

        @block.gpsimd
        def _(pool):
            g = nc.gpsimd
            def const(ins):
                ins.then_inc(s_const, 1)

            const(g.memset(ident[:], 0.0))
            pool.wait_ge(s_const, 1)
            const(g.affine_select(out=ident[:], in_=ident[:], compare_op=ALU.not_equal, fill=1.0, base=0,
                                  pattern=[[1, P]], channel_multiplier=-1))
            g.memset(gh[:].bitcast(F32), 0.0)
            g.memset(gl[:].bitcast(F32), 0.0).then_inc(s_gz, 1)
            const(g.memset(ones[:], 1.0))
            const(g.memset(mask[:], 0.0))
            const(g.memset(smask[:], 0.0))
            const(g.memset(seqs[:], 1.0))
            const(g.memset(keep[:], 1.0))
            const(g.memset(fall[:], 0.0))
            pool.wait_ge(s_const, 8)
            const(g.affine_select(out=mask[:], in_=mask[:], compare_op=ALU.is_ge, fill=BIG, base=0,
                                  pattern=[[1, TP]], channel_multiplier=-1))
            const(g.affine_select(out=smask[:], in_=smask[:], compare_op=ALU.is_ge, fill=BIG, base=0,
                                  pattern=[[DS, NB], [1, DS]], channel_multiplier=-1))
            const(g.affine_select(out=seqs[:], in_=seqs[:], compare_op=ALU.is_ge, fill=0.0, base=0,
                                  pattern=[[-TS, 2], [-DS, NB]], channel_multiplier=1))
            const(g.memset(keep[:, 0:1], 0.0))
            const(g.memset(keep[:, TP:T:DS], 0.0))
            const(g.memset(fall[:, 0:1], -FAR))
            const(g.memset(fall[:, TP:T:DS], -FAR))
            pool.wait_ge(s_const, 15)
            const(g.affine_select(out=smask[:], in_=smask[:], compare_op=ALU.is_ge, fill=BIG, base=0,
                                  pattern=[[-DS, NB], [0, DS]], channel_multiplier=1))
            const(g.affine_select(out=seqs[:], in_=seqs[:], compare_op=ALU.is_ge, fill=0.0, base=DS - 1,
                                  pattern=[[TS, 2], [DS, NB]], channel_multiplier=-1))
            const(g.tensor_tensor(fold[:], ident[:, 0:TS], ident[:, TS:2 * TS], ALU.add))
            pool.wait_ge(s_const, 17)
            const(g.tensor_tensor(onehot[:], seqs[:, 0], seqs[:, 1], ALU.add))
            pool.wait_ge(s_row, 9)
            with nc.allow_non_contiguous_dma(reason="36 stabilisers"):
                pool.dma_start(m_prompt.rearrange("l b h -> h (l b)"), mrw[:, TP - 1:TP]).then_inc(s_mout, 16)
                pool.dma_start(m_sample.rearrange("l b h -> h (l b)"), mrw[:, TP + DS - 1:T:DS]) \
                    .then_inc(s_mout, 16)
            pool.wait_ge(s_rowc, 1)
            g.memset(qm[:].bitcast(F32), 0.0).then_inc(s_qmz, 1)
            with pool.Fori(0, H) as h:
                for half in range(2):
                    if half == 0:
                        pool.wait_ge(s_kwl, h + 1)
                    pool.wait_ge(s_cup, 1 + 8 * h + 4 * half)
                    k3 = kws[:].bitcast(F32).unsqueeze(1).to_broadcast([2 * TS, NB // 2, DK])
                    oh = onehot[:, 4 * half:4 * half + 4].unsqueeze(2).to_broadcast([2 * TS, NB // 2, DK])
                    g.tensor_tensor(kwm[:], k3, oh, ALU.mult).then_inc(s_kwm, 1)
            pool.wait_ge(s_clo, 1)
            pool.dma_start(conv_prompt[0, 0], clast[0:TAPS - 1, :]).then_inc(s_cout, 16)
            pool.dma_start(conv_sample[0].rearrange("b r c -> (b r) c"),
                           clast[TAPS - 1:, :]).then_inc(s_cout, 16)
            pool.wait_ge(evacuated, 2 + G_FF)
            pool.dma_start(gfb[:], g_final.partition_broadcast(P)).then_inc(s_gfb, 16)

        @block.scalar
        def _(act):
            a = nc.scalar
            act.sem_inc(s_mgh, 1)
            act.sem_inc(s_uh, 1)
            act.sem_inc(s_out, 16)
            act.sem_inc(s_outC, 16)
            act.dma_start(vrows[0:KB, :], g_mix.rearrange("l (k p) -> (l k) p", p=P)).then_inc(s_vrows, 16)
            act.dma_start(vrows[KB:2 * KB, :], g_ffn.rearrange("l (k p) -> (l k) p", p=P)).then_inc(s_vrows, 16)
            act.dma_start(vrows[2 * KB:3 * KB, :], g_final.rearrange("(k p) -> k p", p=P)).then_inc(s_vrows, 16)
            act.dma_start(vrows[3 * KB:, :], w_conv.rearrange("l r (k p) -> (l r k) p", p=P)).then_inc(s_vrows, 16)
            act.dma_start(brows[0:NB1, :], b_in[0, 0:CG].rearrange("(k p) -> k p", p=P)).then_inc(s_brows, 16)
            act.dma_start(brows[NB1:, :], b_in[0, CO:].rearrange("(k p) -> k p", p=P)).then_inc(s_brows, 16)
            act.dma_start(crows[:], state_conv[0].rearrange("b r c -> (b r) c")).then_inc(s_brows, 16)
            act.dma_start(nrows[:], state_n[0].rearrange("b h d -> (b h) d")).then_inc(s_brows, 16)
            with nc.allow_non_contiguous_dma(reason="40 numbers"):
                act.dma_start(bi[:], b_in[0, CG:CG + H].rearrange("(h o) -> h o", o=1)).then_inc(s_small, 16)
                act.dma_start(bf[:], b_in[0, CG + H:CO].rearrange("(h o) -> h o", o=1)).then_inc(s_small, 16)
                act.dma_start(m0[:], state_m[0].rearrange("b h -> h b")).then_inc(s_small, 16)

            def split(base, s):
                act.wait_ge(landed[s % RING], 4 * base + 16 * (s // RING) + 16)
                act.wait_ge(unit_used, base + s + 1)
                a.activation(wh[:, s % RING], raw[:, s % RING], ACT.Copy).then_inc(high_done, 1)

            act.wait_ge(s_set, 1)
            for n, nt in enumerate((P, P, NMETA + TS)):
                act.wait_ge(s_xtok[n], 16 if n == 1 else 32)
                if n > 0:
                    act.wait_ge(s_sq, n)
                a.activation(wh[0:nt, 0:2].rearrange("p s k n -> p (s k n)"), xtok[0:nt, n, :], ACT.Square,
                             accum_out=ssum[0:nt, n:n + 1]).then_inc(s_sq, 1)
            act.wait_ge(s_ms, 1)
            a.activation(rcol[:], ssum[:], ACT.Sqrt).then_inc(s_rt, 1)
            act.wait_ge(s_gw, 16)
            act.wait_ge(s_gz, 1)
            a.activation(gh[:, :, 0:H], gw[:, :, 0:H], ACT.Copy).then_inc(s_ghl, 1)
            a.activation(gh[:, :, 32:32 + H], gw[:, :, H:2 * H], ACT.Copy).then_inc(s_ghl, 1)
            act.wait_ge(s_col, 1)
            for k in range(KB):
                act.wait_ge(s_xT, k // 2 + 1)
                a.activation(xh[:, k, :], xT[:, k, :], ACT.Copy, scale=vecT[:, VG + k:VG + k + 1]).then_inc(s_xh, 1)
                if k >= KB // 2 and k % 2 == 1 and k // 2 - KB // 4 < LEAD:
                    split(0, k // 2 - KB // 4)

            def convolution(i, extra=()):
                for p in range(UCV):
                    split(UCV * i, p + LEAD)
                    if p in extra:
                        extra[p]()
                    if p == 3:
                        act.wait_ge(evacuated, 2 + 2 * i + 1)
                        for b in range(GB):
                            ins = a.activation(zu[:, b, :], tmp[:, b, :], ACT.Identity,
                                               bias=biasT[:, ds(BU + GB * i + b, 1)])
                        ins.then_inc(s_zu, 1)
                    if p == 7:
                        act.wait_ge(evacuated, 2 + 2 * i + 2)
                        for b in range(GB):
                            ins = a.activation(tmp[:, b, :], tmp[:, b, :], ACT.Identity,
                                               bias=biasT[:, ds(BC_ + GB * i + b, 1)])
                        ins.then_inc(s_zc, 1)

            def log1p_exp():
                act.wait_ge(s_row, 2)
                a.activation(e1r[:], fgr[:], ACT.Abs).then_inc(s_rowa, 1)
                act.wait_ge(s_rowa, 1)
                a.activation(e1r[:], e1r[:], ACT.Exp, scale=-1.0).then_inc(s_rowa, 1)
                act.wait_ge(s_rowa, 2)
                a.activation(e1r[:], e1r[:], ACT.Ln, bias=1.0).then_inc(s_rowa, 1)

            def row_exps():
                act.wait_ge(s_row, 11)
                a.activation(rows[:, REM:REM + TO], mrw[:, T0:T], ACT.Exp, scale=-1.0).then_inc(s_rowa, 1)
                a.activation(rows[:, RWI:RWI + TS].rearrange("p (b t) -> p b t", t=DS), wir[:],
                             ACT.Exp).then_inc(s_rowa, 1)
                a.activation(wkr[:], wkr[:], ACT.Exp).then_inc(s_rowa, 1)

            with act.Fori(0, H - 1) as i:
                convolution(i)
            convolution(H - 1, {1: log1p_exp, 5: row_exps})

            with act.Fori(0, H) as h:
                def add_bias(g, out, col, func=ACT.Identity):
                    act.wait_ge(evacuated, 2 + G_HEAD + GH * h + g + 1)
                    n = min(out.shape[2], T)
                    for b in range(GB):
                        ins = a.activation(out[:, b, 0:n], tmp[:, b, 0:n], func,
                                           bias=biasT[:, ds(col + GB * h + b, 1)])
                        if out.shape[2] > T:
                            ins = a.activation(out[:, b, T:], tmp[:, b, TP:T], func,
                                               bias=biasT[:, ds(col + GB * h + b, 1)])
                    ins.then_inc(biased, 1)

                for p in range(UH):
                    split(U_HEAD + UH * h, p + LEAD)
                    if p == 1:
                        act.wait_ge(s_bcp, 1 + h + 1)
                        act.wait_ge(s_cst, 1 + 8 * h)
                        act.wait_ge(s_den, 1 + 2 * h)
                        a.activation(bc[:], ps[:, 4:6, :].rearrange("p b n -> p (b n)")[:, 0:RW],
                                     ACT.Copy).then_inc(s_bc, 1)
                    if p == 3:
                        add_bias(0, qT, BQ)
                    if p == 5:
                        act.wait_ge(s_x, h + 1)
                        for n, ((k0, nk), (q0, nq, off)) in enumerate(zip(KT, QT)):
                            ins = a.activation(E[0:nk, off:off + nq], E[0:nk, off:off + nq], ACT.Exp, scale=-1.0,
                                               bias=acol[0:nk, n, ds(h, 1)])
                        ins.then_inc(s_e, 1)
                        act.wait_ge(s_qw, h + 1)
                        act.wait_ge(s_qmz, 1)
                        act.wait_ge(s_cqp, 1 + h)
                        a.activation(q_blocks(0), qw[:], ACT.Copy).then_inc(s_qmh, 1)
                    if p == 7:
                        add_bias(1, kT, BK)
                    if p == 9:
                        act.wait_ge(s_ktr, h + 1)
                        act.wait_ge(s_cup, 1 + 8 * h)
                        for n, (k0, nk) in enumerate(KT[0:3]):
                            a.activation(kw[0:nk, n, :], M[n // 2][0:nk, (n % 2) * DK:(n % 2 + 1) * DK],
                                         ACT.Copy, scale=wkcol[0:nk, n, ds(h, 1)])
                        a.activation(kws[:], M[1][:, DK:2 * DK], ACT.Copy,
                                     scale=wkcol[:, 3, ds(h, 1)]).then_inc(s_kw, 1)
                    if p == 11:
                        act.wait_ge(s_sc, h + 1)
                        add_bias(2, kT, BV)
                    if p == 12:
                        act.wait_ge(s_vtr, h + 1)
                        for n, (k0, nk) in enumerate(KT):
                            a.activation(vt[0:nk, n, :], M[n // 2][0:nk, (n % 2) * DV:(n % 2 + 1) * DV], ACT.Copy)
                        a.activation(vsh[:], M[1][:, DV:2 * DV], ACT.Copy).then_inc(s_vt, 1)
                    if p == 15:
                        act.wait_ge(s_cqp, 1 + h + 1)
                        act.wait_ge(s_num, 1 + h)
                        a.activation(cq[:], M[2][:, 0:DV], ACT.Copy).then_inc(s_cq, 1)
                    if p == 16:
                        act.wait_ge(s_num, 1 + h + 1)
                        a.activation(den[:], M[3][:, 0:TO], ACT.Abs).then_inc(s_abs, 1)
                    if p == 18:
                        act.wait_ge(s_cpp, h + 1)
                        act.wait_ge(s_out, 16 + 48 * h)
                        a.activation(cpo[:].rearrange("p g e -> p (g e)"), M[2], ACT.Copy).then_inc(s_cpo, 1)
                        a.activation(npo[:], M[3][0:1, 0:DK], ACT.Copy).then_inc(s_cpo, 1)
                    if p == 19:
                        add_bias(3, tmp[:, :, 0:TO], BB)
                    if p == 20:
                        act.wait_ge(s_cpo, 2 * h + 2)
                        act.dma_start(C_prompt[0, :, ds(h, 1), :, :]
                                      .rearrange("b o (g p) e -> p (b o g) e", p=P), cpo[:]).then_inc(s_out, 16)
                        act.dma_start(n_prompt[0, :, ds(h, 1), :].rearrange("b o d -> b (o d)"), npo[:]) \
                            .then_inc(s_out, 16)
                        act.wait_ge(s_nso, 1 + h + 1)
                        act.dma_start(n_sample[0, :, ds(h, 1), :].rearrange("b o d -> b (o d)"), nso[:]) \
                            .then_inc(s_out, 16)
                    if p == 23:
                        act.wait_ge(s_cst, 1 + 8 * h + 8)
                        for d in range(GB):
                            act.dma_start(C_sample[0, :, ds(h, 1), P * d:P * d + P, :]
                                          .rearrange("b o p e -> p (b o) e"), Cs[:, :, d, :]).then_inc(s_outC, 16)
                        add_bias(4, tmp[:, :, 0:TO], BO, ACT.Sigmoid)

            act.wait_ge(s_ha, 1 + H)
            act.wait_ge(s_out, 16 + 48 * H)
            act.wait_ge(s_cst, 1 + 8 * H)
            act.wait_ge(s_mout, 32)
            a.activation(hah[:], ha[:], ACT.Copy).then_inc(s_hyh, 1)
            act.wait_ge(s_yb, 1 + H)
            a.activation(ybh[:], yb[:], ACT.Copy).then_inc(s_hyh, 1)

            act.wait_ge(s_clt, 1)
            act.wait_ge(s_hyl, 2)
            a.activation(clast[:], ps[0:clast.shape[0], 4:6, :].rearrange("p b n -> p (b n)"), ACT.Copy) \
                .then_inc(s_clo, 1)

            with act.Fori(0, NMG) as j:
                for p in range(12):
                    split(U_MERGE + 3 * NU * j, p + LEAD)
                    for pos, g, gate, done, col in ((3, 0, sga, s_sga, BGA), (7, 1, sgb, s_sgb, BGB)):
                        if p == pos:
                            act.wait_ge(evacuated, 2 + G_MERGE + 4 * j + g + 1)
                            for b in range(GB):
                                ins = a.activation(gate[:, b, :], gate[:, b, :], ACT.Sigmoid,
                                                   bias=biasT[:, ds(col + GB * j + b, 1)])
                            ins.then_inc(done, 1)
                    if p == 11:
                        act.wait_ge(s_mgs, 1 + 2 * j + 2)
                        act.wait_ge(s_outC, 16 + 32 * H)
                        act.wait_ge(s_cout, 32)
                        a.activation(mgh[:, ds(GB * j, GB), :], sga, ACT.Copy).then_inc(s_mgh, 1)

            with act.Fori(0, NMG // 2) as jj:
                for pair in range(2):
                    j = 2 * jj + pair
                    for p in range(NU):
                        split(U_WO + 8 * jj, 4 * pair + p + LEAD)
                    act.wait_ge(evacuated, 2 + G_WO + j + 1)
                    act.wait_ge(s_acc, j + 1)
                    a.activation(tmp[:, :, 0:TO], xT[:, ds(GB * j, GB), T0:T], ACT.Square).then_inc(s_x1q, 1)
                    for b in range(GB):
                        ins = a.activation(xh[:, ds(GB * j + b, 1), T0:T], xT[:, ds(GB * j + b, 1), T0:T], ACT.Copy,
                                           scale=vecT[:, ds(VF + GB * j + b, 1)])
                    ins.then_inc(s_x1h, 1)
            act.wait_ge(s_r2, 2)
            a.activation(rbc[:, 0:TO], tmp[:, 0, 0:TO], ACT.Sqrt).then_inc(s_r2a, 1)

            def ffn(c, last):
                with act.Fori(0, NMG // 2) as jj:
                    for pair in range(2):
                        j = 2 * jj + pair
                        for p in range(NU):
                            split(U_FF + UCH * c + 8 * jj, 4 * pair + p + LEAD)
                        act.wait_ge(s_uq, 1 + NMG * c + j + 1)
                        a.activation(uh[:, ds(GB * j, GB), :], uq[:], ACT.Copy).then_inc(s_uh, 1)

                def down(jj, tail):
                    for pair in range(2):
                        for p in range(NU):
                            if not (tail and pair == 1 and p + LEAD >= NU):
                                split(U_FF + UCH * c + 4 * NMG + 8 * jj, 4 * pair + p + LEAD)
                        if last:
                            j = 2 * jj + pair
                            act.wait_ge(evacuated, 2 + G_FF + 2 * NMG * c + NMG + j + 1)
                            act.wait_ge(s_ac2, j + 1)
                            a.activation(tmp[:, :, 0:TO], xT[:, ds(GB * j, GB), T0:T], ACT.Square).then_inc(s_x2q, 1)

                with act.Fori(0, NMG // 2 - 1 if last else NMG // 2) as jj:
                    down(jj, False)
                if last:
                    down(NMG // 2 - 1, True)

            with act.Fori(0, NCH - 1) as c:
                ffn(c, False)
            ffn(NCH - 1, True)
            act.wait_ge(s_r3, 2)
            a.activation(rcol[:], ssum[:], ACT.Sqrt).then_inc(s_r3a, 1)

        @block.vector
        def _(dve):
            v = nc.vector
            dve.sem_inc(low_done, RING)
            dve.sem_inc(evacuated, 2)
            for s in (s_ha, s_s, s_cst, s_den, s_cv, s_mgl, s_mgs, s_uq, s_ul, s_nso, s_z, s_yb):
                dve.sem_inc(s, 1)
            v.memset(ssum[:], 1.0).then_inc(s_set, 1)
            dve.wait_ge(s_colT, 1)
            v.tensor_copy(vecT[:], M[0][:, 0:vecT.shape[1]])
            v.tensor_copy(biasT[:], M[0][:, 128:128 + NB1 + NB2])
            v.tensor_copy(stT[:].rearrange("p k b r -> p (k b r)"),
                          M[0][:, 256:256 + stT.shape[1] * NB * (TAPS - 1)])
            v.tensor_copy(nT[:].rearrange("p g b h -> p (g b h)"),
                          M[0][:, 384:384 + GB * NB * H]).then_inc(s_col, 1)

            def split(base, s):
                dve.wait_ge(high_done, base + s + 1)
                dve.wait_ge(landed[s % RING], 4 * base + 16 * (s // RING) + 16)
                dve.wait_ge(unit_used, base + s + 1)
                v.tensor_tensor(wl[:, s % RING], raw[:, s % RING], wh[:, s % RING].bitcast(F32),
                                ALU.subtract).then_inc(low_done, 1)

            def root_step(r, x, t, seen, n):
                v.tensor_tensor(t, r, r, ALU.mult).then_inc(seen, 1)
                dve.wait_ge(seen, n + 1)
                v.tensor_tensor(t, t, x, ALU.mult).then_inc(seen, 1)
                dve.wait_ge(seen, n + 2)
                v.tensor_scalar(t, t, -0.5, 1.5, ALU.mult, ALU.add).then_inc(seen, 1)
                dve.wait_ge(seen, n + 3)
                v.tensor_tensor(r, r, t, ALU.mult).then_inc(seen, 1)
                dve.wait_ge(seen, n + 4)

            for k in range(KB // 2 + 1):
                if k < KB // 2:
                    dve.wait_ge(s_xtr, k + 1)
                    v.tensor_copy(xT[:, 2 * k:2 * k + 2, :], ACC[k % 2][:, :, 0:T]).then_inc(s_xT, 1)
                if k == 0:
                    dve.wait_ge(s_sq, 3)
                    v.tensor_scalar(ssum[:], ssum[:], 1.0 / D, EPS, ALU.mult, ALU.add).then_inc(s_ms, 1)
                if k == 1:
                    dve.wait_ge(s_rt, 1)
                    v.reciprocal(rcol[:], rcol[:]).then_inc(s_rc, 1)
                    dve.wait_ge(s_rc, 1)
                    root_step(rcol[:], ssum[:], rtmp[:], s_rc, 1)
                    for n, m in enumerate((P, P, NMETA + TS)):
                        v.tensor_scalar(rdiag[0:m, n, 0:m], ident[0:m, 0:m], rcol[0:m, n:n + 1], None,
                                        ALU.mult).then_inc(s_rd, 1)
                if k == 2:
                    dve.wait_ge(s_gw, 16)
                    dve.wait_ge(s_ghl, 2)
                    v.tensor_tensor(gl[:, :, 0:H], gw[:, :, 0:H], gh[:, :, 0:H].bitcast(F32),
                                    ALU.subtract).then_inc(s_ghl, 1)
                    v.tensor_tensor(gl[:, :, 32:32 + H], gw[:, :, H:2 * H], gh[:, :, 32:32 + H].bitcast(F32),
                                    ALU.subtract).then_inc(s_ghl, 1)
                if k > 0:
                    for b in (2 * k - 2, 2 * k - 1):
                        dve.wait_ge(s_xh, b + 1)
                        v.scalar_tensor_tensor(xl[:, b, :], xT[:, b, :], vecT[:, VG + b:VG + b + 1],
                                               xh[:, b, :].bitcast(F32), ALU.mult, ALU.subtract).then_inc(s_xl, 1)
            dve.wait_ge(s_rm, 1)
            v.tensor_copy(rbc[:], M[2][:, 0:T]).then_inc(s_r, 1)
            for n in range(LEAD):
                split(0, n)
            dve.wait_ge(s_r, 1)

            scale = rbc[:, 0:T].unsqueeze(1).to_broadcast([P, GB, T])
            scale_o = rbc[:, T0:T].unsqueeze(1).to_broadcast([P, GB, TO])

            def convolution(i, extra=()):
                for p in range(UCV):
                    split(UCV * i, p + LEAD)
                    if p in extra:
                        extra[p]()
                    if p in (3, 7):
                        g = p // 4
                        dve.wait_ge(unit_used, RING + UCV * i + 4 * g + 4)
                        if g == 0:
                            dve.wait_ge(s_z, 1 + i)
                            dve.wait_ge(s_cv, 1 + 12 * i)
                        else:
                            dve.wait_ge(s_zu, i + 1)
                        v.tensor_tensor(tmp[:], ACC[g][:, :, 0:T], scale, ALU.mult).then_inc(evacuated, 1)
                    if p == 7:
                        dve.wait_ge(s_zc, i + 1)
                        v.tensor_copy(zs[:, :, :, 0:TAPS - 1], stT[:, ds(GB * i, GB), :, :])
                        v.tensor_tensor(zp[:], tmp[:, :, 0:TP], zu[:, :, 0:TP], ALU.mult)
                        v.tensor_tensor(zs[:, :, :, TAPS - 1:], tmp[:, :, TP:T].rearrange("p g (b t) -> p g b t", t=DS),
                                        zu[:, :, TP:T].rearrange("p g (b t) -> p g b t", t=DS), ALU.mult) \
                            .then_inc(s_z, 1)
                        dve.wait_ge(s_z, 1 + i + 1)
                        v.tensor_copy(zlast[:, ds(GB * i, GB), 0:TAPS - 1], zp[:, :, TP - TAPS + 1:TP])
                        v.tensor_copy(zlast[:, ds(GB * i, GB), TAPS - 1:].rearrange("p g (b r) -> p g b r", r=TAPS - 1),
                                      zs[:, :, :, DS:DS + TAPS - 1])
                        for r in range(TAPS):
                            for b in range(GB):
                                w = vecT[:, ds(VC + r * (CW // P) + GB * i + b, 1)]
                                out_p = yb[:, ds(GB * i + b, 1), 0:SEQ]
                                out_s = yb[:, ds(GB * i + b, 1), SEQ:TO].rearrange("p o (b t) -> p (o b) t", t=DS)
                                src_p = zp[:, b:b + 1, T0 - TAPS + 1 + r:T0 - TAPS + 1 + r + SEQ]
                                src_s = zs[:, b, :, r:r + DS]
                                for out, src in ((out_p, src_p), (out_s, src_s)):
                                    if r == 0:
                                        v.tensor_scalar(out, src, w, None, ALU.mult).then_inc(s_cv, 1)
                                    else:
                                        v.scalar_tensor_tensor(out, src, w, out, ALU.mult, ALU.add).then_inc(s_cv, 1)
                            dve.wait_ge(s_cv, 1 + 12 * i + 4 * r + 4)

            step = [0]

            def row(ins):
                step[0] += 1
                ins.then_inc(s_row, 1)
                dve.wait_ge(s_row, step[0])

            samp = lambda r: r[:, TP:T].rearrange("p (b t) -> p b t", t=DS)
            mx = samp(rows)

            def gates():
                dve.wait_ge(s_gp, 1)
                dve.wait_ge(s_small, 48)
                v.tensor_tensor(fgr[:], M[3][32:32 + H, 0:T], rbc[32:32 + H, :], ALU.mult)
                v.tensor_tensor(igr[:], M[3][0:H, 0:T], rbc[0:H, :], ALU.mult).then_inc(s_gz, 1)
                dve.wait_ge(s_gz, 2)
                v.tensor_scalar(fgr[:], fgr[:], bf[:, 0:1], None, ALU.add).then_inc(s_row, 1)
                step[0] += 1
                row(v.tensor_scalar(igr[:], igr[:], bi[:, 0:1], None, ALU.add))

            def sums():
                dve.wait_ge(s_rowa, 3)
                row(v.scalar_tensor_tensor(fgr[:], fgr[:], 0.0, e1r[:], ALU.min, ALU.subtract))
                dve.wait_ge(s_const, 19)
                row(v.tensor_tensor_scan(brw[:], keep[:], fgr[:], 0.0, ALU.mult, ALU.add))
                row(v.tensor_tensor(arw[:], igr[:], brw[:], ALU.subtract))
                v.tensor_copy(a1r[:, 1:TP], arw[:, 1:TP])
                v.tensor_copy(samp(a1r)[:, :, 1:DS], samp(arw)[:, :, 1:DS])
                row(v.tensor_scalar(a1r[:, 0:1], arw[:, 0:1], 0.0, None, ALU.max))
                row(v.tensor_tensor(samp(a1r)[:, :, 0], samp(arw)[:, :, 0], m0[:], ALU.max))
                row(v.tensor_tensor_scan(rows[:, 0:T], fall[:], a1r[:], 0.0, ALU.add, ALU.max))

            def exponents():
                row(v.tensor_tensor(mrw[:], brw[:], rows[:, 0:T], ALU.add))
                row(v.tensor_tensor(wir[:], m0[:].unsqueeze(2).to_broadcast([H, NB, DS]), mx, ALU.subtract))
                v.tensor_scalar(wkr[:, 0:TP], arw[:, 0:TP], rows[:, TP - 1:TP], None, ALU.subtract)
                for c in (TP, T):
                    ins = v.tensor_tensor(wkr[:, c:c + TS].rearrange("p (b t) -> p b t", t=DS), samp(arw),
                                          mx[:, :, DS - 1:DS].to_broadcast([H, NB, DS]), ALU.subtract)
                row(ins)

            def decays():
                dve.wait_ge(s_rowa, 6)
                row(v.tensor_copy(decr[:], rows[:, RWI:RWI + TS].rearrange("p (b t) -> p b t", t=DS)
                                  [:, :, DS - 1]))

            with dve.Fori(0, H - 1) as i:
                convolution(i)
            convolution(H - 1, {0: gates, 2: sums, 4: exponents, 6: decays})

            dve.wait_ge(s_rowT, 1)
            for n, (k0, nk) in enumerate(KT):
                m = 2 * nk if n == 3 else nk
                v.tensor_copy(acol[0:nk, n, :], M[0][0:nk, n * H:(n + 1) * H])
                v.tensor_scalar(wkcol[0:m, n, :], M[0][0:m, (4 + n) * H:(5 + n) * H], DK ** -0.5, None, ALU.mult)
            v.tensor_copy(deccol[:], M[0][0:NB, 8 * H:9 * H]).then_inc(s_rowc, 1)
            dve.wait_ge(s_rowc, 1)

            with dve.Fori(0, H) as h:
                def evacuate(g, pos, n):
                    dve.wait_ge(unit_used, RING + U_HEAD + UH * h + pos + 1)
                    if g > 0:
                        dve.wait_ge(biased, GH * h + g)
                    v.tensor_tensor(tmp[:, :, 0:n], ACC[HEAD_ACC[g]][:, :, 0:n], scale if n == T else scale_o,
                                    ALU.mult).then_inc(evacuated, 1)

                for p in range(UH):
                    split(U_HEAD + UH * h, p + LEAD)
                    if p == 0:
                        dve.wait_ge(s_cup, 1 + 8 * h)
                        v.tensor_scalar(rowh[:], rows[:], ident[0:H, ds(h, 1)], None, ALU.mult).then_inc(s_rowh, 1)
                    if p == 3:
                        dve.wait_ge(s_ha, 1 + h)
                        evacuate(0, 3, T)
                    if p == 4:
                        dve.wait_ge(s_bc, h + 1)
                        dve.wait_ge(s_num, 1 + h)
                        for n, ((k0, nk), (q0, nq, off)) in enumerate(zip(KT, QT)):
                            m = mask[0:nk, q0 - k0:q0 - k0 + nq] if n < 3 else \
                                smask[:].rearrange("p b t -> p (b t)")
                            ins = v.scalar_tensor_tensor(E[0:nk, off:off + nq], bc[0:nk, q0:q0 + nq],
                                                         acol[0:nk, n, ds(h, 1)], m, ALU.max, ALU.add)
                        ins.then_inc(s_x, 1)
                        dve.wait_ge(biased, GH * h + 1)
                        v.tensor_tensor(qw[:], qT[:, :, TP:T].rearrange("p g (b t) -> p g b t", t=DS),
                                        bc[:, RWI:RWI + TS].rearrange("p (o b t) -> p o b t", o=1, t=DS)
                                        .to_broadcast([P, GB, NB, DS]), ALU.mult).then_inc(s_qw, 1)
                        dve.wait_ge(s_qw, h + 1)
                        v.tensor_tensor(qn[:], qw[:], nT[:, :, :, ds(h, 1)].to_broadcast([P, GB, NB, DS]),
                                        ALU.mult).then_inc(s_qn, 1)
                    if p == 5:
                        dve.wait_ge(s_qmh, h + 1)
                        v.tensor_tensor(q_blocks(TS), qw[:], q_blocks(0).bitcast(F32), ALU.subtract).then_inc(s_qml, 1)
                    if p == 7:
                        evacuate(1, 7, T)
                    if p == 9:
                        dve.wait_ge(s_kw, h + 1)
                        up = slice(TS, 2 * TS)
                        v.scalar_tensor_tensor(kws[up, :], M[1][up, DK:2 * DK], wkcol[up, 3, ds(h, 1)],
                                               kws[up, :].bitcast(F32), ALU.mult, ALU.subtract).then_inc(s_kwl, 1)
                    if p == 10:
                        dve.wait_ge(s_sc, h + 1)
                        dve.wait_ge(s_e, h + 1)
                        for n, ((k0, nk), (q0, nq, off)) in enumerate(zip(KT, QT)):
                            src = M[2][0:nk, off:off + nq] if n < 2 else M[3][0:nk, off - QT[2][2]:off - QT[2][2] + nq]
                            ins = v.scalar_tensor_tensor(E[0:nk, off:off + nq], src, DK ** -0.5,
                                                         E[0:nk, off:off + nq], ALU.mult, ALU.mult)
                        ins.then_inc(s_s, 1)
                    if p == 11:
                        evacuate(2, 11, T)
                    if p == 12:
                        dve.wait_ge(s_vt, h + 1)
                        v.tensor_tensor(vsl[:], M[1][0:TS, DV:2 * DV], vsh[0:TS, :].bitcast(F32),
                                        ALU.subtract).then_inc(s_vsl, 1)
                    if p == 16:
                        dve.wait_ge(s_abs, h + 1)
                        v.tensor_tensor(den[:], den[:], bc[:, REM:REM + TO], ALU.max).then_inc(s_den, 1)
                        dve.wait_ge(s_den, 1 + 2 * h + 1)
                        v.reciprocal(den[:], den[:]).then_inc(s_den, 1)
                        dve.wait_ge(s_den, 1 + 2 * h + 2)
                        v.tensor_tensor(hT[:], ps[:, 4:6, 0:TO], den[:].unsqueeze(1).to_broadcast([P, GB, TO]),
                                        ALU.mult).then_inc(s_h, 1)
                    if p == 18:
                        dve.wait_ge(s_cpp, h + 1)
                        dve.wait_ge(s_cpo, 2 * h + 2)
                        dve.wait_ge(s_nin, 16 * h + 16)
                        v.scalar_tensor_tensor(nso[:], nin[:], deccol[:, ds(h, 1)], M[3][0:NB, DK:2 * DK],
                                               ALU.mult, ALU.add).then_inc(s_nso, 1)
                    if p == 19:
                        evacuate(3, 19, TO)
                        dve.wait_ge(biased, GH * h + 4)
                        y = yb[:, ds(GB * h, GB), :]
                        v.tensor_tensor(y, tmp[:, :, 0:TO], y, ALU.mult).then_inc(s_yb, 1)
                    if 19 <= p < 23:
                        dve.wait_ge(s_Cin, 32 * h + 32)
                        for b in (2 * (p - 19), 2 * (p - 19) + 1):
                            dve.wait_ge(s_cup, 1 + 8 * h + b + 1)
                            C2 = Cs[:, b].rearrange("p g e -> p (g e)")
                            v.scalar_tensor_tensor(C2, C2, bc[:, RWI + DS * b + DS - 1:RWI + DS * b + DS], M[b % 2],
                                                   ALU.mult, ALU.add).then_inc(s_cst, 1)
                    if p == 23:
                        dve.wait_ge(s_yb, 1 + h + 1)
                        evacuate(4, 23, TO)
                        dve.wait_ge(biased, GH * h + 5)
                        dve.wait_ge(s_h, h + 1)
                        v.tensor_tensor(ha[:, ds(GB * h, GB), :], tmp[:, :, 0:TO], hT[:], ALU.mult).then_inc(s_ha, 1)

            dve.wait_ge(s_ha, 1 + H)
            dve.wait_ge(s_hyh, 1)
            v.tensor_tensor(hal[:], ha[:], hah[:].bitcast(F32), ALU.subtract).then_inc(s_hyl, 1)
            dve.wait_ge(s_hyh, 2)
            v.tensor_tensor(ybl[:], yb[:], ybh[:].bitcast(F32), ALU.subtract).then_inc(s_hyl, 1)
            dve.wait_ge(s_hyl, 2)

            with dve.Fori(0, NMG) as j:
                def evacuate_gate(g, gate):
                    dve.wait_ge(unit_used, RING + U_MERGE + 3 * NU * j + 4 * g + 4)
                    v.tensor_tensor(gate, ACC[g][:, :, 0:TO], scale_o, ALU.mult).then_inc(evacuated, 1)

                for p in range(12):
                    split(U_MERGE + 3 * NU * j, p + LEAD)
                    if p == 3:
                        dve.wait_ge(s_mgh, 1 + j)
                        dve.wait_ge(s_mgl, 1 + j)
                        evacuate_gate(0, sga)
                    if p == 7:
                        dve.wait_ge(s_mgs, 1 + 2 * j)
                        evacuate_gate(1, sgb)
                    if p == 9:
                        dve.wait_ge(s_sga, j + 1)
                        dve.wait_ge(unit_used, RING + U_MERGE + 3 * NU * j + 10)
                        v.tensor_tensor(sga, ACC[0][:, :, 0:TO], sga, ALU.mult).then_inc(evacuated, 1)
                    if p == 11:
                        dve.wait_ge(s_sgb, j + 1)
                        dve.wait_ge(unit_used, RING + U_MERGE + 3 * NU * j + 12)
                        v.tensor_tensor(sgb, ACC[1][:, :, 0:TO], sgb, ALU.mult).then_inc(evacuated, 1)
                        dve.wait_ge(evacuated, 2 + G_MERGE + 4 * j + 4)
                        v.tensor_tensor(sga, sga, sgb, ALU.add).then_inc(s_mgs, 2)
                        dve.wait_ge(s_mgh, 1 + j + 1)
                        v.tensor_tensor(mgl[:, ds(GB * j, GB), :], sga, mgh[:, ds(GB * j, GB), :].bitcast(F32),
                                        ALU.subtract).then_inc(s_mgl, 1)

            v.memset(sqacc[:], 0.0).then_inc(s_acc, 1)
            with dve.Fori(0, NMG // 2) as jj:
                for pair in range(2):
                    j = 2 * jj + pair
                    for p in range(NU):
                        split(U_WO + 8 * jj, 4 * pair + p + LEAD)
                    dve.wait_ge(unit_used, RING + U_WO + 8 * jj + 4 * pair + 4)
                    x1 = xT[:, ds(GB * j, GB), T0:T]
                    v.tensor_tensor(x1, ACC[pair][:, :, 0:TO], x1, ALU.add).then_inc(evacuated, 1)
                    dve.wait_ge(s_x1q, j + 1)
                    dve.wait_ge(s_acc, j + 1)
                    v.tensor_tensor(sqacc[:], sqacc[:], tmp[:, :, 0:TO], ALU.add).then_inc(s_acc, 1)
                    dve.wait_ge(s_x1h, j + 1)
                    for b in range(GB):
                        ins = v.scalar_tensor_tensor(
                            xl[:, ds(GB * j + b, 1), T0:T], xT[:, ds(GB * j + b, 1), T0:T],
                            vecT[:, ds(VF + GB * j + b, 1)], xh[:, ds(GB * j + b, 1), T0:T].bitcast(F32),
                            ALU.mult, ALU.subtract)
                    ins.then_inc(s_x1l, 1)
            dve.wait_ge(s_acc, NMG + 1)
            v.tensor_tensor(sqacc[:, 0, :], sqacc[:, 0, :], sqacc[:, 1, :], ALU.add).then_inc(s_r2, 1)
            dve.wait_ge(s_r2p, 1)
            v.tensor_scalar(tmp[:, 0, 0:TO], M[0][:, 0:TO], 1.0 / D, EPS, ALU.mult, ALU.add).then_inc(s_r2, 1)
            dve.wait_ge(s_r2a, 1)
            v.reciprocal(rbc[:, 0:TO], rbc[:, 0:TO]).then_inc(s_r2, 1)
            dve.wait_ge(s_r2, 3)
            root_step(rbc[:, 0:TO], tmp[:, 0, 0:TO], tmp[:, 1, 0:TO], s_r2, 3)
            scale_u = rbc[:, 0:TO].unsqueeze(1).to_broadcast([P, GB, TO])

            def ffn(c, last):
                with dve.Fori(0, NMG // 2) as jj:
                    for pair in range(2):
                        j = 2 * jj + pair
                        for p in range(NU):
                            split(U_FF + UCH * c + 8 * jj, 4 * pair + p + LEAD)
                        dve.wait_ge(unit_used, RING + U_FF + UCH * c + 8 * jj + 4 * pair + 4)
                        dve.wait_ge(s_uq, 1 + NMG * c + j)
                        v.scalar_tensor_tensor(ur[:], ACC[pair][:, :, 0:TO], 0.0, scale_u, ALU.max, ALU.mult) \
                            .then_inc(evacuated, 1)
                        dve.wait_ge(evacuated, 2 + G_FF + 2 * NMG * c + j + 1)
                        dve.wait_ge(s_uh, 1 + NMG * c + j)
                        dve.wait_ge(s_ul, 1 + NMG * c + j)
                        v.tensor_tensor(uq[:], ur[:], ur[:], ALU.mult).then_inc(s_uq, 1)
                        dve.wait_ge(s_uh, 1 + NMG * c + j + 1)
                        v.tensor_tensor(ul[:, ds(GB * j, GB), :], uq[:], uh[:, ds(GB * j, GB), :].bitcast(F32),
                                        ALU.subtract).then_inc(s_ul, 1)

                def down(jj, tail):
                    for pair in range(2):
                        base = U_FF + UCH * c + 4 * NMG + 8 * jj
                        for p in range(NU):
                            if not (tail and pair == 1 and p + LEAD >= NU):
                                split(base, 4 * pair + p + LEAD)
                        j = 2 * jj + pair
                        dve.wait_ge(unit_used, RING + base + 4 * pair + 4)
                        dve.wait_ge(evacuated, 2 + G_FF + 2 * NMG * c)
                        x2 = xT[:, ds(GB * j, GB), T0:T]
                        v.tensor_tensor(x2, ACC[pair][:, :, 0:TO], x2, ALU.add).then_inc(evacuated, 1)
                        if last:
                            dve.wait_ge(s_x2q, j + 1)
                            dve.wait_ge(s_ac2, j + 1)
                            v.tensor_tensor(sqacc[:], sqacc[:], tmp[:, :, 0:TO], ALU.add).then_inc(s_ac2, 1)

                with dve.Fori(0, NMG // 2 - 1 if last else NMG // 2) as jj:
                    down(jj, False)
                if last:
                    down(NMG // 2 - 1, True)

            with dve.Fori(0, NCH - 1) as c:
                ffn(c, False)
            v.memset(sqacc[:], 0.0).then_inc(s_ac2, 1)
            ffn(NCH - 1, True)
            dve.wait_ge(s_ac2, NMG + 1)
            v.tensor_tensor(sqacc[:, 0, :], sqacc[:, 0, :], sqacc[:, 1, :], ALU.add).then_inc(s_r3, 1)
            dve.wait_ge(s_r3p, 1)
            v.tensor_scalar(ssum[:, 0:2], M[0][:, 0:2], 1.0 / D, EPS, ALU.mult, ALU.add)
            v.tensor_scalar(ssum[0:TS, 2:3], M[0][0:TS, 2:3], 1.0 / D, EPS, ALU.mult, ALU.add).then_inc(s_r3, 1)
            dve.wait_ge(s_r3a, 1)
            v.reciprocal(rcol[:], rcol[:]).then_inc(s_r3, 1)
            dve.wait_ge(s_r3, 3)
            root_step(rcol[:], ssum[:], rtmp[:], s_r3, 3)
            dve.wait_ge(s_gfb, 16)
            for i, (n, q) in enumerate((n, q) for n in range(3) for q in range(KB // 4)):
                nt = P if n < 2 else TS
                dve.wait_ge(s_yt, i + 1)
                v.scalar_tensor_tensor(yo[0:nt, n, 512 * q:512 * q + 512], ps[0:nt, YBANK[i % 6], :],
                                       rcol[0:nt, n:n + 1], gfb[0:nt, 512 * q:512 * q + 512],
                                       ALU.mult, ALU.mult).then_inc(s_y, 1)

        @block.tensor
        def _(pe):
            def product(out, lhsT, rhs, start=True, stop=True):
                return pe.matmul(out, lhsT, rhs, start=start, stop=stop)

            pe.sem_inc(unit_used, RING)
            for s in (s_bcp, s_num, s_cup, s_cqp):
                pe.sem_inc(s, 1)
            pe.wait_ge(s_const, 2)
            pe.wait_ge(s_vrows, 64)
            pe.wait_ge(s_brows, 64)
            nv, nb, nc2 = vrows.shape[0], brows.shape[0], crows.shape[0]
            pe.transpose(M[0][:, 0:nv], vrows[:], ident[0:nv, 0:nv])
            pe.transpose(M[0][:, 128:128 + nb], brows[:], ident[0:nb, 0:nb])
            for k in range(CW // P):
                pe.transpose(M[0][:, 256 + nc2 * k:256 + nc2 * (k + 1)], crows[:, P * k:P * k + P], ident[0:nc2, 0:nc2])
            for g in range(GB):
                ins = pe.transpose(M[0][:, 384 + NB * H * g:384 + NB * H * (g + 1)], nrows[:, P * g:P * g + P],
                                   ident[0:NB * H, 0:NB * H])
            ins.then_inc(s_colT, 1)
            for n in range(3):
                pe.wait_ge(s_xtok[n], 16 if n == 1 else 32)
            for k in range(KB // 2):
                if k >= 2:
                    pe.wait_ge(s_xT, k - 1)
                for b in range(2):
                    for n, nt in enumerate((P, P, NMETA + TS)):
                        c0 = P * (2 * k + b)
                        ins = pe.transpose(ACC[k % 2][:, b, P * n:P * n + nt], xtok[0:nt, n, c0:c0 + P],
                                           ident[0:nt, 0:nt])
                ins.then_inc(s_xtr, 1)
            pe.wait_ge(s_ghl, 4)
            for k in range(KB):
                if k == 4:
                    pe.wait_ge(s_rd, 3)
                    pe.wait_ge(s_const, 3)
                    for n, nt in enumerate((P, P, NMETA + TS)):
                        ins = product(M[2][:, P * n:P * n + nt], ones[0:nt, :], rdiag[0:nt, n, 0:nt])
                    ins.then_inc(s_rm, 1)
                pe.wait_ge(s_xl, k + 1)
                product(M[3][:, 0:T], gh[:, k, :], xh[:, k, :], start=k == 0, stop=False)
                product(M[3][:, 0:T], gh[:, k, :], xl[:, k, :], start=False, stop=False)
                ins = product(M[3][:, 0:T], gl[:, k, :], xh[:, k, :], start=False, stop=k == KB - 1)
            ins.then_inc(s_gp, 1)
            pe.wait_ge(s_col, 1)

            def unit(base, s, acc, rh, rl, kb, c0, first, last):
                pe.wait_ge(low_done, RING + base + s + 1)
                w, n = s % RING, acc.shape[2]
                for b in range(GB):
                    for k in range(UK):
                        hi, lo = (t[:, w, k, P * b:P * b + P] for t in (wh, wl))
                        mh, ml = (t[:, kb + k, c0:c0 + n] for t in (rh, rl))
                        product(acc[:, b, :], hi, mh, start=first and k == 0, stop=False)
                        product(acc[:, b, :], hi, ml, start=False, stop=False)
                        ins = product(acc[:, b, :], lo, mh, start=False, stop=last and k == UK - 1)
                ins.then_inc(unit_used, 1)

            with pe.Fori(0, H) as i:
                for p in range(UCV):
                    if p % 4 == 0:
                        pe.wait_ge(evacuated, 2 * i + p // 4 + 1)
                    unit(UCV * i, p, ACC[p // 4][:, :, 0:T], xh, xl, UK * (p % 4), 0, p % 4 == 0, p % 4 == 3)

            pe.wait_ge(s_row, 12)
            for n, (k0, nk) in enumerate(KT):
                for m, r in enumerate((arw, wkr)):
                    m2 = 2 * nk if n == 3 and r is wkr else nk
                    pe.transpose(M[0][0:m2, (4 * m + n) * H:(4 * m + n + 1) * H], r[:, k0:k0 + m2], ident[0:H, 0:H])
            pe.transpose(M[0][0:NB, 8 * H:9 * H], decr[:], ident[0:H, 0:H]).then_inc(s_rowT, 1)

            def by_token(src, width, done):
                for n, (k0, nk) in enumerate(KT):
                    for d in range(GB):
                        m = 2 * nk if n == 3 else nk
                        c = (n % 2) * width + P * d
                        ins = pe.transpose(M[n // 2][0:m, c:c + P], src[:, d, k0:k0 + m], ident[:])
                ins.then_inc(done, 1)

            with pe.Fori(0, H) as h:
                for p in range(UH):
                    u, base = p % 4, U_HEAD + UH * h
                    g = (0, 1, 2, None, 3, 4)[p // 4]
                    if g is None:
                        if u == 0:
                            pe.wait_ge(s_qml, h + 1)
                            pe.wait_ge(s_s, 1 + h + 1)
                        pe.wait_ge(low_done, RING + base + p + 1)
                        for k in range(NB // 2):
                            b = NB // 2 * (u // GB) + k
                            q = qm[:, u % GB, P * b:P * b + P]
                            product(M[2][:, 0:DV], q, wh[:, u, k, :], start=u == 0 and k == 0, stop=False)
                            ins = product(M[2][:, 0:DV], q, wl[:, u, k, :], start=False, stop=u == 3 and k == 3)
                        ins.then_inc(unit_used, 1)
                        if u == 3:
                            pe.wait_ge(unit_used, RING + base + p + 1)
                            pe.sem_inc(s_cqp, 1)
                    else:
                        n, c0 = (T, 0) if g in (1, 2) else (TO, T0)
                        if u == 0:
                            pe.wait_ge(evacuated, G_HEAD + GH * h + g + 1)
                        if p == 20:
                            pe.wait_ge(s_nso, 1 + h + 1)
                        out = ACC[HEAD_ACC[g]][:, :, 0:n]
                        if g == 0:
                            out, n, c0 = ACC[0][:, :, 0:T], T, 0
                        unit(base, p, out, xh, xl, UK * u, c0, u == 0, u == 3)
                    if p == 1:
                        pe.wait_ge(s_rowh, h + 1)
                        pe.wait_ge(s_cst, 1 + 8 * h)
                        product(ps[:, 4, 0:512], ones[0:H, :], rowh[:, 0:512])
                        product(ps[:, 5, 0:RW - 512], ones[0:H, :], rowh[:, 512:RW]).then_inc(s_bcp, 1)
                    if p == 9:
                        pe.wait_ge(biased, GH * h + 2)
                        pe.wait_ge(s_bc, h + 1)
                        by_token(kT, DK, s_ktr)
                        pe.wait_ge(evacuated, 2 + G_HEAD + GH * h)
                        for n, ((k0, nk), (q0, nq, off)) in enumerate(zip(KT, QT)):
                            out = M[2][0:nk, off:off + nq] if n < 2 else M[3][0:nk, off - QT[2][2]:off - QT[2][2] + nq]
                            for d in range(GB):
                                ins = product(out, kT[:, d, k0:k0 + nk], qT[:, d, q0:q0 + nq], d == 0, d == GB - 1)
                        ins.then_inc(s_sc, 1)
                    if p == 12:
                        pe.wait_ge(biased, GH * h + 3)
                        pe.wait_ge(s_kwl, h + 1)
                        by_token(kT, DV, s_vtr)
                    if p == 16:
                        pe.wait_ge(s_vsl, h + 1)
                        pe.wait_ge(s_qn, h + 1)
                        pe.wait_ge(s_cq, h + 1)
                        pe.wait_ge(s_const, 19)
                        for e in range(GB + 1):
                            out = M[e] if e < GB else M[3]
                            for n, ((k0, nk), (q0, nq, off)) in enumerate(zip(KT, QT)):
                                w = vt[0:nk, n, P * e:P * e + P] if e < GB else ones[0:nk, :]
                                product(out[:, q0 - T0:q0 - T0 + nq], w, E[0:nk, off:off + nq],
                                        start=n in (0, 3), stop=n == 2)
                            if e < GB:
                                ins = product(out[:, TP - T0:TO], cq[:, P * e:P * e + P], fold[:], False, True)
                            else:
                                for d in range(GB):
                                    ins = product(out[:, TP - T0:TO], ones[:], qn[:, d].rearrange("p b t -> p (b t)"),
                                                  start=False, stop=d == GB - 1)
                        ins.then_inc(s_num, 1)
                    if p == 18:
                        pe.wait_ge(s_abs, h + 1)
                        for d in range(GB):
                            for n, (k0, nk) in enumerate(KT[0:3]):
                                product(M[2][:, DV * d:DV * d + DV], kw[0:nk, n, P * d:P * d + P], vt[0:nk, n, :],
                                        n == 0, n == 2)
                        for n, (k0, nk) in enumerate(KT[0:3]):
                            product(M[3][0:1, 0:DK], ones[0:nk, 0:1], kw[0:nk, n, :], n == 0, n == 2)
                        product(M[3][0:NB, DK:2 * DK], onehot[:], kws[:].bitcast(F32)).then_inc(s_cpp, 1)
                    if 19 <= p < 23:
                        i = p - 19
                        pe.wait_ge(s_kwm, 2 * h + i // 2 + 1)
                        if i == 0:
                            pe.wait_ge(s_h, h + 1)
                        else:
                            pe.wait_ge(s_cst, 1 + 8 * h + 2 * i)
                        for b in (2 * i, 2 * i + 1):
                            for d in range(GB):
                                out = M[b % 2][:, DV * d:DV * d + DV]
                                product(out, kwm[:, b % 4, P * d:P * d + P], vsh[:], True, False)
                                ins = product(out, kwm[0:TS, b % 4, P * d:P * d + P], vsl[:], False, True)
                            ins.then_inc(s_cup, 1)

            nl = clast.shape[0]
            pe.wait_ge(s_cst, 1 + 8 * H)
            for k in range(CW // P):
                ins = pe.transpose(M[k // 4][0:nl, P * (k % 4):P * (k % 4) + P], zlast[:, k, :], ident[:])
            ins.then_inc(s_clt, 1)

            with pe.Fori(0, NMG) as j:
                for g in range(4):
                    pe.wait_ge(evacuated, G_MERGE + 4 * j + g + 1)
                    acc = ACC[g % 2][:, :, 0:TO]
                    if g < 2:
                        for u in range(NU):
                            unit(U_MERGE + 3 * NU * j, 4 * g + u, acc, xh, xl, UK * u, T0, u == 0, u == NU - 1)
                    else:
                        pe.wait_ge(s_hyl, g - 1)
                        rh, rl = ((hah, hal), (ybh, ybl))[g - 2]
                        for u in range(2):
                            unit(U_MERGE + 3 * NU * j, 4 + 2 * g + u, acc, rh, rl, UK * u, 0, u == 0, u == 1)
            with pe.Fori(0, NMG // 2) as jj:
                for pair in range(2):
                    pe.wait_ge(evacuated, G_WO + 2 * jj + pair + 1)
                    for u in range(NU):
                        pe.wait_ge(s_mgl, 1 + 2 * u + 2)
                        unit(U_WO + 8 * jj, 4 * pair + u, ACC[pair][:, :, 0:TO], mgh, mgl, UK * u, 0,
                             u == 0, u == NU - 1)
            pe.wait_ge(s_r2, 1)
            product(M[0][:, 0:TO], ones[:], sqacc[:, 0, :]).then_inc(s_r2p, 1)
            with pe.Fori(0, NCH) as c:
                with pe.Fori(0, NMG // 2) as jj:
                    for pair in range(2):
                        pe.wait_ge(evacuated, G_FF + 2 * NMG * c + 2 * jj + pair + 1)
                        for u in range(NU):
                            pe.wait_ge(s_x1l, 2 * u + 2)
                            unit(U_FF + UCH * c + 8 * jj, 4 * pair + u, ACC[pair][:, :, 0:TO], xh, xl, UK * u, T0,
                                 u == 0, u == NU - 1)
                with pe.Fori(0, NMG // 2) as jj:
                    for pair in range(2):
                        pe.wait_ge(evacuated, G_FF + 2 * NMG * c + NMG + 2 * jj + pair + 1)
                        for u in range(NU):
                            pe.wait_ge(s_ul, 1 + NMG * c + 2 * u + 2)
                            unit(U_FF + UCH * c + 4 * NMG + 8 * jj, 4 * pair + u, ACC[pair][:, :, 0:TO], uh, ul,
                                 UK * u, 0, u == 0, u == NU - 1)
            pe.wait_ge(s_r3, 1)
            for n, (c0, nt) in enumerate(((0, P), (P, P), (2 * P, TS))):
                ins = product(M[0][0:nt, n:n + 1], sqacc[:, 0, c0:c0 + nt], ones[:, 0:1])
            ins.then_inc(s_r3p, 1)
            pe.wait_ge(evacuated, 2 + G_FF + 2 * NMG * NCH)
            for i, (n, q) in enumerate((n, q) for n in range(3) for q in range(KB // 4)):
                nt = P if n < 2 else TS
                if i >= 6:
                    pe.wait_ge(s_y, i - 5)
                for k in range(4):
                    ins = pe.transpose(ps[0:nt, YBANK[i % 6], P * k:P * k + P],
                                       xT[:, 4 * q + k, T0 + P * n:T0 + P * n + nt], ident[:])
                ins.then_inc(s_yt, 1)


_INS = ["x_prompt", "x_sample", "state_mlstm_C", "state_mlstm_n", "state_mlstm_m", "state_conv", "meta_tokens",
        "g_mix", "w_in", "b_in", "w_conv", "p_a", "p_b", "w_o", "g_ffn", "w_up", "w_down", "g_final"]


def kernel(**inputs):
    import numpy as np
    import concourse.bacc as bacc
    from concourse.bass_utils import run_bass_kernel_spmd

    nc = bacc.Bacc("TRN2", target_bir_lowering=False, num_devices=1)
    arrays, args = {}, []
    for name in _INS:
        a = np.ascontiguousarray(inputs[name])
        arrays[f"in_{name}_dram"] = a
        args.append(nc.dram_tensor(f"in_{name}_dram", a.shape, mybir.dt.from_np(a.dtype), kind="ExternalInput").ap())
    L, NB, H, DK, DV = inputs["state_mlstm_C"].shape
    taps, cw = inputs["state_conv"].shape[2:]
    shapes = [inputs["x_prompt"].shape, inputs["x_sample"].shape,
              (L, 1, H, DK, DV), (L, 1, H, DK), (L, 1, H), (L, 1, taps, cw),
              (L, NB, H, DK, DV), (L, NB, H, DK), (L, NB, H), (L, NB, taps, cw)]
    for i, shape in enumerate(shapes):
        args.append(nc.dram_tensor(f"out_{i}_dram", tuple(shape), F32, kind="ExternalOutput").ap())
    build(nc, *args)
    r = run_bass_kernel_spmd(nc, [arrays], core_ids=[0])
    return tuple(r.results[0][f"out_{i}_dram"] for i in range(len(shapes)))
```

```python
from contextlib import ExitStack

import concourse.bass as bass
from concourse import mybir

F32 = mybir.dt.float32
F32R = mybir.dt.float32r
ALU = mybir.AluOpType
ACT = mybir.ActivationFunctionType
P = 128
ds = bass.ds

EPS = 1e-6
GAP = 64
BIG = 1e30
FAR = 3e38
RING = 4
LEAD = 3
UK = 4
GC = 256
GB = GC // P


def build(nc, x_prompt, x_sample, state_C, state_n, state_m, state_conv, meta, g_mix, w_in, b_in,
          w_conv, p_a, p_b, w_o, g_ffn, w_up, w_down, g_final,
          y_prompt, y_sample, C_prompt, n_prompt, m_prompt, conv_prompt,
          C_sample, n_sample, m_sample, conv_sample):
    _, SEQ, D = x_prompt.shape
    NB, DS, _ = x_sample.shape
    _, _, H, DK, DV = state_C.shape
    NMETA = meta.shape[0]
    CW = w_conv.shape[2]
    TAPS = w_conv.shape[1]
    FF = w_up.shape[2]
    T0 = NMETA
    TP = NMETA + SEQ
    TS = NB * DS
    T = TP + TS
    TO = T - T0
    KB = D // P
    assert DK == GC and DV == GC and H * DV == CW == H * GC and D % (P * UK) == 0
    assert T <= 512 and TP % P == NMETA and TS <= P and TAPS == 3
    MW = H * DV
    CQ, CK, CV, CG = 0, H * DK, 2 * H * DK, 2 * H * DK + MW
    CO = CG + 2 * H
    CU, CC, CB = CO + MW, CO + MW + CW, CO + MW + 2 * CW
    CGA, CGB = CO + MW + 3 * CW, CO + MW + 3 * CW + D
    NB1, NB2 = CG // P, (CGB + D - CO) // P
    BQ, BK, BV = 0, CK // P, CV // P
    BO = NB1
    BU, BC_, BB = BO + MW // P, BO + (CU + CW - CO) // P, BO + (CB - CO) // P
    BGA, BGB = BO + (CGA - CO) // P, BO + (CGB - CO) // P
    KT = [(0, P), (P, P), (2 * P, NMETA), (TP, TS)]
    QT = [(T0, TP - T0, 0), (P, TP - P, TP - T0), (2 * P, TP - 2 * P, 2 * TP - T0 - P),
          (TP, TS, 3 * TP - T0 - 3 * P)]
    SW = QT[3][2] + TS
    RW = T + TO + TS
    REM, RWI = T, T + TO

    NU = D // (P * UK)
    NMG = D // GC
    NCH = FF // D
    assert NU == RING and NU % 2 == 0
    UCV, UH = 2 * NU, 6 * NU
    U_HEAD = UCV * H
    U_MERGE = U_HEAD + UH * H
    U_WO = U_MERGE + 3 * NU * NMG
    U_FF = U_WO + NU * NMG
    UCH = 2 * NU * NMG
    G_C = 5
    ORDER = [0] * NU + [1] * NU + [2] * NU + [G_C, 3, G_C, 3, G_C, G_C, 3, 3] + [4] * NU
    PART = [ORDER[:p].count(g) for p, g in enumerate(ORDER)]
    TZ0 = T0 - (TAPS - 1)
    TZ, ZP = T - TZ0, TP - TZ0
    GH = 5
    G_HEAD = 2 * H
    G_MERGE = G_HEAD + GH * H
    G_WO = G_MERGE + 4 * NMG
    G_FF = G_WO + NMG

    with ExitStack() as ctx:
        def sem(name):
            return ctx.enter_context(nc.semaphore(name))

        def tile(stack, name, shape, dt=F32):
            return stack.enter_context(nc.sbuf_tensor(name, shape, dt))

        raw = tile(ctx, "raw", [P, RING, UK, GC])
        wh = tile(ctx, "w_high", [P, RING, UK, GC], F32R)
        wl = tile(ctx, "w_low", [P, RING, UK, GC], F32R)
        xT = tile(ctx, "x_T", [P, KB, T])
        xh = tile(ctx, "x_high", [P, KB, T], F32R)
        xl = tile(ctx, "x_low", [P, KB, T], F32R)
        ident = tile(ctx, "ident", [P, P])
        ones = tile(ctx, "ones", [P, P])
        rbc = tile(ctx, "r_bc", [P, T])
        biasT = tile(ctx, "bias_T", [P, NB1 + NB2])
        vecT = tile(ctx, "vec_T", [P, 3 * KB + TAPS * CW // P])
        VG, VF, VL, VC = 0, KB, 2 * KB, 3 * KB
        tmp = tile(ctx, "tmp", [P, GB, T])
        spart = tile(ctx, "sum_sq_halves", [P, 2, 3])
        ssum = tile(ctx, "mean_sq_cols", [P, 3])
        rcol = tile(ctx, "r_cols", [P, 3])
        rtmp = tile(ctx, "r_tmp", [P, 3])
        zlast = tile(ctx, "z_last", [P, CW // P, (TAPS - 1) * (1 + NB)])
        sqacc = tile(ctx, "sq_acc", [P, GB, TO])

        heads = ExitStack()
        yb = tile(heads, "y_b", [P, CW // P, TO])
        mask = tile(heads, "mask", [P, TP])
        smask = tile(heads, "sample_mask", [TS, NB, DS])
        onehot = tile(heads, "onehot", [2 * TS, NB], F32R)
        fold = tile(heads, "fold", [2 * TS, TS])
        acol = tile(heads, "a_cols", [P, 4, H])
        wkcol = tile(heads, "wk_cols", [P, 4, H])
        deccol = tile(heads, "decay_cols", [NB, H])
        stT = tile(heads, "conv_state_T", [P, CW // P, NB, TAPS - 1])
        nT = tile(heads, "n_T", [P, GB, NB, H])
        rsplit = tile(heads, "rows_split", [32 + H, RW], F32R)
        pick = tile(heads, "pick_head", [32 + H, H])
        chosen = tile(heads, "chosen_head", [32 + H, P], F32R)
        mrw = tile(heads, "m_row", [H, T])
        with ExitStack() as st:
            xtok = tile(st, "x_tok", [P, 3, D])
            rows = tile(st, "rows", [H, RW])
            gw = tile(st, "gate_w", [P, KB, 32])
            gws = tile(st, "gate_w_split", [P, KB, P], F32R)
            keep = tile(st, "keep_row", [H, T])
            fall = tile(st, "reset_row", [H, T])
            igr = tile(st, "ig_row", [H, T])
            fgr = tile(st, "fg_row", [H, T])
            seqs = tile(st, "sequence_of", [2 * TS, 2, NB])
            e1r = tile(st, "e1_row", [H, T])
            brw = tile(st, "b_row", [H, T])
            arw = tile(st, "a_row", [H, T])
            a1r = tile(st, "a1_row", [H, T])
            wkr = tile(st, "wk_row", [H, T + TS])
            wir = tile(st, "wint_row", [H, NB, DS])
            decr = tile(st, "decay_row", [H, NB])
            bi = tile(st, "ig_bias", [H, 1])
            bf = tile(st, "fg_bias", [H, 1])
            m0 = tile(st, "m0_row", [H, NB])
            brows = tile(st, "bias_rows", [NB1 + NB2, P])
            vrows = tile(st, "vec_rows", [3 * KB + TAPS * CW // P, P])
            crows = tile(st, "conv_rows", [NB * (TAPS - 1), CW])
            nrows = tile(st, "n_rows", [NB * H, DK])
            rdiag = tile(st, "r_diag", [P, 3, P])
        with ExitStack() as st:
            zu = tile(st, "zu", [P, GB, TZ])
            zp = tile(st, "z_prompt", [P, GB, ZP])
            zs = tile(st, "z_sample", [P, GB, NB, DS + TAPS - 1])
        QS = P + DS
        with ExitStack() as st:
            kwm = tile(st, "kw_masked", [2 * TS, NB // 2, DK], F32R)
            kw = tile(st, "kw_tok", [P, 3, DK])
            kws = tile(st, "kw_sample", [2 * TS, DK], F32R)
            vt = tile(st, "v_tok", [P, 4, DV + 1])
            vsh = tile(st, "v_sample_high", [2 * TS, DV], F32R)
            vsl = tile(st, "v_sample_low", [TS, DV], F32R)
            E = tile(st, "key_weights", [P, SW])
            bc = tile(st, "rows_bc", [P, RW])
            den = tile(st, "den", [P, TO])
            qw = tile(st, "q_inter", [P, GB, NB, DS])
            qn = tile(st, "q_n", [P, GB, NB, DS])
            qm = tile(st, "q_masked", [P, GB, NB * QS], F32R)
            cq = tile(st, "C_q", [P, DV])
            qT = tile(st, "q_T", [P, GB, T])
            kT = tile(st, "k_T", [P, GB, T + TS])
            hT = tile(st, "h_T", [P, GB, TO])
            cpo = tile(st, "C_prompt_out", [P, GB, DV + 1])
            nin = tile(st, "n_in", [NB, DK])
            nso = tile(st, "n_sample_out", [NB, DK])
            tile(st, "gap", [P, GAP])
            Cs = tile(st, "C_state", [P, NB, GB, DV])
            ha = tile(st, "h_a", [P, MW // P, TO])
        heads.close()
        with ExitStack() as st:
            mgh = tile(st, "merged_high", [P, KB, TO], F32R)
            hah = tile(st, "h_a_high", [P, MW // P, TO], F32R)
            hal = tile(st, "h_a_low", [P, MW // P, TO], F32R)
            ybh = tile(st, "y_b_high", [P, CW // P, TO], F32R)
            ybl = tile(st, "y_b_low", [P, CW // P, TO], F32R)
            mgl = tile(st, "merged_low", [P, KB, TO], F32R)
            clast = tile(st, "conv_last", [(TAPS - 1) * (1 + NB), CW])
        sga, sgb = tmp[:, :, 0:TO], sqacc[:]
        with ExitStack() as st:
            uh = tile(st, "u_high", [P, KB, TO], F32R)
            ul = tile(st, "u_low", [P, KB, TO], F32R)
            yo = tile(st, "y_out", [P, 3, D])
            gfb = tile(st, "g_final_bc", [P, D])
            ur = tile(st, "u_relu", [P, GB, TO])
            uq = tile(st, "u_squared", [P, GB, TO])

        ps = ctx.enter_context(nc.psum_tensor("ps", [P, 8, 512], F32))
        ACC = [ps[:, 0:2, :], ps[:, 2:4, :], ps[:, 6:8, :]]
        M = [ps[:, 4 + n, :] for n in range(4)]
        HEAD_ACC = [0, 1, 0, 1, 2]
        XBANKS = [ACC[1], ACC[2]]
        YPARTS = [(0, 0), (0, 1), (0, 2), (1, 0), (1, 1), (0, 3), (1, 2), (1, 3), (2, 0), (2, 1), (2, 2), (2, 3)]
        YBANK = [5, 6, 7, 0, 1, 2, 3]
        squares = yb[:].rearrange("p k t -> p (k t)")

        landed = [sem(f"raw_landed{s}") for s in range(RING)]
        high_done = sem("high_done")
        low_done = sem("low_done")
        unit_used = sem("unit_used")
        evacuated = sem("evacuated")
        biased = sem("biased")
        s_const = sem("const_built")
        s_vrows = sem("vec_rows_in")
        s_brows = sem("bias_rows_in")
        s_xtok = [sem(f"x_tok_in{n}") for n in range(6)]
        s_gw = sem("gate_w_in")
        s_small = sem("small_in")
        s_colT = sem("cols_transposed")
        s_col = sem("cols_ready")
        s_xtr = sem("x_transposed")
        s_xT = sem("x_T_ready")
        s_xh = sem("x_high_ready")
        s_xl = sem("x_low_ready")
        s_sq = sem("sum_sq_ready")
        s_ms = sem("mean_sq_ready")
        s_rt = sem("root_ready")
        s_rc = sem("r_col_ready")
        s_rd = sem("r_diag_ready")
        s_rm = sem("r_bc_product")
        s_r = sem("r_bc_ready")
        s_gz = sem("gate_w_zeroed")
        s_ghl = sem("gate_w_split")
        s_gp = sem("gate_product")
        s_row = sem("row_step")
        s_rowa = sem("row_step_act")
        s_rowT = sem("rows_transposed")
        s_rowc = sem("row_cols_ready")
        s_rsp = sem("rows_split_ready")
        s_pick = sem("pick_ready")
        s_chosen = sem("chosen_head_ready")
        s_bcp = sem("rows_bc_product")
        s_bc = sem("rows_bc_ready")
        s_x = sem("exponent_ready")
        s_e = sem("key_weights_ready")
        s_qw = sem("q_inter_ready")
        s_qn = sem("q_n_ready")
        s_ktr = sem("k_transposed")
        s_kw = sem("kw_ready")
        s_kwm = sem("kw_masked_ready")
        s_sc = sem("score_product")
        s_s = sem("scores_ready")
        s_vtr = sem("v_transposed")
        s_vt = sem("v_tok_ready")
        s_num = sem("num_den_product")
        s_abs = sem("abs_den_ready")
        s_den = sem("den_steps")
        s_h = sem("h_ready")
        s_np = sem("n_product")
        s_cpp = sem("C_prompt_product")
        s_cpo = sem("C_prompt_ready")
        s_nso = sem("n_sample_ready")
        s_cup = sem("C_update_product")
        s_cst = sem("C_state_new")
        s_Cin = sem("C_state_in")
        s_nin = sem("n_in")
        s_out = sem("small_states_stored")
        s_outC = sem("C_sample_stored")
        s_zu = sem("zu_ready")
        s_zc = sem("zc_ready")
        s_z = sem("z_ready")
        s_qmh = sem("q_masked_high")
        s_qml = sem("q_masked_low")
        s_qmz = sem("q_masked_zeroed")
        s_kwl = sem("kw_low_ready")
        s_vsl = sem("v_low_ready")
        s_cqp = sem("C_q_product")
        s_cq = sem("C_q_ready")
        s_set = sem("columns_set")
        s_cv = sem("conv_step")
        s_yb = sem("y_b_ready")
        s_ha = sem("h_a_ready")
        s_hyh = sem("h_y_high")
        s_hyl = sem("h_y_low")
        s_clt = sem("conv_last_transposed")
        s_clo = sem("conv_last_ready")
        s_mout = sem("m_stored")
        s_cout = sem("conv_stored")
        s_sga = sem("gate_a_ready")
        s_sgb = sem("gate_b_ready")
        s_mgs = sem("merged_step")
        s_mgh = sem("merged_high_ready")
        s_mgl = sem("merged_low_ready")
        s_x1h = sem("x1_high_ready")
        s_x1q = sem("x1_sq_ready")
        s_x1l = sem("x1_low_ready")
        s_acc = sem("sq_acc_step")
        s_r2p = sem("r2_product")
        s_r2 = sem("r2_step")
        s_r2a = sem("r2_root")
        s_uq = sem("u_sq_ready")
        s_uh = sem("u_high_ready")
        s_ul = sem("u_low_ready")
        s_x2q = sem("x2_sq_ready")
        s_ac2 = sem("sq_acc2_step")
        s_r3p = sem("r3_product")
        s_r3 = sem("r3_step")
        s_r3a = sem("r3_root")
        s_tab = sem("root_table_loaded")
        s_yt = sem("y_transposed")
        s_y = sem("y_ready")
        s_yout = sem("y_stored")
        s_gfb = sem("g_final_in")

        def cut(w):
            return w[0].rearrange("(u k p) n -> p u k n", k=UK, p=P)

        win, wpa, wpb, wwo, wup, wdn = (cut(w) for w in (w_in, p_a, p_b, w_o, w_up, w_down))

        block = ctx.enter_context(nc.Block())

        def q_blocks(col):
            return qm[:].rearrange("p g (b c) -> p g b c", c=QS)[:, :, :, col:col + DS]

        @block.sync
        def _(sp):
            def tokens(half):
                c = slice(D // 2 * half, D // 2 * half + D // 2)
                in0, in1, in2 = s_xtok[3 * half:3 * half + 3]
                sp.dma_start(xtok[0:NMETA, 0, c], meta[:, c]).then_inc(in0, 16)
                sp.dma_start(xtok[NMETA:P, 0, c], x_prompt[0, 0:P - NMETA, c]).then_inc(in0, 16)
                sp.dma_start(xtok[:, 1, c], x_prompt[0, P - NMETA:2 * P - NMETA, c]).then_inc(in1, 16)
                sp.dma_start(xtok[0:NMETA, 2, c], x_prompt[0, SEQ - NMETA:SEQ, c]).then_inc(in2, 16)
                sp.dma_start(xtok[NMETA:NMETA + TS, 2, c],
                             x_sample.rearrange("b t d -> (b t) d")[:, c]).then_inc(in2, 16)

            def stream(base, s, w, part, col):
                sp.wait_ge(low_done, base + s + 1)
                sp.dma_start(raw[:, s % RING:s % RING + 1], w[:, ds(part, 1), :, ds(col, GC)]) \
                  .then_inc(landed[s % RING], 16)

            def convolution(i, extra=()):
                for g, col in enumerate((CU, CC)):
                    for u in range(NU):
                        if NU * g + u in extra:
                            extra[NU * g + u]()
                        stream(UCV * i, NU * g + u, win, u, col + GC * i)

            def small():
                sp.dma_start(brows[0:NB1, :], b_in[0, 0:CG].rearrange("(k p) -> k p", p=P)).then_inc(s_brows, 16)
                sp.dma_start(brows[NB1:, :], b_in[0, CO:].rearrange("(k p) -> k p", p=P)).then_inc(s_brows, 16)
                sp.dma_start(crows[:], state_conv[0].rearrange("b r c -> (b r) c")).then_inc(s_brows, 16)
                sp.dma_start(nrows[:], state_n[0].rearrange("b h d -> (b h) d")).then_inc(s_brows, 16)

            def gates():
                sp.dma_start(gw[:], w_in[0, :, CG:CG + 32].rearrange("(k p) n -> p k n", p=P)).then_inc(s_gw, 16)
                with nc.allow_non_contiguous_dma(reason="40 numbers"):
                    sp.dma_start(bi[:], b_in[0, CG:CG + H].rearrange("(h o) -> h o", o=1)).then_inc(s_small, 16)
                    sp.dma_start(bf[:], b_in[0, CG + H:CO].rearrange("(h o) -> h o", o=1)).then_inc(s_small, 16)
                    sp.dma_start(m0[:], state_m[0].rearrange("b h -> h b")).then_inc(s_small, 16)

            tokens(0)
            convolution(0, {1: lambda: tokens(1), 3: small, 4: gates})
            with sp.Fori(1, H) as i:
                convolution(i)
            with sp.Fori(0, H) as h:
                for p, (g, u) in enumerate(zip(ORDER, PART)):
                    if g != G_C:
                        stream(U_HEAD + UH * h, p, win, u, (CQ, CK, CV, CB, CO)[g] + GC * h)
                    else:
                        b0, d = NB // 2 * (u // GB), u % GB
                        sp.wait_ge(low_done, U_HEAD + UH * h + p + 1)
                        sp.dma_start(raw[:, p % RING], state_C[0, b0:b0 + NB // 2, ds(h, 1), P * d:P * d + P, :]
                                     .rearrange("b o p e -> p (b o) e")).then_inc(landed[p % RING], 16)
                    if p == 2 * NU:
                        sp.wait_ge(s_nso, 1 + h)
                        sp.dma_start(nin[:], state_n[0, :, ds(h, 1), :].rearrange("b o d -> b (o d)")) \
                            .then_inc(s_nin, 16)
                    if 2 * NU <= p < 3 * NU:
                        b0, d = NB // 2 * (u // GB), u % GB
                        if u == 0:
                            sp.wait_ge(s_rowc, 1)
                            sp.wait_ge(s_outC, 16 + 32 * h)
                        sp.dma_start(Cs[:, b0:b0 + NB // 2, d, :],
                                     state_C[0, b0:b0 + NB // 2, ds(h, 1), P * d:P * d + P, :]
                                     .rearrange("b o p e -> p (b o) e")).then_inc(s_Cin, 16)
            with sp.Fori(1, NMG + 1) as j1:
                first = U_MERGE - 3 * NU + 3 * NU * j1
                for g, col in enumerate((CGA, CGB)):
                    for u in range(NU):
                        stream(first, 4 * g + u, win, u, GC * j1 + (col - GC))
                for g, w in enumerate((wpa, wpb)):
                    for u in range(MW // (P * UK)):
                        stream(first, 8 + 2 * g + u, w, u, GC * j1 + (-GC))
            with sp.Fori(0, NMG) as j:
                for u in range(NU):
                    stream(U_WO + 4 * j, u, wwo, u, GC * j)
            with sp.Fori(0, NCH) as c:
                with sp.Fori(0, NMG) as j:
                    for u in range(NU):
                        stream(U_FF + UCH * c + 4 * j, u, wup, u, D * c + GC * j)
                with sp.Fori(0, NMG) as j:
                    for u in range(NU):
                        stream(U_FF + UCH * c + 4 * NMG + 4 * j, u, wdn, NU * c + u, GC * j)
            for i, (n, q) in enumerate(YPARTS):
                c = slice(512 * q, 512 * q + 512)
                dst = y_prompt[0, P * n:P * n + P, c] if n < 2 else y_sample.rearrange("b t d -> (b t) d")[:, c]
                sp.wait_ge(s_y, i + 1)
                sp.dma_start(dst, yo[0:P if n < 2 else TS, n, c]).then_inc(s_yout, 16)
            sp.wait_ge(s_yout, 16 * len(YPARTS))
            sp.wait_ge(s_out, 16 + 48 * H)
            sp.wait_ge(s_outC, 16 + 32 * H)
            sp.wait_ge(s_mout, 32)
            sp.wait_ge(s_cout, 32)

        @block.gpsimd
        def _(pool):
            g = nc.gpsimd
            def const(ins):
                ins.then_inc(s_const, 1)

            const(g.memset(ident[:], 0.0))
            pool.wait_ge(s_const, 1)
            const(g.affine_select(out=ident[:], in_=ident[:], compare_op=ALU.not_equal, fill=1.0, base=0,
                                  pattern=[[1, P]], channel_multiplier=-1))
            const(g.memset(ones[:], 1.0))
            g.memset(gws[:].bitcast(F32), 0.0).then_inc(s_gz, 1)
            const(g.memset(mask[:], 0.0))
            const(g.memset(smask[:], 0.0))
            const(g.memset(seqs[:], 1.0))
            const(g.memset(keep[:], 1.0))
            const(g.memset(fall[:], 0.0))
            pool.wait_ge(s_const, 8)
            const(g.affine_select(out=mask[:], in_=mask[:], compare_op=ALU.is_ge, fill=BIG, base=0,
                                  pattern=[[1, TP]], channel_multiplier=-1))
            const(g.affine_select(out=smask[:], in_=smask[:], compare_op=ALU.is_ge, fill=BIG, base=0,
                                  pattern=[[DS, NB], [1, DS]], channel_multiplier=-1))
            const(g.affine_select(out=seqs[:], in_=seqs[:], compare_op=ALU.is_ge, fill=0.0, base=0,
                                  pattern=[[-TS, 2], [-DS, NB]], channel_multiplier=1))
            const(g.memset(keep[:, 0:1], 0.0))
            const(g.memset(keep[:, TP:T:DS], 0.0))
            const(g.memset(fall[:, 0:1], -FAR))
            const(g.memset(fall[:, TP:T:DS], -FAR))
            pool.wait_ge(s_const, 15)
            const(g.affine_select(out=smask[:], in_=smask[:], compare_op=ALU.is_ge, fill=BIG, base=0,
                                  pattern=[[-DS, NB], [0, DS]], channel_multiplier=1))
            const(g.affine_select(out=seqs[:], in_=seqs[:], compare_op=ALU.is_ge, fill=0.0, base=DS - 1,
                                  pattern=[[TS, 2], [DS, NB]], channel_multiplier=-1))
            const(g.tensor_tensor(fold[:], ident[:, 0:TS], ident[:, TS:2 * TS], ALU.add))
            pool.wait_ge(s_const, 17)
            const(g.tensor_tensor(onehot[:], seqs[:, 0], seqs[:, 1], ALU.add))
            g.memset(pick[:], 0.0).then_inc(s_pick, 1)
            g.memset(rsplit[:].bitcast(F32), 0.0).then_inc(s_pick, 1)
            for n in range(2):
                pool.wait_ge(s_pick, n + 2)
                g.affine_select(out=pick[:], in_=pick[:], compare_op=ALU.not_equal, fill=1.0, base=-32 * n,
                                pattern=[[-1, H]], channel_multiplier=1).then_inc(s_pick, 1)
            pool.wait_ge(s_row, 9)
            with nc.allow_non_contiguous_dma(reason="36 stabilisers"):
                pool.dma_start(m_prompt.rearrange("l b h -> h (l b)"), mrw[:, TP - 1:TP]).then_inc(s_mout, 16)
                pool.dma_start(m_sample.rearrange("l b h -> h (l b)"), mrw[:, TP + DS - 1:T:DS]) \
                    .then_inc(s_mout, 16)
            pool.wait_ge(s_rowc, 1)
            pool.wait_ge(s_rsp, 2)
            g.memset(vt[:, :, DV:DV + 1], 1.0).then_inc(s_qmz, 1)
            g.memset(qm[:].bitcast(F32), 0.0).then_inc(s_qmz, 1)
            with pool.Fori(0, H) as h:
                pool.wait_ge(s_kwl, h + 1)
                pool.wait_ge(s_cup, 1 + 8 * h)
                for b in range(NB):
                    if b >= NB // 2:
                        pool.wait_ge(s_cup, 1 + 8 * h + b - NB // 2 + 1)
                    own = onehot[:, b:b + 1].bitcast(F32).to_broadcast([2 * TS, DK])
                    g.tensor_tensor(kwm[:, b % 4, :], kws[:].bitcast(F32), own, ALU.mult).then_inc(s_kwm, 1)
            pool.wait_ge(s_clo, 1)
            pool.dma_start(conv_prompt[0, 0], clast[0:TAPS - 1, :]).then_inc(s_cout, 16)
            pool.dma_start(conv_sample[0].rearrange("b r c -> (b r) c"),
                           clast[TAPS - 1:, :]).then_inc(s_cout, 16)
            pool.wait_ge(evacuated, 2 + G_FF)
            pool.dma_start(gfb[:], g_final.partition_broadcast(P)).then_inc(s_gfb, 16)

        @block.scalar
        def _(act):
            a = nc.scalar
            act.sem_inc(s_mgh, 1)
            act.sem_inc(s_uh, 1)
            act.sem_inc(s_out, 16)
            act.sem_inc(s_outC, 16)
            act.dma_start(vrows[0:KB, :], g_mix.rearrange("l (k p) -> (l k) p", p=P)).then_inc(s_vrows, 16)
            act.dma_start(vrows[KB:2 * KB, :], g_ffn.rearrange("l (k p) -> (l k) p", p=P)).then_inc(s_vrows, 16)
            act.dma_start(vrows[2 * KB:3 * KB, :], g_final.rearrange("(k p) -> k p", p=P)).then_inc(s_vrows, 16)
            act.dma_start(vrows[3 * KB:, :], w_conv.rearrange("l r (k p) -> (l r k) p", p=P)).then_inc(s_vrows, 16)
            def split(base, s):
                act.wait_ge(landed[s % RING], 4 * base + 16 * (s // RING) + 16)
                act.wait_ge(unit_used, base + s + 1)
                a.activation(wh[:, s % RING], raw[:, s % RING], ACT.Copy).then_inc(high_done, 1)

            def sum_squares(half, n):
                nt, done = (P, P, NMETA + TS)[n], 3 * half + n
                act.wait_ge(s_xtok[done], 16 if n == 1 else 32)
                if done > 0:
                    act.wait_ge(s_sq, done)
                a.activation(squares[0:nt, 0:D // 2], xtok[0:nt, n, D // 2 * half:D // 2 * half + D // 2], ACT.Square,
                             accum_out=spart[0:nt, half, n:n + 1]).then_inc(s_sq, 1)

            act.wait_ge(s_set, 1)
            for n in range(2):
                sum_squares(0, n)
            act.wait_ge(s_col, 1)
            for k in range(KB):
                act.wait_ge(s_xtr, k // 2 + 1)
                a.activation(xh[:, k, :], XBANKS[k // 2 % 2][:, k % 2, 0:T], ACT.Copy,
                             scale=vecT[:, VG + k:VG + k + 1]).then_inc(s_xh, 1)
                if k % 4 == 3 and k // 4 < LEAD:
                    split(0, k // 4)
                    if k < 4:
                        sum_squares(0, 2)
                    sum_squares(1, k // 4)

            def root():
                act.wait_ge(s_ms, 2)
                a.activation(rcol[:], ssum[:], ACT.Sqrt).then_inc(s_rt, 1)

            def gate_weights():
                act.wait_ge(s_gw, 16)
                act.wait_ge(s_gz, 1)
                a.activation(gws[:, :, 0:H], gw[:, :, 0:H], ACT.Copy).then_inc(s_ghl, 1)
                a.activation(gws[:, :, 32:32 + H], gw[:, :, H:2 * H], ACT.Copy).then_inc(s_ghl, 1)

            def convolution(i, extra=()):
                for p in range(UCV):
                    split(UCV * i, p + LEAD)
                    if p in extra:
                        extra[p]()
                    if p == 3:
                        act.wait_ge(evacuated, 2 + 2 * i + 1)
                        for b in range(GB):
                            ins = a.activation(zu[:, b, :], tmp[:, b, 0:TZ], ACT.Identity,
                                               bias=biasT[:, ds(BU + GB * i + b, 1)])
                        ins.then_inc(s_zu, 1)
                    if p == 7:
                        act.wait_ge(evacuated, 2 + 2 * i + 2)
                        for b in range(GB):
                            ins = a.activation(tmp[:, b, 0:TZ], tmp[:, b, 0:TZ], ACT.Identity,
                                               bias=biasT[:, ds(BC_ + GB * i + b, 1)])
                        ins.then_inc(s_zc, 1)

            def log1p_exp():
                act.wait_ge(s_row, 2)
                a.activation(e1r[:], fgr[:], ACT.Abs).then_inc(s_rowa, 1)
                act.wait_ge(s_rowa, 1)
                a.activation(e1r[:], e1r[:], ACT.Exp, scale=-1.0).then_inc(s_rowa, 1)
                act.wait_ge(s_rowa, 2)
                a.activation(e1r[:], e1r[:], ACT.Ln, bias=1.0).then_inc(s_rowa, 1)

            def row_exps():
                act.wait_ge(s_row, 11)
                a.activation(rows[:, REM:REM + TO], mrw[:, T0:T], ACT.Exp, scale=-1.0).then_inc(s_rowa, 1)
                a.activation(rows[:, RWI:RWI + TS].rearrange("p (b t) -> p b t", t=DS), wir[:],
                             ACT.Exp).then_inc(s_rowa, 1)
                a.activation(wkr[:], wkr[:], ACT.Exp).then_inc(s_rowa, 1)

            convolution(0, {1: root, 2: gate_weights, 3: lambda: act.wait_ge(s_col, 2)})
            with act.Fori(1, H - 1) as i:
                convolution(i)
            convolution(H - 1, {1: log1p_exp, 4: row_exps})

            act.wait_ge(s_pick, 2)
            act.wait_ge(s_row, 12)
            a.activation(rsplit[0:H, :], rows[:], ACT.Copy).then_inc(s_rsp, 1)

            with act.Fori(0, H) as h:
                def add_bias(g, out, col, func=ACT.Identity):
                    act.wait_ge(evacuated, 2 + G_HEAD + GH * h + g + 1)
                    n = min(out.shape[2], T)
                    for b in range(GB):
                        ins = a.activation(out[:, b, 0:n], tmp[:, b, 0:n], func,
                                           bias=biasT[:, ds(col + GB * h + b, 1)])
                        if out.shape[2] > T:
                            ins = a.activation(out[:, b, T:], tmp[:, b, TP:T], func,
                                               bias=biasT[:, ds(col + GB * h + b, 1)])
                    ins.then_inc(biased, 1)

                for p in range(UH):
                    split(U_HEAD + UH * h, p + LEAD)
                    if p == 2:
                        act.wait_ge(s_bcp, 1 + h + 1)
                        act.wait_ge(s_cst, 1 + 8 * h)
                        act.wait_ge(s_den, 1 + 2 * h)
                        a.activation(bc[:], ps[:, 4:6, :].rearrange("p b n -> p (b n)")[:, 0:RW],
                                     ACT.Copy).then_inc(s_bc, 1)
                    if p == 3:
                        add_bias(0, qT[:, :, T0:T], BQ)
                    if p == 5:
                        act.wait_ge(s_x, h + 1)
                        for n, ((k0, nk), (q0, nq, off)) in enumerate(zip(KT, QT)):
                            ins = a.activation(E[0:nk, off:off + nq], E[0:nk, off:off + nq], ACT.Exp, scale=-1.0,
                                               bias=acol[0:nk, n, ds(h, 1)])
                        ins.then_inc(s_e, 1)
                        act.wait_ge(s_qw, h + 1)
                        act.wait_ge(s_qmz, 2)
                        act.wait_ge(s_cqp, 1 + h)
                        a.activation(q_blocks(0), qw[:], ACT.Copy).then_inc(s_qmh, 1)
                    if p == 7:
                        add_bias(1, kT, BK)
                    if p == 9:
                        act.wait_ge(s_ktr, h + 1)
                        act.wait_ge(s_cup, 1 + 8 * h)
                        for n, (k0, nk) in enumerate(KT[0:3]):
                            a.activation(kw[0:nk, n, :], M[n // 2][0:nk, (n % 2) * DK:(n % 2 + 1) * DK],
                                         ACT.Copy, scale=wkcol[0:nk, n, ds(h, 1)])
                        a.activation(kws[:], M[1][:, DK:2 * DK], ACT.Copy,
                                     scale=wkcol[:, 3, ds(h, 1)]).then_inc(s_kw, 1)
                    if p == 11:
                        act.wait_ge(s_sc, h + 1)
                        add_bias(2, kT, BV)
                    if p == 13:
                        act.wait_ge(s_vtr, h + 1)
                        for n, (k0, nk) in enumerate(KT):
                            a.activation(vt[0:nk, n, 0:DV], M[n // 2][0:nk, (n % 2) * DV:(n % 2 + 1) * DV], ACT.Copy)
                        a.activation(vsh[:], M[1][:, DV:2 * DV], ACT.Copy).then_inc(s_vt, 1)
                    if p == 17:
                        act.wait_ge(s_cqp, 1 + h + 1)
                        act.wait_ge(s_num, 1 + h)
                        a.activation(cq[:], M[2][:, 0:DV], ACT.Copy).then_inc(s_cq, 1)
                    if p == 18:
                        act.wait_ge(s_num, 1 + h + 1)
                        a.activation(den[:], M[3][:, 0:TO], ACT.Abs).then_inc(s_abs, 1)
                        act.wait_ge(s_cpp, h + 1)
                        act.wait_ge(s_out, 16 + 48 * h)
                        a.activation(cpo[:], ps[:, 6:8, 0:DV + 1], ACT.Copy).then_inc(s_cpo, 1)
                    if p == 19:
                        add_bias(3, tmp[:, :, 0:TO], BB)
                    if p == 20:
                        act.wait_ge(s_cpo, h + 1)
                        act.dma_start(C_prompt[0, :, ds(h, 1), :, :]
                                      .rearrange("b o (g p) e -> p (b o g) e", p=P), cpo[:, :, 0:DV]).then_inc(s_out, 16)
                        with nc.allow_non_contiguous_dma(reason="a column"):
                            act.dma_start(n_prompt[0, :, ds(h, 1), :].rearrange("b o (g p) -> p (b o) g", p=P),
                                          cpo[:, :, DV:DV + 1].rearrange("p g o -> p o g")).then_inc(s_out, 16)
                        act.wait_ge(s_nso, 1 + h + 1)
                        act.dma_start(n_sample[0, :, ds(h, 1), :].rearrange("b o d -> b (o d)"), nso[:]) \
                            .then_inc(s_out, 16)
                    if p == 23:
                        act.wait_ge(s_cst, 1 + 8 * h + 8)
                        for d in range(GB):
                            act.dma_start(C_sample[0, :, ds(h, 1), P * d:P * d + P, :]
                                          .rearrange("b o p e -> p (b o) e"), Cs[:, :, d, :]).then_inc(s_outC, 16)
                        add_bias(4, tmp[:, :, 0:TO], BO, ACT.Sigmoid)

            def high(k):
                if k == 0:
                    act.wait_ge(s_ha, 1 + H)
                    act.wait_ge(s_out, 16 + 48 * H)
                    act.wait_ge(s_cst, 1 + 8 * H)
                    act.wait_ge(s_mout, 32)
                    act.wait_ge(s_yb, 1 + H)
                a.activation(hah[:, 2 * k:2 * k + 2, :], ha[:, 2 * k:2 * k + 2, :], ACT.Copy).then_inc(s_hyh, 1)
                a.activation(ybh[:, 2 * k:2 * k + 2, :], yb[:, 2 * k:2 * k + 2, :], ACT.Copy).then_inc(s_hyh, 1)

            def last_rows():
                act.wait_ge(s_clt, 1)
                act.wait_ge(s_hyl, 8)
                a.activation(clast[:], ps[0:clast.shape[0], 4:6, :].rearrange("p b n -> p (b n)"), ACT.Copy) \
                    .then_inc(s_clo, 1)

            def merge(j, extra=()):
                for p in range(12):
                    split(U_MERGE + 3 * NU * j, p + LEAD)
                    if p in extra:
                        extra[p]()
                    for pos, g, gate, done, col in ((3, 0, sga, s_sga, BGA), (7, 1, sgb, s_sgb, BGB)):
                        if p == pos:
                            act.wait_ge(evacuated, 2 + G_MERGE + 4 * j + g + 1)
                            for b in range(GB):
                                ins = a.activation(gate[:, b, :], gate[:, b, :], ACT.Sigmoid,
                                                   bias=biasT[:, ds(col + GB * j + b, 1)])
                            ins.then_inc(done, 1)
                    if p == 11:
                        act.wait_ge(s_mgs, 1 + 2 * j + 2)
                        act.wait_ge(s_outC, 16 + 32 * H)
                        act.wait_ge(s_cout, 32)
                        a.activation(mgh[:, ds(GB * j, GB), :], sga, ACT.Copy).then_inc(s_mgh, 1)

            assert CW // P == 8 and MW == CW
            merge(0, {0: lambda: high(0), 1: lambda: high(1), 2: lambda: high(2), 4: lambda: high(3), 6: last_rows})
            with act.Fori(1, NMG) as j:
                merge(j)

            with act.Fori(0, NMG // 2) as jj:
                for pair in range(2):
                    j = 2 * jj + pair
                    for p in range(NU):
                        split(U_WO + 8 * jj, 4 * pair + p + LEAD)
                    act.wait_ge(evacuated, 2 + G_WO + j + 1)
                    act.wait_ge(s_acc, j + 1)
                    a.activation(tmp[:, :, 0:TO], xT[:, ds(GB * j, GB), T0:T], ACT.Square).then_inc(s_x1q, 1)
                    for b in range(GB):
                        ins = a.activation(xh[:, ds(GB * j + b, 1), T0:T], xT[:, ds(GB * j + b, 1), T0:T], ACT.Copy,
                                           scale=vecT[:, ds(VF + GB * j + b, 1)])
                    ins.then_inc(s_x1h, 1)
            a.activation(spart[:, 0], ssum[:], ACT.Sqrt).then_inc(s_tab, 1)

            def root():
                act.wait_ge(s_r2, 2)
                a.activation(rbc[:, 0:TO], tmp[:, 0, 0:TO], ACT.Sqrt).then_inc(s_r2a, 1)

            def ffn(c, first=False, last=False):
                def up(jj, extra=()):
                    for pair in range(2):
                        j = 2 * jj + pair
                        for p in range(NU):
                            split(U_FF + UCH * c + 8 * jj, 4 * pair + p + LEAD)
                            if NU * pair + p in extra:
                                extra[NU * pair + p]()
                        act.wait_ge(s_uq, 1 + NMG * c + j + 1)
                        a.activation(uh[:, ds(GB * j, GB), :], uq[:], ACT.Copy).then_inc(s_uh, 1)

                if first:
                    up(0, {1: root})
                with act.Fori(1 if first else 0, NMG // 2) as jj:
                    up(jj)

                def down(jj, tail):
                    for pair in range(2):
                        for p in range(NU):
                            if not (tail and pair == 1 and p + LEAD >= NU):
                                split(U_FF + UCH * c + 4 * NMG + 8 * jj, 4 * pair + p + LEAD)
                        if last:
                            j = 2 * jj + pair
                            act.wait_ge(evacuated, 2 + G_FF + 2 * NMG * c + NMG + j + 1)
                            act.wait_ge(s_ac2, j + 1)
                            a.activation(tmp[:, :, 0:TO], xT[:, ds(GB * j, GB), T0:T], ACT.Square).then_inc(s_x2q, 1)

                with act.Fori(0, NMG // 2 - 1 if last else NMG // 2) as jj:
                    down(jj, False)
                if last:
                    down(NMG // 2 - 1, True)

            ffn(0, first=True)
            with act.Fori(1, NCH - 1) as c:
                ffn(c)
            ffn(NCH - 1, last=True)
            act.wait_ge(s_tab, 1)
            a.activation(spart[:, 0], ssum[:], ACT.Sqrt).then_inc(s_tab, 1)
            act.wait_ge(s_r3, 2)
            a.activation(rcol[:], ssum[:], ACT.Sqrt).then_inc(s_r3a, 1)

        @block.vector
        def _(dve):
            v = nc.vector
            dve.sem_inc(low_done, RING)
            dve.sem_inc(evacuated, 2)
            for s in (s_ha, s_s, s_cst, s_den, s_cv, s_mgl, s_mgs, s_uq, s_ul, s_nso, s_z, s_yb):
                dve.sem_inc(s, 1)
            v.memset(spart[:], 1.0).then_inc(s_set, 1)
            dve.wait_ge(s_colT, 1)
            v.tensor_copy(vecT[:], M[0][:, 0:vecT.shape[1]]).then_inc(s_col, 1)

            def split(base, s):
                dve.wait_ge(high_done, base + s + 1)
                dve.wait_ge(landed[s % RING], 4 * base + 16 * (s // RING) + 16)
                dve.wait_ge(unit_used, base + s + 1)
                v.tensor_tensor(wl[:, s % RING], raw[:, s % RING], wh[:, s % RING].bitcast(F32),
                                ALU.subtract).then_inc(low_done, 1)

            def root_step(r, x, t, seen, n):
                v.tensor_tensor(t, r, r, ALU.mult).then_inc(seen, 1)
                dve.wait_ge(seen, n + 1)
                v.tensor_tensor(t, t, x, ALU.mult).then_inc(seen, 1)
                dve.wait_ge(seen, n + 2)
                v.tensor_scalar(t, t, -0.5, 1.5, ALU.mult, ALU.add).then_inc(seen, 1)
                dve.wait_ge(seen, n + 3)
                v.tensor_tensor(r, r, t, ALU.mult).then_inc(seen, 1)
                dve.wait_ge(seen, n + 4)

            for k in range(KB):
                dve.wait_ge(s_xh, k + 1)
                v.scalar_tensor_tensor(xl[:, k, :], XBANKS[k // 2 % 2][:, k % 2, 0:T], vecT[:, VG + k:VG + k + 1],
                                       xh[:, k, :].bitcast(F32), ALU.mult, ALU.subtract).then_inc(s_xl, 1)
                if k % 2 == 1:
                    v.tensor_copy(xT[:, k - 1:k + 1, T0:T], XBANKS[k // 2 % 2][:, :, T0:T]).then_inc(s_xT, 1)
                if k % 4 == 3 and k // 4 < LEAD:
                    split(0, k // 4)

            def columns():
                dve.wait_ge(s_colT, 2)
                v.tensor_copy(biasT[:], M[0][:, 128:128 + NB1 + NB2])
                v.tensor_copy(stT[:].rearrange("p k b r -> p (k b r)"),
                              M[0][:, 256:256 + stT.shape[1] * NB * (TAPS - 1)])
                v.tensor_copy(nT[:].rearrange("p g b h -> p (g b h)"),
                              M[0][:, 384:384 + GB * NB * H]).then_inc(s_col, 1)
                dve.wait_ge(s_sq, 6)
                v.tensor_tensor(ssum[:], spart[:, 0], spart[:, 1], ALU.add).then_inc(s_ms, 1)
                dve.wait_ge(s_ms, 1)
                v.tensor_scalar(ssum[:], ssum[:], 1.0 / D, EPS, ALU.mult, ALU.add).then_inc(s_ms, 1)
                dve.wait_ge(s_ms, 2)
                dve.wait_ge(s_rt, 1)
                v.reciprocal(rcol[:], rcol[:]).then_inc(s_rc, 1)
                dve.wait_ge(s_rc, 1)
                root_step(rcol[:], ssum[:], rtmp[:], s_rc, 1)
                dve.wait_ge(s_const, 2)
                for n, m in enumerate((P, P, NMETA + TS)):
                    v.tensor_scalar(rdiag[0:m, n, 0:m], ident[0:m, 0:m], rcol[0:m, n:n + 1], None,
                                    ALU.mult).then_inc(s_rd, 1)

            def scales():
                dve.wait_ge(s_rm, 1)
                v.tensor_copy(rbc[:], M[1][:, 0:T]).then_inc(s_r, 1)
                dve.wait_ge(s_r, 1)

            def gate_weights():
                dve.wait_ge(s_gw, 16)
                dve.wait_ge(s_ghl, 2)
                v.tensor_tensor(gws[:, :, 64:64 + H], gw[:, :, 0:H], gws[:, :, 0:H].bitcast(F32),
                                ALU.subtract).then_inc(s_ghl, 1)
                v.tensor_tensor(gws[:, :, 96:96 + H], gw[:, :, H:2 * H], gws[:, :, 32:32 + H].bitcast(F32),
                                ALU.subtract).then_inc(s_ghl, 1)

            scale = rbc[:, 0:T].unsqueeze(1).to_broadcast([P, GB, T])
            scale_z = rbc[:, TZ0:T].unsqueeze(1).to_broadcast([P, GB, TZ])
            scale_o = rbc[:, T0:T].unsqueeze(1).to_broadcast([P, GB, TO])

            def convolution(i, extra=()):
                for p in range(UCV):
                    split(UCV * i, p + LEAD)
                    if p in extra:
                        extra[p]()
                    if p in (3, 7):
                        g = p // 4
                        dve.wait_ge(unit_used, RING + UCV * i + 4 * g + 4)
                        if g == 0:
                            dve.wait_ge(s_z, 1 + i)
                            dve.wait_ge(s_cv, 1 + 12 * i)
                        else:
                            dve.wait_ge(s_zu, i + 1)
                        v.tensor_tensor(tmp[:, :, 0:TZ], ACC[g][:, :, 0:TZ], scale_z, ALU.mult).then_inc(evacuated, 1)
                    if p == 7:
                        dve.wait_ge(s_zc, i + 1)
                        v.tensor_copy(zs[:, :, :, 0:TAPS - 1], stT[:, ds(GB * i, GB), :, :])
                        v.tensor_tensor(zp[:], tmp[:, :, 0:ZP], zu[:, :, 0:ZP], ALU.mult)
                        v.tensor_tensor(zs[:, :, :, TAPS - 1:], tmp[:, :, ZP:TZ].rearrange("p g (b t) -> p g b t", t=DS),
                                        zu[:, :, ZP:TZ].rearrange("p g (b t) -> p g b t", t=DS), ALU.mult) \
                            .then_inc(s_z, 1)
                        dve.wait_ge(s_z, 1 + i + 1)
                        v.tensor_copy(zlast[:, ds(GB * i, GB), 0:TAPS - 1], zp[:, :, ZP - TAPS + 1:ZP])
                        v.tensor_copy(zlast[:, ds(GB * i, GB), TAPS - 1:].rearrange("p g (b r) -> p g b r", r=TAPS - 1),
                                      zs[:, :, :, DS:DS + TAPS - 1])
                        for r in range(TAPS):
                            for b in range(GB):
                                w = vecT[:, ds(VC + r * (CW // P) + GB * i + b, 1)]
                                out_p = yb[:, ds(GB * i + b, 1), 0:SEQ]
                                out_s = yb[:, ds(GB * i + b, 1), SEQ:TO].rearrange("p o (b t) -> p (o b) t", t=DS)
                                src_p = zp[:, b:b + 1, r:r + SEQ]
                                src_s = zs[:, b, :, r:r + DS]
                                for out, src in ((out_p, src_p), (out_s, src_s)):
                                    if r == 0:
                                        v.tensor_scalar(out, src, w, None, ALU.mult).then_inc(s_cv, 1)
                                    else:
                                        v.scalar_tensor_tensor(out, src, w, out, ALU.mult, ALU.add).then_inc(s_cv, 1)
                            dve.wait_ge(s_cv, 1 + 12 * i + 4 * r + 4)

            step = [0]

            def row(ins):
                step[0] += 1
                ins.then_inc(s_row, 1)
                dve.wait_ge(s_row, step[0])

            samp = lambda r: r[:, TP:T].rearrange("p (b t) -> p b t", t=DS)
            mx = samp(rows)

            def gates():
                dve.wait_ge(s_gp, 1)
                dve.wait_ge(s_small, 48)
                for out, low, row0 in ((fgr, e1r, 32), (igr, arw, 0)):
                    v.tensor_tensor(out[:], M[3][row0:row0 + H, 0:T], rbc[row0:row0 + H, :], ALU.mult)
                    row1 = row0 + 64
                    ins = v.tensor_tensor(low[:], M[3][row1:row1 + H, 0:T], rbc[row1:row1 + H, :], ALU.mult)
                ins.then_inc(s_gz, 1)
                dve.wait_ge(s_gz, 2)
                v.scalar_tensor_tensor(fgr[:], fgr[:], bf[:, 0:1], e1r[:], ALU.add, ALU.add).then_inc(s_row, 1)
                step[0] += 1
                row(v.scalar_tensor_tensor(igr[:], igr[:], bi[:, 0:1], arw[:], ALU.add, ALU.add))

            def sums():
                dve.wait_ge(s_rowa, 3)
                row(v.scalar_tensor_tensor(fgr[:], fgr[:], 0.0, e1r[:], ALU.min, ALU.subtract))
                dve.wait_ge(s_const, 19)
                row(v.tensor_tensor_scan(brw[:], keep[:], fgr[:], 0.0, ALU.mult, ALU.add))
                row(v.tensor_tensor(arw[:], igr[:], brw[:], ALU.subtract))
                v.tensor_copy(a1r[:, 1:TP], arw[:, 1:TP])
                v.tensor_copy(samp(a1r)[:, :, 1:DS], samp(arw)[:, :, 1:DS])
                row(v.tensor_scalar(a1r[:, 0:1], arw[:, 0:1], 0.0, None, ALU.max))
                row(v.tensor_tensor(samp(a1r)[:, :, 0], samp(arw)[:, :, 0], m0[:], ALU.max))
                row(v.tensor_tensor_scan(rows[:, 0:T], fall[:], a1r[:], 0.0, ALU.add, ALU.max))

            def exponents():
                row(v.tensor_tensor(mrw[:], brw[:], rows[:, 0:T], ALU.add))
                row(v.tensor_tensor(wir[:], m0[:].unsqueeze(2).to_broadcast([H, NB, DS]), mx, ALU.subtract))
                v.tensor_scalar(wkr[:, 0:TP], arw[:, 0:TP], rows[:, TP - 1:TP], None, ALU.subtract)
                for c in (TP, T):
                    ins = v.tensor_tensor(wkr[:, c:c + TS].rearrange("p (b t) -> p b t", t=DS), samp(arw),
                                          mx[:, :, DS - 1:DS].to_broadcast([H, NB, DS]), ALU.subtract)
                row(ins)

            def decays():
                dve.wait_ge(s_rowa, 6)
                row(v.tensor_copy(decr[:], rows[:, RWI:RWI + TS].rearrange("p (b t) -> p b t", t=DS)
                                  [:, :, DS - 1]))

            convolution(0, {1: columns, 3: scales, 5: gate_weights})
            with dve.Fori(1, H - 1) as i:
                convolution(i)
            convolution(H - 1, {0: gates, 1: sums, 3: exponents, 4: decays})

            dve.wait_ge(s_rowT, 1)
            for n, (k0, nk) in enumerate(KT):
                m = 2 * nk if n == 3 else nk
                v.tensor_copy(acol[0:nk, n, :], M[0][0:nk, n * H:(n + 1) * H])
                v.tensor_scalar(wkcol[0:m, n, :], M[0][0:m, (4 + n) * H:(5 + n) * H], DK ** -0.5, None, ALU.mult)
            v.tensor_copy(deccol[:], M[0][0:NB, 8 * H:9 * H]).then_inc(s_rowc, 1)
            dve.wait_ge(s_rowc, 1)

            dve.wait_ge(s_rsp, 1)
            v.tensor_tensor(rsplit[32:32 + H, :], rows[:], rsplit[0:H, :].bitcast(F32), ALU.subtract).then_inc(s_rsp, 1)

            with dve.Fori(0, H) as h:
                def evacuate(g, pos, n):
                    dve.wait_ge(unit_used, RING + U_HEAD + UH * h + pos + 1)
                    if g > 0:
                        dve.wait_ge(biased, GH * h + g)
                    v.tensor_tensor(tmp[:, :, 0:n], ACC[HEAD_ACC[g]][:, :, 0:n], scale if n == T else scale_o,
                                    ALU.mult).then_inc(evacuated, 1)

                for p in range(UH):
                    split(U_HEAD + UH * h, p + LEAD)
                    if p == 0:
                        dve.wait_ge(s_pick, 4)
                        dve.wait_ge(s_const, 3)
                        dve.wait_ge(s_bcp, 1 + h)
                        v.tensor_scalar(chosen[:], ones[0:32 + H, :], pick[:, ds(h, 1)], None,
                                        ALU.mult).then_inc(s_chosen, 1)
                    if p == 3:
                        dve.wait_ge(s_ha, 1 + h)
                        evacuate(0, 3, TO)
                    if p == 4:
                        dve.wait_ge(s_bc, h + 1)
                        dve.wait_ge(s_num, 1 + h)
                        for n, ((k0, nk), (q0, nq, off)) in enumerate(zip(KT, QT)):
                            m = mask[0:nk, q0 - k0:q0 - k0 + nq] if n < 3 else \
                                smask[:].rearrange("p b t -> p (b t)")
                            ins = v.scalar_tensor_tensor(E[0:nk, off:off + nq], bc[0:nk, q0:q0 + nq],
                                                         acol[0:nk, n, ds(h, 1)], m, ALU.max, ALU.add)
                        ins.then_inc(s_x, 1)
                        dve.wait_ge(biased, GH * h + 1)
                        v.tensor_tensor(qw[:], qT[:, :, TP:T].rearrange("p g (b t) -> p g b t", t=DS),
                                        bc[:, RWI:RWI + TS].rearrange("p (o b t) -> p o b t", o=1, t=DS)
                                        .to_broadcast([P, GB, NB, DS]), ALU.mult).then_inc(s_qw, 1)
                        dve.wait_ge(s_qw, h + 1)
                        v.tensor_tensor(qn[:], qw[:], nT[:, :, :, ds(h, 1)].to_broadcast([P, GB, NB, DS]),
                                        ALU.mult).then_inc(s_qn, 1)
                    if p == 5:
                        dve.wait_ge(s_qmh, h + 1)
                        v.tensor_tensor(q_blocks(TS), qw[:], q_blocks(0).bitcast(F32), ALU.subtract).then_inc(s_qml, 1)
                    if p == 7:
                        evacuate(1, 7, T)
                    if p == 9:
                        dve.wait_ge(s_kw, h + 1)
                        up = slice(TS, 2 * TS)
                        v.scalar_tensor_tensor(kws[up, :], M[1][up, DK:2 * DK], wkcol[up, 3, ds(h, 1)],
                                               kws[up, :].bitcast(F32), ALU.mult, ALU.subtract).then_inc(s_kwl, 1)
                    if p == 10:
                        dve.wait_ge(s_sc, h + 1)
                        dve.wait_ge(s_e, h + 1)
                        for n, ((k0, nk), (q0, nq, off)) in enumerate(zip(KT, QT)):
                            src = M[2][0:nk, off:off + nq] if n < 2 else M[3][0:nk, off - QT[2][2]:off - QT[2][2] + nq]
                            ins = v.scalar_tensor_tensor(E[0:nk, off:off + nq], src, DK ** -0.5,
                                                         E[0:nk, off:off + nq], ALU.mult, ALU.mult)
                        ins.then_inc(s_s, 1)
                    if p == 11:
                        evacuate(2, 11, T)
                    if p == 13:
                        dve.wait_ge(s_vt, h + 1)
                        v.tensor_tensor(vsl[:], M[1][0:TS, DV:2 * DV], vsh[0:TS, :].bitcast(F32),
                                        ALU.subtract).then_inc(s_vsl, 1)
                        dve.wait_ge(s_np, h + 1)
                        dve.wait_ge(s_nin, 16 * h + 16)
                        dve.wait_ge(s_out, 16 + 48 * h)
                        v.scalar_tensor_tensor(nso[:], nin[:], deccol[:, ds(h, 1)], M[3][0:NB, 0:DK],
                                               ALU.mult, ALU.add).then_inc(s_nso, 1)
                    if p == 18:
                        dve.wait_ge(s_abs, h + 1)
                        v.tensor_tensor(den[:], den[:], bc[:, REM:REM + TO], ALU.max).then_inc(s_den, 1)
                        dve.wait_ge(s_den, 1 + 2 * h + 1)
                        v.reciprocal(den[:], den[:]).then_inc(s_den, 1)
                        dve.wait_ge(s_den, 1 + 2 * h + 2)
                        v.tensor_tensor(hT[:], ps[:, 4:6, 0:TO], den[:].unsqueeze(1).to_broadcast([P, GB, TO]),
                                        ALU.mult).then_inc(s_h, 1)
                    if p == 19:
                        evacuate(3, 19, TO)
                    if 19 <= p < 23:
                        dve.wait_ge(s_Cin, 64 * h + 64)
                        for b in (2 * (p - 19), 2 * (p - 19) + 1):
                            dve.wait_ge(s_cup, 1 + 8 * h + b + 1)
                            C2 = Cs[:, b].rearrange("p g e -> p (g e)")
                            v.scalar_tensor_tensor(C2, C2, bc[:, RWI + DS * b + DS - 1:RWI + DS * b + DS], M[b % 2],
                                                   ALU.mult, ALU.add).then_inc(s_cst, 1)
                    if p == 19:
                        dve.wait_ge(biased, GH * h + 4)
                        y = yb[:, ds(GB * h, GB), :]
                        v.tensor_tensor(y, tmp[:, :, 0:TO], y, ALU.mult).then_inc(s_yb, 1)
                    if p == 23:
                        dve.wait_ge(s_yb, 1 + h + 1)
                        evacuate(4, 23, TO)
                        dve.wait_ge(biased, GH * h + 5)
                        dve.wait_ge(s_h, h + 1)
                        v.tensor_tensor(ha[:, ds(GB * h, GB), :], tmp[:, :, 0:TO], hT[:], ALU.mult).then_inc(s_ha, 1)

            def low(k):
                if k == 0:
                    dve.wait_ge(s_ha, 1 + H)
                for i, (dst, src, hi) in enumerate(((hal, ha, hah), (ybl, yb, ybh))):
                    dve.wait_ge(s_hyh, 2 * k + i + 1)
                    v.tensor_tensor(dst[:, 2 * k:2 * k + 2, :], src[:, 2 * k:2 * k + 2, :],
                                    hi[:, 2 * k:2 * k + 2, :].bitcast(F32), ALU.subtract).then_inc(s_hyl, 1)

            def merge(j, extra=()):
                def evacuate_gate(g, gate):
                    dve.wait_ge(unit_used, RING + U_MERGE + 3 * NU * j + 4 * g + 4)
                    v.tensor_tensor(gate, ACC[g][:, :, 0:TO], scale_o, ALU.mult).then_inc(evacuated, 1)

                for p in range(12):
                    split(U_MERGE + 3 * NU * j, p + LEAD)
                    if p in extra:
                        extra[p]()
                    if p == 3:
                        dve.wait_ge(s_mgh, 1 + j)
                        dve.wait_ge(s_mgl, 1 + j)
                        evacuate_gate(0, sga)
                    if p == 7:
                        dve.wait_ge(s_mgs, 1 + 2 * j)
                        evacuate_gate(1, sgb)
                    if p == 9:
                        dve.wait_ge(s_sga, j + 1)
                        dve.wait_ge(unit_used, RING + U_MERGE + 3 * NU * j + 10)
                        v.tensor_tensor(sga, ACC[0][:, :, 0:TO], sga, ALU.mult).then_inc(evacuated, 1)
                    if p == 11:
                        dve.wait_ge(s_sgb, j + 1)
                        dve.wait_ge(unit_used, RING + U_MERGE + 3 * NU * j + 12)
                        v.tensor_tensor(sgb, ACC[1][:, :, 0:TO], sgb, ALU.mult).then_inc(evacuated, 1)
                        dve.wait_ge(evacuated, 2 + G_MERGE + 4 * j + 4)
                        dve.wait_ge(s_hyl, 8)
                        v.tensor_tensor(sga, sga, sgb, ALU.add).then_inc(s_mgs, 2)
                        dve.wait_ge(s_mgh, 1 + j + 1)
                        v.tensor_tensor(mgl[:, ds(GB * j, GB), :], sga, mgh[:, ds(GB * j, GB), :].bitcast(F32),
                                        ALU.subtract).then_inc(s_mgl, 1)

            merge(0, {0: lambda: low(0), 1: lambda: low(1), 2: lambda: low(2), 4: lambda: low(3)})
            with dve.Fori(1, NMG) as j:
                merge(j)

            v.memset(sqacc[:], 0.0).then_inc(s_acc, 1)
            with dve.Fori(0, NMG // 2) as jj:
                for pair in range(2):
                    j = 2 * jj + pair
                    for p in range(NU):
                        split(U_WO + 8 * jj, 4 * pair + p + LEAD)
                    dve.wait_ge(unit_used, RING + U_WO + 8 * jj + 4 * pair + 4)
                    dve.wait_ge(s_xT, KB // 2)
                    x1 = xT[:, ds(GB * j, GB), T0:T]
                    v.tensor_tensor(x1, ACC[pair][:, :, 0:TO], x1, ALU.add).then_inc(evacuated, 1)
                    dve.wait_ge(s_x1q, j + 1)
                    dve.wait_ge(s_acc, j + 1)
                    v.tensor_tensor(sqacc[:], sqacc[:], tmp[:, :, 0:TO], ALU.add).then_inc(s_acc, 1)
                    dve.wait_ge(s_x1h, j + 1)
                    for b in range(GB):
                        ins = v.scalar_tensor_tensor(
                            xl[:, ds(GB * j + b, 1), T0:T], xT[:, ds(GB * j + b, 1), T0:T],
                            vecT[:, ds(VF + GB * j + b, 1)], xh[:, ds(GB * j + b, 1), T0:T].bitcast(F32),
                            ALU.mult, ALU.subtract)
                    ins.then_inc(s_x1l, 1)
            dve.wait_ge(s_acc, NMG + 1)
            v.tensor_tensor(sqacc[:, 0, :], sqacc[:, 0, :], sqacc[:, 1, :], ALU.add).then_inc(s_r2, 1)
            scale_u = rbc[:, 0:TO].unsqueeze(1).to_broadcast([P, GB, TO])

            def root():
                dve.wait_ge(s_r2p, 1)
                v.tensor_scalar(tmp[:, 0, 0:TO], M[0][:, 0:TO], 1.0 / D, EPS, ALU.mult, ALU.add).then_inc(s_r2, 1)
                dve.wait_ge(s_r2a, 1)
                v.reciprocal(rbc[:, 0:TO], rbc[:, 0:TO]).then_inc(s_r2, 1)
                dve.wait_ge(s_r2, 3)
                root_step(rbc[:, 0:TO], tmp[:, 0, 0:TO], tmp[:, 1, 0:TO], s_r2, 3)

            def ffn(c, first=False, last=False):
                def up(jj, extra=()):
                    for pair in range(2):
                        j = 2 * jj + pair
                        for p in range(NU):
                            split(U_FF + UCH * c + 8 * jj, 4 * pair + p + LEAD)
                            if NU * pair + p in extra:
                                extra[NU * pair + p]()
                        dve.wait_ge(unit_used, RING + U_FF + UCH * c + 8 * jj + 4 * pair + 4)
                        dve.wait_ge(s_uq, 1 + NMG * c + j)
                        v.scalar_tensor_tensor(ur[:], ACC[pair][:, :, 0:TO], 0.0, scale_u, ALU.max, ALU.mult) \
                            .then_inc(evacuated, 1)
                        dve.wait_ge(evacuated, 2 + G_FF + 2 * NMG * c + j + 1)
                        dve.wait_ge(s_uh, 1 + NMG * c + j)
                        dve.wait_ge(s_ul, 1 + NMG * c + j)
                        v.tensor_tensor(uq[:], ur[:], ur[:], ALU.mult).then_inc(s_uq, 1)
                        dve.wait_ge(s_uh, 1 + NMG * c + j + 1)
                        v.tensor_tensor(ul[:, ds(GB * j, GB), :], uq[:], uh[:, ds(GB * j, GB), :].bitcast(F32),
                                        ALU.subtract).then_inc(s_ul, 1)

                if first:
                    up(0, {1: root})
                with dve.Fori(1 if first else 0, NMG // 2) as jj:
                    up(jj)

                def down(jj, tail):
                    for pair in range(2):
                        base = U_FF + UCH * c + 4 * NMG + 8 * jj
                        for p in range(NU):
                            if not (tail and pair == 1 and p + LEAD >= NU):
                                split(base, 4 * pair + p + LEAD)
                        j = 2 * jj + pair
                        dve.wait_ge(unit_used, RING + base + 4 * pair + 4)
                        dve.wait_ge(evacuated, 2 + G_FF + 2 * NMG * c)
                        x2 = xT[:, ds(GB * j, GB), T0:T]
                        v.tensor_tensor(x2, ACC[pair][:, :, 0:TO], x2, ALU.add).then_inc(evacuated, 1)
                        if last:
                            dve.wait_ge(s_x2q, j + 1)
                            dve.wait_ge(s_ac2, j + 1)
                            v.tensor_tensor(sqacc[:], sqacc[:], tmp[:, :, 0:TO], ALU.add).then_inc(s_ac2, 1)

                with dve.Fori(0, NMG // 2 - 1 if last else NMG // 2) as jj:
                    down(jj, False)
                if last:
                    down(NMG // 2 - 1, True)

            ffn(0, first=True)
            with dve.Fori(1, NCH - 1) as c:
                ffn(c)
            v.memset(sqacc[:], 0.0).then_inc(s_ac2, 1)
            ffn(NCH - 1, last=True)
            dve.wait_ge(s_ac2, NMG + 1)
            v.tensor_tensor(sqacc[:, 0, :], sqacc[:, 0, :], sqacc[:, 1, :], ALU.add).then_inc(s_r3, 1)
            dve.wait_ge(s_r3p, 1)
            dve.wait_ge(s_tab, 2)
            v.tensor_scalar(ssum[:, 0:2], M[0][:, 0:2], 1.0 / D, EPS, ALU.mult, ALU.add)
            v.tensor_scalar(ssum[0:TS, 2:3], M[0][0:TS, 2:3], 1.0 / D, EPS, ALU.mult, ALU.add).then_inc(s_r3, 1)
            dve.wait_ge(s_r3a, 1)
            v.reciprocal(rcol[:], rcol[:]).then_inc(s_r3, 1)
            dve.wait_ge(s_r3, 3)
            root_step(rcol[:], ssum[:], rtmp[:], s_r3, 3)
            dve.wait_ge(s_gfb, 16)
            for i, (n, q) in enumerate(YPARTS):
                nt = P if n < 2 else TS
                dve.wait_ge(s_yt, i + 1)
                v.scalar_tensor_tensor(yo[0:nt, n, 512 * q:512 * q + 512], ps[0:nt, YBANK[i % len(YBANK)], :],
                                       rcol[0:nt, n:n + 1], gfb[0:nt, 512 * q:512 * q + 512],
                                       ALU.mult, ALU.mult).then_inc(s_y, 1)

        @block.tensor
        def _(pe):
            def product(out, lhsT, rhs, start=True, stop=True):
                return pe.matmul(out, lhsT, rhs, start=start, stop=stop)

            pe.sem_inc(unit_used, RING)
            for s in (s_bcp, s_num, s_cup, s_cqp):
                pe.sem_inc(s, 1)
            pe.wait_ge(s_const, 2)
            pe.wait_ge(s_vrows, 64)
            nv, nb, nc2 = vrows.shape[0], brows.shape[0], crows.shape[0]
            pe.transpose(M[0][:, 0:nv], vrows[:], ident[0:nv, 0:nv]).then_inc(s_colT, 1)

            def tokens(k):
                for n in range(3):
                    pe.wait_ge(s_xtok[3 * (k // (KB // 4)) + n], 16 if n == 1 else 32)
                if k >= 2:
                    pe.wait_ge(s_xl, 2 * k - 2)
                    pe.wait_ge(s_xT, k - 1)
                for b in range(2):
                    for n, nt in enumerate((P, P, NMETA + TS)):
                        c0 = P * (2 * k + b)
                        ins = pe.transpose(XBANKS[k % 2][:, b, P * n:P * n + nt], xtok[0:nt, n, c0:c0 + P],
                                           ident[0:nt, 0:nt])
                ins.then_inc(s_xtr, 1)

            def columns():
                pe.wait_ge(s_brows, 64)
                pe.transpose(M[0][:, 128:128 + nb], brows[:], ident[0:nb, 0:nb])
                for k in range(CW // P):
                    pe.transpose(M[0][:, 256 + nc2 * k:256 + nc2 * (k + 1)], crows[:, P * k:P * k + P],
                                 ident[0:nc2, 0:nc2])
                for g in range(GB):
                    ins = pe.transpose(M[0][:, 384 + NB * H * g:384 + NB * H * (g + 1)], nrows[:, P * g:P * g + P],
                                       ident[0:NB * H, 0:NB * H])
                ins.then_inc(s_colT, 1)

            def scales():
                pe.wait_ge(s_rd, 3)
                pe.wait_ge(s_const, 3)
                for n, nt in enumerate((P, P, NMETA + TS)):
                    ins = product(M[1][:, P * n:P * n + nt], ones[0:nt, :], rdiag[0:nt, n, 0:nt])
                ins.then_inc(s_rm, 1)

            def gates():
                pe.wait_ge(s_ghl, 4)
                for k in range(KB):
                    product(M[3][:, 0:T], gws[:, k, :], xh[:, k, :], start=k == 0, stop=False)
                    ins = product(M[3][:, 0:T], gws[:, k, :], xl[:, k, :], start=False, stop=k == KB - 1)
                ins.then_inc(s_gp, 1)

            def unit(base, s, acc, rh, rl, kb, c0, first, last):
                pe.wait_ge(low_done, RING + base + s + 1)
                w, n = s % RING, acc.shape[2]
                for b in range(GB):
                    for k in range(UK):
                        hi, lo = (t[:, w, k, P * b:P * b + P] for t in (wh, wl))
                        mh, ml = (t[:, kb + k, c0:c0 + n] for t in (rh, rl))
                        product(acc[:, b, :], hi, mh, start=first and k == 0, stop=False)
                        product(acc[:, b, :], hi, ml, start=False, stop=False)
                        ins = product(acc[:, b, :], lo, mh, start=False, stop=last and k == UK - 1)
                ins.then_inc(unit_used, 1)

            def convolution(i, extra=()):
                for p in range(UCV):
                    if p in extra:
                        for work in extra[p]:
                            work()
                    if p % 4 == 0:
                        pe.wait_ge(evacuated, 2 * i + p // 4 + 1)
                    unit(UCV * i, p, ACC[p // 4][:, :, 0:TZ], xh, xl, UK * (p % 4), TZ0, p % 4 == 0, p % 4 == 3)

            def four_blocks(u):
                return [lambda: tokens(2 * u), lambda: tokens(2 * u + 1), lambda: pe.wait_ge(s_xl, UK * u)]

            tokens(0)
            tokens(1)
            convolution(0, {0: four_blocks(1), 1: four_blocks(2), 2: four_blocks(3) + [columns],
                            3: [lambda: pe.wait_ge(s_xl, KB)], 4: [scales]})
            with pe.Fori(1, H - 1) as i:
                convolution(i)
            gates()
            convolution(H - 1)

            pe.wait_ge(s_row, 12)
            for n, (k0, nk) in enumerate(KT):
                for m, r in enumerate((arw, wkr)):
                    nr = 2 * nk if n == 3 and r is wkr else nk
                    pe.transpose(M[0][0:nr, (4 * m + n) * H:(4 * m + n + 1) * H], r[:, k0:k0 + nr], ident[0:H, 0:H])
            pe.transpose(M[0][0:NB, 8 * H:9 * H], decr[:], ident[0:H, 0:H]).then_inc(s_rowT, 1)

            def by_token(src, width, done):
                for n, (k0, nk) in enumerate(KT):
                    for d in range(GB):
                        m = 2 * nk if n == 3 else nk
                        c = (n % 2) * width + P * d
                        ins = pe.transpose(M[n // 2][0:m, c:c + P], src[:, d, k0:k0 + m], ident[:])
                ins.then_inc(done, 1)

            with pe.Fori(0, H) as h:
                for p in range(UH):
                    g, u, base = ORDER[p], PART[p], U_HEAD + UH * h
                    if g == G_C:
                        if u == 0:
                            pe.wait_ge(s_qml, h + 1)
                            pe.wait_ge(s_s, 1 + h + 1)
                        pe.wait_ge(low_done, RING + base + p + 1)
                        for k in range(NB // 2):
                            b = NB // 2 * (u // GB) + k
                            q = qm[:, u % GB, P * b:P * b + P]
                            product(M[2][:, 0:DV], q, wh[:, p % RING, k, :], start=u == 0 and k == 0, stop=False)
                            ins = product(M[2][:, 0:DV], q, wl[:, p % RING, k, :], start=False, stop=u == 3 and k == 3)
                        ins.then_inc(unit_used, 1)
                        if u == 3:
                            pe.wait_ge(unit_used, RING + base + p + 1)
                            pe.sem_inc(s_cqp, 1)
                    else:
                        n, c0 = (T, 0) if g in (1, 2) else (TO, T0)
                        if u == 0:
                            pe.wait_ge(evacuated, G_HEAD + GH * h + g + 1)
                        if p == 20:
                            pe.wait_ge(s_cpo, h + 1)
                        out = ACC[HEAD_ACC[g]][:, :, 0:n]
                        unit(base, p, out, xh, xl, UK * u, c0, u == 0, u == 3)
                    if p == 2:
                        pe.wait_ge(s_rsp, 2)
                        pe.wait_ge(s_chosen, h + 1)
                        pe.wait_ge(s_cst, 1 + 8 * h)
                        product(ps[:, 4, 0:512], chosen[:], rsplit[:, 0:512])
                        product(ps[:, 5, 0:RW - 512], chosen[:], rsplit[:, 512:RW]).then_inc(s_bcp, 1)
                    if p == 9:
                        pe.wait_ge(biased, GH * h + 2)
                        pe.wait_ge(s_bc, h + 1)
                        by_token(kT, DK, s_ktr)
                        pe.wait_ge(evacuated, 2 + G_HEAD + GH * h)
                        for n, ((k0, nk), (q0, nq, off)) in enumerate(zip(KT, QT)):
                            out = M[2][0:nk, off:off + nq] if n < 2 else M[3][0:nk, off - QT[2][2]:off - QT[2][2] + nq]
                            for d in range(GB):
                                ins = product(out, kT[:, d, k0:k0 + nk], qT[:, d, q0:q0 + nq], d == 0, d == GB - 1)
                        ins.then_inc(s_sc, 1)
                    if p == 13:
                        pe.wait_ge(biased, GH * h + 3)
                        pe.wait_ge(s_kwl, h + 1)
                        by_token(kT, DV, s_vtr)
                        pe.wait_ge(s_const, 19)
                        product(M[3][0:NB, 0:DK], onehot[:], kws[:]).then_inc(s_np, 1)
                    if p == 18:
                        pe.wait_ge(s_vsl, h + 1)
                        pe.wait_ge(s_qn, h + 1)
                        pe.wait_ge(s_cq, h + 1)
                        pe.wait_ge(s_nso, 1 + h + 1)
                        for e in range(GB + 1):
                            out = M[e] if e < GB else M[3]
                            for n, ((k0, nk), (q0, nq, off)) in enumerate(zip(KT, QT)):
                                w = vt[0:nk, n, P * e:P * e + P] if e < GB else ones[0:nk, :]
                                product(out[:, q0 - T0:q0 - T0 + nq], w, E[0:nk, off:off + nq],
                                        start=n in (0, 3), stop=n == 2)
                            if e < GB:
                                ins = product(out[:, TP - T0:TO], cq[:, P * e:P * e + P], fold[:], False, True)
                            else:
                                for d in range(GB):
                                    ins = product(out[:, TP - T0:TO], ones[:], qn[:, d].rearrange("p b t -> p (b t)"),
                                                  start=False, stop=d == GB - 1)
                        ins.then_inc(s_num, 1)
                        pe.wait_ge(s_qmz, 2)
                        for d in range(GB):
                            if d == 1:
                                pe.wait_ge(s_abs, h + 1)
                            for n, (k0, nk) in enumerate(KT[0:3]):
                                ins = product(M[2 + d][:, 0:DV + 1], kw[0:nk, n, P * d:P * d + P],
                                              vt[0:nk, n, :], n == 0, n == 2)
                        ins.then_inc(s_cpp, 1)
                    if 19 <= p < 23:
                        i = p - 19
                        if i == 0:
                            pe.wait_ge(s_h, h + 1)
                        else:
                            pe.wait_ge(s_cst, 1 + 8 * h + 2 * i)
                        for b in (2 * i, 2 * i + 1):
                            pe.wait_ge(s_kwm, NB * h + b + 1)
                            for d in range(GB):
                                out = M[b % 2][:, DV * d:DV * d + DV]
                                product(out, kwm[:, b % 4, P * d:P * d + P], vsh[:], True, False)
                                ins = product(out, kwm[0:TS, b % 4, P * d:P * d + P], vsl[:], False, True)
                            ins.then_inc(s_cup, 1)

            nl = clast.shape[0]
            pe.wait_ge(s_cst, 1 + 8 * H)
            for k in range(CW // P):
                ins = pe.transpose(M[k // 4][0:nl, P * (k % 4):P * (k % 4) + P], zlast[:, k, :], ident[:])
            ins.then_inc(s_clt, 1)

            with pe.Fori(0, NMG) as j:
                for g in range(4):
                    pe.wait_ge(evacuated, G_MERGE + 4 * j + g + 1)
                    acc = ACC[g % 2][:, :, 0:TO]
                    if g < 2:
                        for u in range(NU):
                            unit(U_MERGE + 3 * NU * j, 4 * g + u, acc, xh, xl, UK * u, T0, u == 0, u == NU - 1)
                    else:
                        pe.wait_ge(s_hyl, 8)
                        rh, rl = ((hah, hal), (ybh, ybl))[g - 2]
                        for u in range(2):
                            unit(U_MERGE + 3 * NU * j, 4 + 2 * g + u, acc, rh, rl, UK * u, 0, u == 0, u == 1)
            with pe.Fori(0, NMG // 2) as jj:
                for pair in range(2):
                    pe.wait_ge(evacuated, G_WO + 2 * jj + pair + 1)
                    for u in range(NU):
                        pe.wait_ge(s_mgl, 1 + 2 * u + 2)
                        unit(U_WO + 8 * jj, 4 * pair + u, ACC[pair][:, :, 0:TO], mgh, mgl, UK * u, 0,
                             u == 0, u == NU - 1)
            def up(c, jj, extra=()):
                for pair in range(2):
                    pe.wait_ge(evacuated, G_FF + 2 * NMG * c + 2 * jj + pair + 1)
                    for u in range(NU):
                        pe.wait_ge(s_x1l, 2 * u + 2)
                        unit(U_FF + UCH * c + 8 * jj, 4 * pair + u, ACC[pair][:, :, 0:TO], xh, xl, UK * u, T0,
                             u == 0, u == NU - 1)
                        if NU * pair + u in extra:
                            extra[NU * pair + u]()

            def down(c, jj, extra=()):
                for pair in range(2):
                    pe.wait_ge(evacuated, G_FF + 2 * NMG * c + NMG + 2 * jj + pair + 1)
                    for u in range(NU):
                        pe.wait_ge(s_ul, 1 + NMG * c + 2 * u + 2)
                        unit(U_FF + UCH * c + 4 * NMG + 8 * jj, 4 * pair + u, ACC[pair][:, :, 0:TO], uh, ul,
                             UK * u, 0, u == 0, u == NU - 1)
                        if NU * pair + u in extra:
                            extra[NU * pair + u]()

            def rms_product():
                pe.wait_ge(s_r2, 1)
                product(M[0][:, 0:TO], ones[:], sqacc[:, 0, :]).then_inc(s_r2p, 1)

            def by_tokens(parts, groups):
                pe.wait_ge(evacuated, 2 + G_FF + 2 * NMG * NCH - NMG + groups)
                for i in parts:
                    n, q = YPARTS[i]
                    nt = P if n < 2 else TS
                    if i >= len(YBANK):
                        pe.wait_ge(s_y, i - len(YBANK) + 1)
                    for k in range(4):
                        ins = pe.transpose(ps[0:nt, YBANK[i % len(YBANK)], P * k:P * k + P],
                                           xT[:, 4 * q + k, T0 + P * n:T0 + P * n + nt], ident[:])
                    ins.then_inc(s_yt, 1)

            up(0, 0, {1: rms_product})
            with pe.Fori(1, NMG // 2) as jj:
                up(0, jj)
            with pe.Fori(0, NMG // 2) as jj:
                down(0, jj)
            with pe.Fori(1, NCH - 1) as c:
                with pe.Fori(0, NMG // 2) as jj:
                    up(c, jj)
                with pe.Fori(0, NMG // 2) as jj:
                    down(c, jj)
            with pe.Fori(0, NMG // 2) as jj:
                up(NCH - 1, jj)
            with pe.Fori(0, NMG // 2 - 1) as jj:
                down(NCH - 1, jj)
            down(NCH - 1, NMG // 2 - 1, {4: lambda: by_tokens(range(0, 3), NMG - 2)})
            by_tokens(range(3, 5), NMG - 1)
            pe.wait_ge(s_r3, 1)
            for n, (c0, nt) in enumerate(((0, P), (P, P), (2 * P, TS))):
                ins = product(M[0][0:nt, n:n + 1], sqacc[:, 0, c0:c0 + nt], ones[:, 0:1])
            ins.then_inc(s_r3p, 1)
            by_tokens(range(5, len(YPARTS)), NMG)


_INS = ["x_prompt", "x_sample", "state_mlstm_C", "state_mlstm_n", "state_mlstm_m", "state_conv", "meta_tokens",
        "g_mix", "w_in", "b_in", "w_conv", "p_a", "p_b", "w_o", "g_ffn", "w_up", "w_down", "g_final"]


def kernel(**inputs):
    import numpy as np
    import concourse.bacc as bacc
    from concourse.bass_utils import run_bass_kernel_spmd

    nc = bacc.Bacc("TRN2", target_bir_lowering=False, num_devices=1)
    arrays, args = {}, []
    for name in _INS:
        a = np.ascontiguousarray(inputs[name])
        arrays[f"in_{name}_dram"] = a
        args.append(nc.dram_tensor(f"in_{name}_dram", a.shape, mybir.dt.from_np(a.dtype), kind="ExternalInput").ap())
    L, NB, H, DK, DV = inputs["state_mlstm_C"].shape
    taps, cw = inputs["state_conv"].shape[2:]
    shapes = [inputs["x_prompt"].shape, inputs["x_sample"].shape,
              (L, 1, H, DK, DV), (L, 1, H, DK), (L, 1, H), (L, 1, taps, cw),
              (L, NB, H, DK, DV), (L, NB, H, DK), (L, NB, H), (L, NB, taps, cw)]
    for i, shape in enumerate(shapes):
        args.append(nc.dram_tensor(f"out_{i}_dram", tuple(shape), F32, kind="ExternalOutput").ap())
    build(nc, *args)
    r = run_bass_kernel_spmd(nc, [arrays], core_ids=[0])
    return tuple(r.results[0][f"out_{i}_dram"] for i in range(len(shapes)))
```
